# Optimizing a Trainium2 kernel written in Bass

```python
import math
import jax, jax.numpy as jnp
from jax import lax
import numpy as np

D_MODEL = 1024
BATCH = 1
SEQ = 1024
DEPTH = 2
DEC_BATCH = 8
DEC_SEQ = 4
PAST_LEN = 8192
PAGE_SIZE = 128

N_EVEN = (DEPTH + 1) // 2
N_ODD = DEPTH // 2
GLA_HEADS = 4
GLA_V_WIDTH = D_MODEL // 2
GLA_DV = GLA_V_WIDTH // GLA_HEADS
GLA_DK = GLA_DV // 2
GLA_K_WIDTH = GLA_HEADS * GLA_DK
GLA_RANK = 16
GLA_TAU = 16.0
GLA_CHUNK = 16
S5_WIDTH = D_MODEL - GLA_V_WIDTH
S5_GROUP = 16
S5_GROUPS = S5_WIDTH // S5_GROUP
S5_STATE = 64
LRU_WIDTH = D_MODEL
LRU_BLOCKS = 8
LRU_BLOCK = LRU_WIDTH // LRU_BLOCKS
LRU_C = 8.0
CONV_WIDTH = 4
D_FF = 4 * D_MODEL
NORM_EPS = 1e-6
EVEN_IN_WIDTH = 2 * GLA_K_WIDTH + 2 * GLA_V_WIDTH + GLA_RANK + S5_WIDTH

kernel_name = 'hybrid_gla_s5_rglru_step'

def rmsnorm(x, g):
    xf = x.astype(jnp.float32)
    y = xf * lax.rsqrt(jnp.mean(xf * xf, axis=-1, keepdims=True) + NORM_EPS) * g.astype(jnp.float32)
    return y.astype(x.dtype)

def gla_chunked(q, k, v, log_a, s0):
    bsz, slen, nh, dk = q.shape
    dv = v.shape[-1]
    c = math.gcd(slen, GLA_CHUNK)
    n = slen // c

    def blocks(t):
        return t.astype(jnp.float32).reshape(bsz, n, c, nh, -1).transpose(1, 0, 3, 2, 4)

    qb, kb, vb, gb = blocks(q), blocks(k), blocks(v), blocks(log_a)
    cum = jnp.cumsum(gb, axis=3)
    last = cum[:, :, :, -1:, :]
    q_t = qb * jnp.exp(cum) * (dk ** -0.5)
    k_t = kb * jnp.exp(-cum)
    k_end = kb * jnp.exp(last - cum)
    mask = jnp.tril(jnp.ones((c, c), dtype=bool))
    scores = jnp.where(mask, jnp.einsum('nbhid,nbhjd->nbhij', q_t, k_t), 0.0)
    o_intra = jnp.einsum('nbhij,nbhje->nbhie', scores, vb)

    def step(state, inp):
        q_c, k_c, v_c, dec = inp
        o = jnp.einsum('bhid,bhde->bhie', q_c, state)
        state = jnp.exp(dec)[..., 0, :, None] * state + jnp.einsum('bhjd,bhje->bhde', k_c, v_c)
        return state, o

    s_fin, o_inter = lax.scan(step, s0.astype(jnp.float32), (q_t, k_end, vb, last))
    o = (o_intra + o_inter).transpose(1, 0, 3, 2, 4).reshape(bsz, slen, nh, dv)
    return o, s_fin

def s5_scan(u, h0_re, h0_im, a_re, a_im, log_dt, b_re, b_im, c_re, c_im, d_skip):
    f32 = jnp.float32
    a_re = a_re.astype(f32)
    a_im = a_im.astype(f32)
    dt = jnp.exp(log_dt.astype(f32))[:, None]
    mag = jnp.exp(dt * a_re)
    ab_re = mag * jnp.cos(dt * a_im)
    ab_im = mag * jnp.sin(dt * a_im)
    den = a_re * a_re + a_im * a_im
    coef_re = ((ab_re - 1.0) * a_re + ab_im * a_im) / den
    coef_im = (ab_im * a_re - (ab_re - 1.0) * a_im) / den
    b_re = b_re.astype(f32)
    b_im = b_im.astype(f32)
    bb_re = coef_re[..., None] * b_re - coef_im[..., None] * b_im
    bb_im = coef_re[..., None] * b_im + coef_im[..., None] * b_re
    bu_re = jnp.einsum('bsgc,gpc->bsgp', u, bb_re)
    bu_im = jnp.einsum('bsgc,gpc->bsgp', u, bb_im)
    h0_re = h0_re.astype(f32)
    h0_im = h0_im.astype(f32)
    bu_re = bu_re.at[:, 0].add(ab_re * h0_re - ab_im * h0_im)
    bu_im = bu_im.at[:, 0].add(ab_re * h0_im + ab_im * h0_re)
    ar = jnp.broadcast_to(ab_re, bu_re.shape)
    ai = jnp.broadcast_to(ab_im, bu_im.shape)

    def combine(e1, e2):
        ar1, ai1, br1, bi1 = e1
        ar2, ai2, br2, bi2 = e2
        return (ar2 * ar1 - ai2 * ai1,
                ar2 * ai1 + ai2 * ar1,
                ar2 * br1 - ai2 * bi1 + br2,
                ar2 * bi1 + ai2 * br1 + bi2)

    _, _, h_re, h_im = lax.associative_scan(combine, (ar, ai, bu_re, bu_im), axis=1)
    y = (jnp.einsum('bsgp,gcp->bsgc', h_re, c_re.astype(f32))
         - jnp.einsum('bsgp,gcp->bsgc', h_im, c_im.astype(f32))
         + d_skip.astype(f32) * u)
    return y, h_re[:, -1], h_im[:, -1]

def causal_conv(x, buf, w, bias):
    slen = x.shape[1]
    xp = jnp.concatenate([buf.astype(x.dtype), x], axis=1)
    out = bias.astype(jnp.float32)
    for j in range(CONV_WIDTH):
        out = out + xp[:, j:j + slen].astype(jnp.float32) * w[j].astype(jnp.float32)
    return out, xp[:, slen:].astype(jnp.float32)

def rg_lru(x, h0, w_r, b_r, w_i, b_i, lam):
    bsz, slen, _ = x.shape
    xb = x.reshape(bsz, slen, LRU_BLOCKS, LRU_BLOCK)
    r = jax.nn.sigmoid(jnp.einsum('bsnc,ncd->bsnd', xb, w_r).reshape(bsz, slen, LRU_WIDTH) + b_r)
    i = jax.nn.sigmoid(jnp.einsum('bsnc,ncd->bsnd', xb, w_i).reshape(bsz, slen, LRU_WIDTH) + b_i)
    log_a = -LRU_C * r.astype(jnp.float32) * jax.nn.softplus(-lam.astype(jnp.float32))
    a = jnp.exp(log_a)
    b = jnp.sqrt(-jnp.expm1(2.0 * log_a)) * (i * x)
    b = b.at[:, 0].add(a[:, 0] * h0.astype(jnp.float32))

    def combine(e1, e2):
        return (e1[0] * e2[0], e2[0] * e1[1] + e2[1])

    _, h = lax.associative_scan(combine, (a, b), axis=1)
    return h, h[:, -1]

def even_mixer(x, s_gla, s_re, s_im, g_norm, w_in, w_a2, b_a2, g_head, a_re, a_im, log_dt,
               b_re, b_im, c_re, c_im, d_skip, w_glu, b_glu, w_out):
    f32 = jnp.float32
    bsz, slen, _ = x.shape
    p = rmsnorm(x, g_norm) @ w_in
    o1 = GLA_K_WIDTH
    o2 = 2 * GLA_K_WIDTH
    o3 = o2 + GLA_V_WIDTH
    o4 = o3 + GLA_V_WIDTH
    o5 = o4 + GLA_RANK
    q = p[..., :o1].reshape(bsz, slen, GLA_HEADS, GLA_DK)
    k = p[..., o1:o2].reshape(bsz, slen, GLA_HEADS, GLA_DK)
    v = p[..., o2:o3].reshape(bsz, slen, GLA_HEADS, GLA_DV)
    g = p[..., o3:o4]
    a_lr = p[..., o4:o5]
    u = p[..., o5:]
    log_a = (jax.nn.log_sigmoid((a_lr @ w_a2 + b_a2).astype(f32)) / GLA_TAU).reshape(bsz, slen, GLA_HEADS, GLA_DK)
    o, s_gla_new = gla_chunked(q, k, v, log_a, s_gla)
    o = rmsnorm(o, g_head.reshape(GLA_HEADS, GLA_DV)).reshape(bsz, slen, GLA_V_WIDTH) * jax.nn.silu(g.astype(f32))
    y5, s_re_new, s_im_new = s5_scan(u.astype(f32).reshape(bsz, slen, S5_GROUPS, S5_GROUP), s_re, s_im,
                                     a_re, a_im, log_dt, b_re, b_im, c_re, c_im, d_skip)
    z = jax.nn.gelu(y5.reshape(bsz, slen, S5_WIDTH))
    z = z * jax.nn.sigmoid(z @ w_glu.astype(f32) + b_glu.astype(f32))
    mix = jnp.concatenate([o, z], axis=-1).astype(x.dtype) @ w_out
    return mix, s_gla_new, s_re_new, s_im_new

def odd_mixer(x, s_lru, s_conv, g_norm, w_in, conv_w, conv_b, w_r, b_r, w_i, b_i, lam, w_out):
    p = rmsnorm(x, g_norm) @ w_in
    gate = jax.nn.gelu(p[..., :LRU_WIDTH].astype(jnp.float32))
    xc, conv_new = causal_conv(p[..., LRU_WIDTH:], s_conv, conv_w, conv_b)
    h, lru_new = rg_lru(xc, s_lru, w_r, b_r, w_i, b_i, lam)
    mix = (gate * h).astype(x.dtype) @ w_out
    return mix, lru_new, conv_new

def channel_mixer(x, g_norm, w_up, w_down):
    h = jnp.square(jax.nn.relu(rmsnorm(x, g_norm) @ w_up))
    return h @ w_down

def setup_inputs(seed: int = 0) -> dict:
    key = jax.random.key(seed)
    ks = iter(jax.random.split(key, 64))
    f32 = jnp.float32

    def nrm(shape, scale):
        return scale * jax.random.normal(next(ks), shape, f32)

    def gain(shape):
        return 1.0 + nrm(shape, 0.02)

    out_scale = (2.0 * DEPTH) ** -0.5
    lam_u = jax.random.uniform(next(ks), (N_ODD, LRU_WIDTH), f32, 0.9, 0.999)
    return {
        'x_prompt': nrm((BATCH, SEQ, D_MODEL), 1.0),
        'x_sample': nrm((DEC_BATCH, DEC_SEQ, D_MODEL), 1.0),
        'state_gla': nrm((N_EVEN, DEC_BATCH, GLA_HEADS, GLA_DK, GLA_DV), 1.0),
        'state_s5_re': nrm((N_EVEN, DEC_BATCH, S5_GROUPS, S5_STATE), 0.3),
        'state_s5_im': nrm((N_EVEN, DEC_BATCH, S5_GROUPS, S5_STATE), 0.3),
        'state_lru': nrm((N_ODD, DEC_BATCH, LRU_WIDTH), 0.5),
        'state_conv': nrm((N_ODD, DEC_BATCH, CONV_WIDTH - 1, LRU_WIDTH), 1.0),
        'norm_mix_even': gain((N_EVEN, D_MODEL)),
        'w_in_even': nrm((N_EVEN, D_MODEL, EVEN_IN_WIDTH), D_MODEL ** -0.5),
        'gla_w_a2': nrm((N_EVEN, GLA_RANK, GLA_K_WIDTH), GLA_RANK ** -0.5),
        'gla_b_a2': nrm((N_EVEN, GLA_K_WIDTH), 0.1),
        'gla_norm': gain((N_EVEN, GLA_V_WIDTH)),
        's5_a_re': -0.5 + nrm((N_EVEN, S5_GROUPS, S5_STATE), 0.01),
        's5_a_im': math.pi * jnp.arange(S5_STATE, dtype=f32) + nrm((N_EVEN, S5_GROUPS, S5_STATE), 0.01),
        's5_log_dt': jax.random.uniform(next(ks), (N_EVEN, S5_GROUPS), f32, math.log(1e-3), math.log(1e-1)),
        's5_b_re': nrm((N_EVEN, S5_GROUPS, S5_STATE, S5_GROUP), (2.0 * S5_GROUP) ** -0.5),
        's5_b_im': nrm((N_EVEN, S5_GROUPS, S5_STATE, S5_GROUP), (2.0 * S5_GROUP) ** -0.5),
        's5_c_re': nrm((N_EVEN, S5_GROUPS, S5_GROUP, S5_STATE), S5_STATE ** -0.5),
        's5_c_im': nrm((N_EVEN, S5_GROUPS, S5_GROUP, S5_STATE), S5_STATE ** -0.5),
        's5_d': nrm((N_EVEN, S5_GROUPS, S5_GROUP), 1.0),
        's5_w_glu': nrm((N_EVEN, S5_WIDTH, S5_WIDTH), S5_WIDTH ** -0.5),
        's5_b_glu': nrm((N_EVEN, S5_WIDTH), 0.01),
        'w_out_even': nrm((N_EVEN, GLA_V_WIDTH + S5_WIDTH, D_MODEL), (GLA_V_WIDTH + S5_WIDTH) ** -0.5 * out_scale),
        'norm_mix_odd': gain((N_ODD, D_MODEL)),
        'w_in_odd': nrm((N_ODD, D_MODEL, 2 * LRU_WIDTH), D_MODEL ** -0.5),
        'conv_w': nrm((N_ODD, CONV_WIDTH, LRU_WIDTH), CONV_WIDTH ** -0.5),
        'conv_b': nrm((N_ODD, LRU_WIDTH), 0.01),
        'lru_w_r': nrm((N_ODD, LRU_BLOCKS, LRU_BLOCK, LRU_BLOCK), LRU_BLOCK ** -0.5),
        'lru_b_r': nrm((N_ODD, LRU_WIDTH), 0.01),
        'lru_w_i': nrm((N_ODD, LRU_BLOCKS, LRU_BLOCK, LRU_BLOCK), LRU_BLOCK ** -0.5),
        'lru_b_i': nrm((N_ODD, LRU_WIDTH), 0.01),
        'lru_lam': jnp.log(lam_u) - jnp.log1p(-lam_u),
        'w_out_odd': nrm((N_ODD, LRU_WIDTH, D_MODEL), LRU_WIDTH ** -0.5 * out_scale),
        'norm_mlp': gain((DEPTH, D_MODEL)),
        'w_up': nrm((DEPTH, D_MODEL, D_FF), D_MODEL ** -0.5),
        'w_down': nrm((DEPTH, D_FF, D_MODEL), D_FF ** -0.5 * out_scale),
        'norm_final': gain((D_MODEL,)),
    }

def reference(x_prompt, x_sample, state_gla, state_s5_re, state_s5_im, state_lru, state_conv,
              norm_mix_even, w_in_even, gla_w_a2, gla_b_a2, gla_norm, s5_a_re, s5_a_im, s5_log_dt,
              s5_b_re, s5_b_im, s5_c_re, s5_c_im, s5_d, s5_w_glu, s5_b_glu, w_out_even,
              norm_mix_odd, w_in_odd, conv_w, conv_b, lru_w_r, lru_b_r, lru_w_i, lru_b_i, lru_lam, w_out_odd,
              norm_mlp, w_up, w_down, norm_final):
    f32 = jnp.float32
    bp = x_prompt.shape[0]
    yp, ys = x_prompt, x_sample
    gla_p, re_p, im_p, lru_p, conv_p = [], [], [], [], []
    gla_s, re_s, im_s, lru_s, conv_s = [], [], [], [], []
    for layer in range(DEPTH):
        if layer % 2 == 0:
            e = layer // 2
            prm = (norm_mix_even[e], w_in_even[e], gla_w_a2[e], gla_b_a2[e], gla_norm[e], s5_a_re[e], s5_a_im[e],
                   s5_log_dt[e], s5_b_re[e], s5_b_im[e], s5_c_re[e], s5_c_im[e], s5_d[e], s5_w_glu[e], s5_b_glu[e],
                   w_out_even[e])
            mp, sg, sr, si = even_mixer(yp, jnp.zeros((bp, GLA_HEADS, GLA_DK, GLA_DV), f32),
                                        jnp.zeros((bp, S5_GROUPS, S5_STATE), f32),
                                        jnp.zeros((bp, S5_GROUPS, S5_STATE), f32), *prm)
            gla_p.append(sg); re_p.append(sr); im_p.append(si)
            ms, sg, sr, si = even_mixer(ys, state_gla[e], state_s5_re[e], state_s5_im[e], *prm)
            gla_s.append(sg); re_s.append(sr); im_s.append(si)
        else:
            o = layer // 2
            prm = (norm_mix_odd[o], w_in_odd[o], conv_w[o], conv_b[o], lru_w_r[o], lru_b_r[o], lru_w_i[o],
                   lru_b_i[o], lru_lam[o], w_out_odd[o])
            mp, sl, sc = odd_mixer(yp, jnp.zeros((bp, LRU_WIDTH), f32),
                                   jnp.zeros((bp, CONV_WIDTH - 1, LRU_WIDTH), f32), *prm)
            lru_p.append(sl); conv_p.append(sc)
            ms, sl, sc = odd_mixer(ys, state_lru[o], state_conv[o], *prm)
            lru_s.append(sl); conv_s.append(sc)
        yp = yp + mp
        ys = ys + ms
        yp = yp + channel_mixer(yp, norm_mlp[layer], w_up[layer], w_down[layer])
        ys = ys + channel_mixer(ys, norm_mlp[layer], w_up[layer], w_down[layer])
    y_prompt = rmsnorm(yp, norm_final)
    y_sample = rmsnorm(ys, norm_final)
    return (y_prompt, y_sample,
            jnp.stack(gla_p), jnp.stack(re_p), jnp.stack(im_p), jnp.stack(lru_p), jnp.stack(conv_p),
            jnp.stack(gla_s), jnp.stack(re_s), jnp.stack(im_s), jnp.stack(lru_s), jnp.stack(conv_s))


_drawn_inputs = setup_inputs


def setup_inputs(seed=0):
    import zlib

    import numpy as np

    out = dict(_drawn_inputs(seed))
    spreads = {}
    factors = {'gla_norm': 8.0,
     's5_a_re': 66.033,
     's5_b_glu': 64.0,
     'norm_mix_odd': 2.853,
     'lru_b_r': 40.777,
     'lru_b_i': 24.237,
     'norm_mlp': 3.509,
     'norm_final': 19.291,
     'conv_b': 7.994,
     's5_c_re': 2.901,
     's5_c_im': 2.889}
    for name, (base, spread) in spreads.items():
        noise = np.random.default_rng([zlib.crc32(name.encode()), seed]).standard_normal(out[name].shape)
        drawn = base * np.exp(spread * noise) if base else spread * noise
        out[name] = __import__('jax').numpy.asarray(drawn.astype(out[name].dtype))
    for name, factor in factors.items():
        out[name] = (out[name] * factor).astype(out[name].dtype)
    return out
```

```python
from contextlib import ExitStack

import concourse.bass as bass
from concourse import mybir

F32 = mybir.dt.float32
F32R = mybir.dt.float32r
ALU = mybir.AluOpType
ACT = mybir.ActivationFunctionType

P = 128
D = 1024
KT = D // P
SEQ = 1024
NB, NS = 8, 4
T = SEQ + NB * NS
CH = 352
NCH = T // CH
FT = 4 * D // P
EPS = 1e-6

PAR = {}
_at = 0
for _name, _n in (("g_mix_even", 8), ("g_mlp0", 8), ("g_mix_odd", 8), ("g_mlp1", 8), ("g_final", 8),
                  ("g_head", 4), ("b_a2", 2), ("s5_d", 4), ("b_glu", 4), ("conv_w", 32), ("conv_b", 8),
                  ("b_r", 8), ("b_i", 8), ("lam", 8)):
    PAR[_name] = (_at, _at + _n)
    _at += _n
NPAR = _at
PAR5 = {}
_at = 0
for _name, _n in (("a_re", 16), ("a_im", 16), ("log_dt", 16), ("b_re", 256), ("b_im", 256),
                  ("c_re", 256), ("c_im", 256), ("h0_re", 128), ("h0_im", 128)):
    PAR5[_name] = (_at, _at + _n)
    _at += _n
NPAR5 = _at
CST = {"ident": (0, 128), "tri": (128, 256), "smask": (256, 288), "bmask": (288, 296), "tri8": (296, 360)}
NCST = 360


class Chain:

    def __init__(self, eng, sem):
        self.eng, self.sem, self.n, self.var, self.per = eng, sem, 0, None, 0

    def run(self, ins):
        self.n += 1
        return ins.then_inc(self.sem, 1)

    def value(self):
        return self.n if self.var is None else self.var * self.per + self.n

    def wait(self):
        self.eng.wait_ge(self.sem, self.value())

    def link(self, ins):
        self.run(ins)
        self.wait()

    def loop(self, var, per):
        self.var, self.per, self.first = var, per, self.n

    def end(self, trips):
        assert self.n - self.first == self.per, (self.n - self.first, self.per)
        self.var, self.n = None, self.first + self.per * trips


def index(names):
    return {name: n for n, name in enumerate(names)}


HG = FT // 2
MLP_TILES = 2 * FT
STREAM = index(["u0", "u1", "u2", "u3", "alr", "q0", "q1", "k0", "k1", "g0", "g1", "g2", "g3",
                "v0", "v1", "v2", "v3", "glu0", "glu1"] + [f"oute{m}" for m in range(KT)]
               + [f"mlp0_{n}" for n in range(MLP_TILES)]
               + [f"xb{n}" for n in range(KT)] + [f"gate{n}" for n in range(KT)]
               + [f"outo{m}" for m in range(KT)] + [f"mlp1_{n}" for n in range(MLP_TILES)])
NT = len(STREAM)
RAW, SLOTS = 2, 4
POOL_LOADS = 20

_odd = ["xb0", "xb1"]
for _n in range(KT):
    _odd += [f"r{_n}", f"i{_n}"] + ([f"xb{_n + 2}"] if _n + 2 < KT else [f"gate{_n + 2 - KT}"])
_odd += [f"gate{_n}" for _n in range(2, KT)]
ACC = index(["norm0", "u0", "u1", "u2", "u3", "alr", "lg0", "lg1", "q0", "q1", "k0", "k1",
             "g0", "g1", "g2", "g3", "v0", "v1", "v2", "glu0", "glu1", "glu2", "glu3",
             "head0", "head1", "head2", "head3"] + [f"oute{m}" for m in range(KT)]
            + ["norm1"] + [f"mlp0_{n}" for n in range(HG * (2 + KT))]
            + ["norm2"] + _odd + [f"outo{m}" for m in range(KT)]
            + ["norm3"] + [f"mlp1_{n}" for n in range(HG * (2 + KT))] + ["norm4"])

SPLIT = {}
_at = 0
for _name, _n in (("norm0", 8), ("z", 4), ("zg", 4), ("o", 4), ("norm1", 8), ("norm2", 8), ("mix", 8), ("norm3", 8)):
    SPLIT[_name] = _at
    _at += _n

L = 8
NC = SEQ // L
PQ = 4
GQ = 8
NG = 4
CW = NC + 2 * NB
YW = NC + NB
GC = 128
NGC = SEQ // GC
BL = 16
NBL = GC // BL
MAGIC = 1.5 * 2.0 ** 23
TWO_PI_1, TWO_PI_2, TWO_PI_3 = 6.28125, 0.0019350051879882812, 3.0199159819567e-07


def trunk_kernel(nc, x_t, w_stream, par_d, par5_d, cst_d, w_a2, w_ri, st_gla, odd_lru, odd_conv,
                 y_t, s5_out, lru_out, conv_out, gla_p, gla_s):
    u_scr = nc.dram_tensor("u_scratch", (NG, P, L, CW), F32, kind="Internal").ap()
    y_scr = nc.dram_tensor("y_scratch", (NG, P, GQ, YW), F32, kind="Internal").ap()
    z_scr = nc.dram_tensor("z_scratch", (NG, P, T), F32, kind="Internal").ap()
    g_scr = nc.dram_tensor("g_scratch", (NG, P, T), F32, kind="Internal").ap()

    with ExitStack() as ctx:
        def sem(name):
            return ctx.enter_context(nc.semaphore(name))

        def sb(stack, name, shape, dt=F32):
            return stack.enter_context(nc.sbuf_tensor(name, shape, dt))

        XH = sb(ctx, "XH", [P, KT, T], F32R)
        XL = sb(ctx, "XL", [P, KT, T], F32R)
        WR = sb(ctx, "WR", [P, RAW, 1024])
        WH = sb(ctx, "WH", [P, SLOTS, 1024], F32R)
        WL = sb(ctx, "WL", [P, SLOTS, 1024], F32R)
        TT = sb(ctx, "TT", [P, 4, T])
        par = sb(ctx, "par", [P, NPAR])
        cst = sb(ctx, "cst", [P, NCST])
        ones = sb(ctx, "ones", [P, P])
        few = sb(ctx, "few", [P, 4])
        sp4 = sb(ctx, "sp4", [P, KT])
        spt = sb(ctx, "spt", [P, KT])
        SO = sb(ctx, "SO", [P, 2, 16, 1 + NB])
        with ExitStack() as area:
            X0 = sb(area, "X0", [P, KT, T])
        with ExitStack() as area:
            Q = sb(area, "Q", [P, 2, T])
            K = sb(area, "K", [P, 2, T])
            LA = sb(area, "LA", [P, 2, T])
            with ExitStack() as s5a:
                XA = sb(s5a, "XA", [P, 2, PQ, L, 16])
                WIN = sb(s5a, "WIN", [P, 2, PQ, P])
                WO = sb(s5a, "WO", [P, 2, PQ, L, 16])
                M = sb(s5a, "M", [P, GQ, L, 16])
                T7 = sb(s5a, "T7", [P, GQ * 16])
                PT = sb(s5a, "PT", [P, 2, PQ, NC])
                U = sb(s5a, "U", [P, 2, GQ, CW])
                VH = sb(s5a, "VH", [P, 2 * PQ * 144])
                G = sb(s5a, "G", [P, GQ * YW])
                UR = sb(s5a, "UR", [P, L, CW])
                p5 = sb(s5a, "p5", [P, NPAR5])
                pw = sb(s5a, "pw", [P, 2, 9, 16])
                rot = sb(s5a, "rot", [P, 2, 10, 16])
                sm = sb(s5a, "sm", [P, 12, 16])
                CB = sb(s5a, "CB", [P, 2, 16, 32])
                wa2 = sb(s5a, "wa2", [16, 2 * P])
            with ExitStack() as gla:
                V = sb(gla, "V", [P, NGC + 1, 512])
                QM = sb(gla, "QM", [P, 2 * T])
                QI = sb(gla, "QI", [P, 2 * SEQ])
                KX = sb(gla, "KX", [P, 2, 1152])
                SC = sb(gla, "SC", [P, 2, 256])
                KTR = sb(gla, "KTR", [P, 2, P])
                S = sb(gla, "S", [P, 2, P])
                GB = sb(gla, "GB", [P, NGC, NBL, NBL])
                gs = sb(gla, "gs", [P, 6, 64])
                SS = sb(gla, "SS", [P, NB, P])
        X = sb(ctx, "X", [P, KT, T])
        with ExitStack() as area:
            HH = sb(area, "HH", [P, 4, T], F32R)
            HL = sb(area, "HL", [P, 4, T], F32R)
        HB = sb(ctx, "HB", [P, KT, T])
        XP = sb(ctx, "XP", [P, 2, 3 + SEQ + 7 * NB])
        WRI = sb(ctx, "WRI", [P, 2, 2, P])
        st_lru = sb(ctx, "st_lru", [P, KT, NB])
        st_conv = sb(ctx, "st_conv", [P, KT, NB, 3])
        LN = sb(ctx, "LN", [P, KT, 1 + NB])
        CN = sb(ctx, "CN", [P, KT, 3 * (1 + NB)])
        acc = ctx.enter_context(nc.psum_tensor("acc", [P, 2, NCH, 512], F32))
        ms = ctx.enter_context(nc.psum_tensor("ms", [P, 2, 512], F32))
        glb = acc[:, :, :, :].rearrange("p s c n -> p (s c) n")

        par_in, par5_in, cst_in, wa2_in = sem("par_in"), sem("par5_in"), sem("cst_in"), sem("wa2_in")
        x_in = [sem(f"x_in{k}") for k in range(KT)]
        xr_in = sem("xr_in")
        w_first = [sem(f"w_first{r}") for r in range(RAW)]
        w_in = [sem(f"w_in{r}") for r in range(RAW)]
        u_out, m_in, y_out, y_in, ud_in = sem("u_out"), sem("m_in"), sem("y_out"), sem("y_in"), sem("ud_in")
        u_in = [sem("u_in0"), sem("u_in1")]
        z_out, g_out = sem("z_out"), [sem("g_out0"), sem("g_out1")]
        z_in = [sem("z_in0"), sem("z_in1")]
        g_in = sem("g_in")
        ss_in, ss_out, s_out = sem("ss_in"), sem("ss_out"), sem("s_out")
        odd_in, wri_in = sem("odd_in"), [sem("wri_in0"), sem("wri_in1")]
        y_sent, small_out = sem("y_sent"), sem("small_out")
        w_hi, w_ready, w_used = sem("w_hi"), sem("w_ready"), sem("w_used")
        acc_done = [sem("acc_done0"), sem("acc_done1")]
        acc_read = [sem("acc_read0"), sem("acc_read1")]
        sq_done, ssq_add, rs_done, xn_done = sem("sq_done"), sem("ssq_add"), sem("rs_done"), sem("xn_done")
        xh_done, xl_done = sem("xh_done"), sem("xl_done")
        h_sq, h_ready = sem("h_sq"), sem("h_ready")
        ms_done, ms_read = sem("ms_done"), sem("ms_read")
        prep_act, prep_dve, const_ready = sem("prep_act"), sem("prep_dve"), sem("const_ready")
        ur_ready, xa_ready, wo_ready, st_ready, zin_done, z_done = (sem("ur_ready"), sem("xa_ready"), sem("wo_ready"),
                                                                    sem("st_ready"), sem("zin_done"), sem("z_done"))
        alr_ready, lg_dve, lg_act, g_done = sem("alr_ready"), sem("lg_dve"), sem("lg_act"), sem("g_done")
        z_ready, gg_done = sem("z_ready"), sem("gg_done")
        ga, gd, pair_ready = sem("ga"), sem("gd"), sem("pair_ready")
        kx_ready, sc_done, sc_ready, kt_done, kt_ready = (sem("kx_ready"), sem("sc_done"), sem("sc_ready"),
                                                          sem("kt_done"), sem("kt_ready"))
        o_done, o_read, kv_done, s_ready = sem("o_done"), sem("o_read"), sem("kv_done"), sem("s_ready")
        sm_done, smk_ready, smc_ready, so_done, so_read, skv_done, sst_ready = (
            sem("sm_done"), sem("smk_ready"), sem("smc_ready"), sem("so_done"), sem("so_read"), sem("skv_done"),
            sem("sst_ready"))
        xp_ready, conv_done, sig_done, gt_done, hb_ready = (sem("xp_ready"), sem("conv_done"), sem("sig_done"),
                                                            sem("gt_done"), sem("hb_ready"))
        tg_done, sp_act = sem("tg_done"), sem("sp_act")
        dve_step, act_step = sem("dve_step"), sem("act_step")

        def p_col(name, n):
            return par[:, PAR[name][0] + n:PAR[name][0] + n + 1]

        def p5c(name):
            return p5[:, PAR5[name][0]:PAR5[name][1]]

        def c_(name):
            return cst[:, CST[name][0]:CST[name][1]]

        def cut(ap):
            return ap.rearrange("p (c n) -> p c n", n=CH)

        def bank(t):
            return acc[:, t % 2, :, 0:CH]

        def done_wait(eng, name, a=None):
            t = ACC[name]
            eng.wait_ge(acc_done[t % 2], t // 2 + 1)

        def read_wait(eng, name):
            t = ACC[name]
            eng.wait_ge(acc_read[t % 2], t // 2 + 1)

        MS = index("a0 b0 c0 d0 a1 b1 e0 f0 c1 d1 a2 b2 e1 f1 c2 d2 a3 b3 e2 f2 c3 d3 e3 f3".split())
        ident, tri = c_("ident"), c_("tri").rearrange("p (i n) -> p i n", i=NBL)
        VV = VH[:, 0:2 * PQ * YW].rearrange("p (r q n) -> p r q n", r=2, q=PQ)
        HV = VH[:, :].rearrange("p (r q n) -> p r q n", r=2, q=PQ)
        YR = VH[:, 0:L * YW].rearrange("p (l n) -> p l n", l=L)
        GV = G[:, 0:2 * PQ * NC].rearrange("p (r q n) -> p r q n", r=2, q=PQ)
        YG = G[:, :].rearrange("p (g n) -> p g n", g=GQ)
        ALR = UR[:, :, :].rearrange("p l n -> p (l n)")[0:16, 0:T]
        block = ctx.enter_context(nc.Block())

        @block.sync
        def _(sp):
            for k in range(KT):
                sp.dma_start(X0[:, k, :], x_t[k]).then_inc(x_in[k], 16)
            sp.dma_start(par[:, :], par_d).then_inc(par_in, 16)
            sp.dma_start(cst[:, :], cst_d).then_inc(cst_in, 16)
            sp.wait_ge(xn_done, KT)
            sp.dma_start(p5[:, :], par5_d).then_inc(par5_in, 16)
            sp.dma_start(wa2[:, :], w_a2).then_inc(wa2_in, 16)

            def store_u(q):
                read_wait(sp, f"u{q}")
                sp.dma_start(u_scr[q], UR[:, :, :]).then_inc(u_out, 16)

            def load_u(q):
                sp.wait_ge(u_out, 16 * (q + 1))
                if q >= 2:
                    sp.wait_ge(zin_done, q - 1)
                src = u_scr[q].rearrange("(g c) l w -> l c g w", g=GQ)
                for j in range(L):
                    sp.dma_start(U[16 * j:16 * j + 16, q % 2, :, :], src[j]).then_inc(u_in[q % 2], 16)

            def load_m(q):
                sp.wait_ge(ms_read, MS[f"b{q}"] + 1)
                if q >= 1:
                    sp.wait_ge(ms_done, MS[f"f{q - 1}"] + 1)
                for i in range(L):
                    sp.dma_start(M[0:16 * (i + 1), :, i, :],
                                 T7[16 * (L - 1 - i):P, :].rearrange("p (g c) -> p g c", c=16)).then_inc(m_in, 16)

            def turn_y(q):
                sp.wait_ge(ms_read, MS[f"f{q}"] + 1)
                sp.dma_start(y_scr[q], YG).then_inc(y_out, 16)
                sp.wait_ge(y_out, 16 * (q + 1))
                src = y_scr[q].rearrange("(i c) g n -> g c i n", i=L)
                for g in range(GQ):
                    sp.dma_start(YR[16 * g:16 * g + 16], src[g]).then_inc(y_in, 16)
                sp.dma_start(U[:, q % 2, :, :].rearrange("p g w -> p (g w)"),
                             u_scr[q].rearrange("p l w -> p (l w)")).then_inc(ud_in, 16)

            store_u(0)
            load_u(0)
            store_u(1)
            load_u(1)
            store_u(2)
            sp.wait_ge(u_out, 48)
            store_u(3)
            load_m(0)
            for q in range(NG):
                if q + 1 < NG:
                    load_m(q + 1)
                turn_y(q)
                if q + 2 < NG:
                    load_u(q + 2)
                sp.wait_ge(z_done, q + 1)
                sp.dma_start(z_scr[q], TT[:, 2, :]).then_inc(z_out, 16)
            sp.wait_ge(z_out, 16 * NG)
            for r in range(2):
                sp.wait_ge(g_out[r], 32)
            for k in range(NG):
                if k >= 2:
                    sp.wait_ge(xl_done, SPLIT["z"] + k - 1)
                sp.dma_start(TT[:, k % 2, :], z_scr[k]).then_inc(z_in[k % 2], 16)
            for k in range(NG):
                sp.wait_ge(xl_done, (SPLIT["z"] + k + 3) if k < 2 else (SPLIT["zg"] + k - 1))
                sp.dma_start(TT[:, k % 2, :], z_scr[k]).then_inc(z_in[k % 2], 16)
            def load_w(n, r, first=False):
                sp.wait_ge(w_ready, n - (RAW - 1))
                sp.dma_start(WR[:, r, :], w_stream[n]).then_inc(w_in[r], 16)

            gla_w = STREAM["glu0"] + 6
            for n in range(POOL_LOADS, gla_w):
                load_w(n, n % RAW)
            for p in range(2):
                if p:
                    sp.wait_ge(ss_out, 16)
                sp.dma_start(SS[:, :, :], st_gla[p]).then_inc(ss_in, 16)
                sp.wait_ge(sst_ready, NB * (p + 1))
                sp.dma_start(gla_s[p], SS[:, :, :]).then_inc(ss_out, 16)
            sp.dma_start(gla_p, S[:, :, :]).then_inc(s_out, 16)
            for h in range(4):
                sp.wait_ge(sst_ready, 2 * NB)
                if h:
                    sp.wait_ge(xl_done, SPLIT["o"] + h)
                sp.dma_start(TT[:, 3, :], g_scr[h]).then_inc(g_in, 16)
            sp.wait_ge(xl_done, SPLIT["o"] + 4)
            sp.wait_ge(s_out, 16)
            sp.wait_ge(ss_out, 32)
            for k in range(KT):
                sp.dma_start(X[:, k, :], x_t[k]).then_inc(xr_in, 16)
            at = gla_w
            while (NT - at) % 4:
                load_w(at, at % RAW)
                at += 1
            with sp.Fori(0, (NT - at) // 4) as i:
                for j in range(4):
                    n = at + j
                    sp.wait_ge(w_ready, i * 4 + (n - (RAW - 1)))
                    sp.dma_start(WR[:, n % RAW, :], w_stream[i * 4 + n]).then_inc(w_in[n % RAW], 16)
            for k in range(KT):
                sp.wait_ge(xn_done, 4 * KT + k + 1)
                sp.dma_start(y_t[k], X[:, k, :]).then_inc(y_sent, 16)
            sp.wait_ge(y_sent, 16 * KT)
            sp.wait_ge(small_out, 3 * 16)

        @block.gpsimd
        def _(pool):
            def split(r, s, loaded, used, count):
                pool.wait_ge(*loaded)
                if used is not None:
                    pool.wait_ge(w_used, used)
                pool.tensor_tensor(WH[:, s, :], WR[:, r, :], ones[:, 0:1].broadcast_to([P, 1024]), ALU.mult).then_inc(w_hi, 1)
                pool.wait_ge(w_hi, count)
                pool.tensor_tensor(WL[:, s, :], WR[:, r, :], WH[:, s, :].bitcast(F32), ALU.subtract).then_inc(w_ready, 1)

            for n in range(RAW):
                pool.dma_start(WR[:, n, :], w_stream[n]).then_inc(w_first[n], 16)
            pool.wait_ge(const_ready, 1)
            at = POOL_LOADS
            while (NT - at) % 4:
                at += 1
            for n in range(at):
                loaded = ((w_first[n % RAW], 16 * (n // RAW + 1)) if n < POOL_LOADS else
                          (w_in[n % RAW], 16 * ((n - POOL_LOADS) // RAW + 1)))
                split(n % RAW, n % SLOTS, loaded, n - SLOTS + 1 if n >= SLOTS else None, n + 1)
                if n + RAW < POOL_LOADS:
                    pool.wait_ge(w_ready, n + 1)
                    pool.dma_start(WR[:, n % RAW, :], w_stream[n + RAW]).then_inc(w_first[n % RAW], 16)
            with pool.Fori(0, (NT - at) // 4) as i:
                for j in range(4):
                    n = at + j
                    split(n % RAW, n % SLOTS, (w_in[n % RAW], i * 32 + 16 * ((n - POOL_LOADS) // RAW + 1)), i * 4 + (n - SLOTS + 1), i * 4 + (n + 1))

        @block.tensor
        def _(pe):
            held = [0]

            def mm(out, lhs, rhs, start, stop):
                ins = pe.matmul(out, lhs, rhs, start=start, stop=stop)
                if held[0]:
                    held[0] -= 1
                    ins.then_inc(w_used, 1)
                return ins

            PASSES = ((WH, 0), (WH, 1), (WL, 0))

            def claim(t, prev=None):
                if prev is not None or t >= 2:
                    pe.wait_ge(acc_read[t % 2], t // 2 if prev is None else prev)

            def product(t, slots, cols, ops, nk=KT, xn=None, last_w=False):
                for k in range(nk):
                    if xn is not None:
                        pe.wait_ge(xl_done, xn + k + 1)
                    if last_w and k:
                        held[0] += 1
                    s, col = slots(k), cols(k)
                    for c in range(NCH):
                        for i, (w, x) in enumerate(PASSES):
                            last = mm(acc[:, t % 2, c, 0:CH], w[:, s, col:col + P],
                                      ops[x](k)[:, c * CH:(c + 1) * CH], k == 0 and i == 0, k == nk - 1 and i == 2)
                last.then_inc(acc_done[t % 2], 1)

            XOPS = (lambda k: XH[:, k, :], lambda k: XL[:, k, :])

            def project(name, acc_name, xn=None, need=True):
                n, t = STREAM[name], ACC[acc_name]
                pe.wait_ge(w_ready, n + 1)
                claim(t)
                product(t, lambda k: n % SLOTS, lambda k: k * P, XOPS, xn=xn)
                held[0] += 1

            def norm(r):
                t = ACC[f"norm{r}"]
                pe.wait_ge(ssq_add, KT * (r + 1))
                claim(t)
                for c in range(NCH):
                    last = mm(acc[:, t % 2, c, 0:CH], ones[:, :], TT[:, 2, c * CH:(c + 1) * CH], True, True)
                last.then_inc(acc_done[t % 2], 1)

            def ms_claim(step):
                if MS[step]:
                    pe.wait_ge(ms_read, MS[step])

            def step_a(q):
                pe.wait_ge(xa_ready, q + 1)
                ms_claim(f"a{q}")
                for r in range(2):
                    for g in range(PQ):
                        last = pe.transpose(ms[:, r, g * P:(g + 1) * P],
                                            XA[:, r, g, :, :].rearrange("p l c -> p (l c)"), ident)
                last.then_inc(ms_done, 1)

            def step_b(q):
                ms_claim(f"b{q}")
                for g in range(PQ):
                    for r in range(2):
                        last = pe.matmul(ms[:, 0, g * 32:(g + 1) * 32], XA[:, r, g, :, :].rearrange("p l c -> p (l c)"),
                                         CB[:, r, PQ * q + g, :], start=(r == 0), stop=(r == 1))
                last.then_inc(ms_done, 1)

            def step_cd(q, r):
                if r == 0:
                    pe.wait_ge(u_in[q % 2], 16 * L * (q // 2 + 1))
                ms_claim(("c", "d")[r] + str(q))
                for g in range(GQ):
                    h = 64 * (g % 2)
                    last = pe.matmul(ms[h:h + 64, g // 4, (g // 2 % 2) * YW:(g // 2 % 2 + 1) * YW],
                                     WIN[:, r, g // 2, h:h + 64], U[:, q % 2, g, NB:NB + YW], start=True, stop=True)
                last.then_inc(ms_done, 1)

            def step_ef(q, half):
                if half == 0:
                    pe.wait_ge(m_in, 16 * L * (q + 1))
                    pe.wait_ge(st_ready, q + 1)
                ms_claim(("e", "f")[half] + str(q))
                for g in range(4 * half, 4 * half + 4):
                    h = 64 * (g % 2)
                    out = ms[:, g % 2, (g // 2 % 2) * YW:(g // 2 % 2 + 1) * YW]
                    pe.matmul(out, M[:, g, :, :].rearrange("p l c -> p (l c)"), U[:, q % 2, g, 0:YW], start=True, stop=False)
                    for r in range(2):
                        last = pe.matmul(out, WO[h:h + 64, r, g // 2, :, :].rearrange("p l c -> p (l c)"),
                                         HV[h:h + 64, r, g // 2, 0:YW], start=False, stop=(r == 1))
                last.then_inc(ms_done, 1)

            def logits(p):
                t = ACC[f"lg{p}"]
                claim(t)
                for c in range(NCH):
                    last = mm(acc[:, t % 2, c, 0:CH], wa2[0:16, p * P:(p + 1) * P], ALR[:, c * CH:(c + 1) * CH], True, True)
                last.then_inc(acc_done[t % 2], 1)

            def values():
                n = STREAM["v0"]
                for j in range(3):
                    t = ACC[f"v{j}"]
                    claim(t)
                    for b in range(3):
                        at = min((3 * j + b) * GC, T - GC)
                        for k in range(KT):
                            if j == b == k % 2 == 0:
                                pe.wait_ge(w_ready, n + k // 2 + 1)
                            if j == b == 2 and k % 2 == 0 and k:
                                held[0] += 1
                            s, col = (n + k // 2) % SLOTS, (k % 2) * 512
                            for i, (w, x) in enumerate(((WH, XH), (WL, XH), (WH, XL))):
                                last = mm(acc[:, t % 2, b, :], x[:, k, at:at + GC], w[:, s, col:col + 512],
                                          k == 0 and i == 0, k == KT - 1 and i == 2)
                    last.then_inc(acc_done[t % 2], 1)
                held[0] += 1

            pe.wait_ge(const_ready, 1)
            norm(0)
            project("u0", "u0", xn=SPLIT["norm0"])
            pe.wait_ge(cst_in, 16)
            step_a(0)
            project("u1", "u1")
            step_b(0)
            project("u2", "u2")
            step_cd(0, 0)
            project("u3", "u3")
            step_cd(0, 1)
            project("alr", "alr")
            step_a(1)
            step_b(1)
            pe.wait_ge(alr_ready, 1)
            pe.wait_ge(wa2_in, 16)
            logits(0)
            logits(1)
            project("q0", "q0")
            step_ef(0, 0)
            step_ef(0, 1)
            project("q1", "q1")
            step_cd(1, 0)
            step_cd(1, 1)
            project("k0", "k0")
            step_a(2)
            step_b(2)
            project("k1", "k1")
            step_ef(1, 0)
            step_ef(1, 1)
            project("g0", "g0")
            step_cd(2, 0)
            step_cd(2, 1)
            project("g1", "g1")
            step_a(3)
            step_b(3)
            project("g2", "g2")
            step_ef(2, 0)
            step_ef(2, 1)
            project("g3", "g3")
            step_cd(3, 0)
            step_cd(3, 1)
            step_ef(3, 0)
            step_ef(3, 1)
            values()
            for m in range(4):
                n, t = STREAM["glu0"] + m // 2, ACC[f"glu{m}"]
                pe.wait_ge(w_ready, n + 1)
                claim(t)
                product(t, lambda k: n % SLOTS, lambda k: (m % 2) * 512 + k * P, XOPS, nk=4,
                        xn=SPLIT["z"] if m == 0 else None)
                if m % 2:
                    held[0] += 1
            read_wait(pe, "glu2")
            read_wait(pe, "glu3")
            vs = V[0:32, NGC, :]

            def gla_front(it):
                p, c, b = it // NGC, it % NGC, it % 2
                pe.wait_ge(pair_ready, p + 1)
                if it == 0:
                    pe.wait_ge(ms_read, len(MS))
                if it >= 2:
                    pe.wait_ge(kt_ready, it - 1)
                pe.transpose(ms[:, b, 0:P], TT[:, 0, c * GC:(c + 1) * GC], ident).then_inc(kt_done, 1)
                pe.wait_ge(kx_ready, it + 1)
                if it >= 2:
                    pe.wait_ge(sc_ready, it - 1)
                for i in range(NBL):
                    at = (c * NBL + i) * 2 * BL
                    last = pe.matmul(glb[:, b, i * 2 * BL:(i + 1) * 2 * BL], KX[:, b, i * GC:(i + 1) * GC],
                                     QM[:, at:at + 2 * BL], start=True, stop=True)
                last.then_inc(sc_done, 1)

            def gla_back(it):
                p, c, b = it // NGC, it % NGC, it % 2
                pe.wait_ge(sc_ready, it + 1)
                if it >= 2:
                    pe.wait_ge(o_read, it - 1)
                if c:
                    pe.wait_ge(s_ready, it)
                    pe.matmul(glb[:, 2 + b, 0:2 * GC], S[:, p, :], QI[:, c * 2 * GC:(c + 1) * 2 * GC],
                              start=True, stop=False)
                for e in range(2):
                    h = 2 * p + e
                    last = pe.matmul(glb[:, 2 + b, e * GC:(e + 1) * GC], V[:, c, h * P:(h + 1) * P],
                                     SC[:, b, e * GC:(e + 1) * GC], start=(c == 0), stop=(c == 0 or e == 1))
                last.then_inc(o_done, 1)
                pe.wait_ge(kt_ready, it + 1)
                if it:
                    pe.wait_ge(s_ready, it)
                for e in range(2):
                    h = 2 * p + e
                    last = pe.matmul(glb[64 * e:64 * e + 64, 5, 0:P], KTR[:, b, 64 * e:64 * e + 64],
                                     V[:, c, h * P:(h + 1) * P], start=True, stop=True)
                last.then_inc(kv_done, 1)

            def gla_sample(p):
                pe.wait_ge(kt_ready, NGC * (p + 1))
                pe.wait_ge(sc_ready, NGC * (p + 1))
                pe.transpose(glb[0:32, 4, 0:P], TT[:, 0, SEQ:T], ident).then_inc(sm_done, 1)
                qs = QM[:, 2 * SEQ:2 * T]
                pe.matmul(glb[0:32, 0, 0:64], TT[:, 1, SEQ:T], qs, start=True, stop=True).then_inc(sm_done, 1)
                pe.wait_ge(smc_ready, p + 1)
                pe.wait_ge(ss_in, 16 * (p + 1))
                pe.wait_ge(o_read, NGC * (p + 1))
                for e in range(2):
                    h = 2 * p + e
                    pe.matmul(glb[:, 2, e * 32:(e + 1) * 32], vs[:, h * P:(h + 1) * P], SC[0:32, 0, e * 32:(e + 1) * 32],
                              start=(e == 0), stop=False, skip_group_check=True)
                two = glb[:, 2, 0:64].rearrange("p (e n) -> p e n", e=2)
                qs2 = qs.rearrange("p (e n) -> p e n", e=2)
                for s in range(NB):
                    last = pe.matmul(two[:, :, s * NS:(s + 1) * NS], SS[:, s, :], qs2[:, :, s * NS:(s + 1) * NS],
                                     start=False, stop=(s == NB - 1), skip_group_check=True)
                last.then_inc(so_done, 1)
                pe.wait_ge(smk_ready, p + 1)
                pe.wait_ge(s_ready, NGC * (p + 1))
                kts = KX[0:32, :, :].rearrange("p a n -> p (a n)")
                for s in range(NB):
                    for e in range(2):
                        h = 2 * p + e
                        last = pe.matmul(glb[64 * e:64 * e + 64, 5 if s < 4 else 1, (s % 4) * P:(s % 4 + 1) * P],
                                         kts[:, s * P + 64 * e:s * P + 64 * e + 64], vs[:, h * P:(h + 1) * P],
                                         start=True, stop=True)
                last.then_inc(skv_done, 1)

            for p in range(2):
                if p:
                    pe.wait_ge(sst_ready, NB)
                    pe.wait_ge(so_read, 1)
                gla_front(NGC * p)
                for it in range(NGC * p, NGC * (p + 1)):
                    if it + 1 < NGC * (p + 1):
                        gla_front(it + 1)
                    gla_back(it)
                gla_sample(p)
            pe.wait_ge(sst_ready, 2 * NB)
            pe.wait_ge(so_read, 2)
            for h in range(4):
                t = ACC[f"head{h}"]
                pe.wait_ge(sq_done, KT + h + 1)
                claim(t)
                for c in range(NCH):
                    last = mm(acc[:, t % 2, c, 0:CH], ones[:, :], TT[:, 0, c * CH:(c + 1) * CH], True, True)
                last.then_inc(acc_done[t % 2], 1)
            pe.wait_ge(xl_done, SPLIT["o"] + 4)
            for m in range(KT):
                project(f"oute{m}", f"oute{m}")

            def mlp(layer, r):
                norm(r)
                w0, t0, xn = STREAM[f"mlp{layer}_0"], ACC[f"mlp{layer}_0"], SPLIT[f"norm{r}"]
                h0 = FT * layer

                def up(a, par_a, base_w, base_t, per):
                    for j in range(2):
                        n, t = base_w + j, base_t + j
                        pe.wait_ge(w_ready, per(4) + (n + 1))
                        pe.wait_ge(acc_read[t % 2], per(5) + t // 2)
                        product(t, lambda k: n % SLOTS, lambda k: k * P, XOPS,
                                xn=xn if base_w == w0 and j == 0 else None)
                        held[0] += 1

                def down(hready, par_a, base_w, base_t, per):
                    pe.wait_ge(w_ready, per(4) + (base_w + 2))
                    pe.wait_ge(h_ready, hready)
                    ops = (lambda k: HH[:, 2 * par_a + k, :], lambda k: HL[:, 2 * par_a + k, :])
                    for m in range(KT):
                        t = base_t + m
                        pe.wait_ge(acc_read[t % 2], per(5) + t // 2)
                        product(t, lambda k: (base_w + k) % SLOTS, lambda k: m * P, ops, nk=2,
                                last_w=(m == KT - 1))
                    held[0] += 1

                up(0, 0, w0, t0, lambda x: 0)
                with pe.Fori(0, HG // 2 - 1) as i:
                    for j in range(2):
                        per = lambda x: i * (2 * x)
                        up(None, (j + 1) % 2, w0 + 2 + 4 * j, t0 + 2 + 10 * j, per)
                        down(i * 4 + (h0 + 2 * j + 2), j, w0 + 4 + 4 * j, t0 + 4 + 10 * j, per)
                a = HG - 2
                flat = lambda x: 0
                up(a + 1, 1, w0 + 2 + 4 * a, t0 + 2 + 10 * a, flat)
                down(h0 + 2 * a + 2, 0, w0 + 4 + 4 * a, t0 + 4 + 10 * a, flat)
                down(h0 + 2 * a + 4, 1, w0 + 6 + 4 * a, t0 + 12 + 10 * a, flat)

            mlp(0, 1)
            norm(2)

            def gates(n):
                pe.wait_ge(conv_done, n + 1)
                pe.wait_ge(wri_in[n % 2], 16 * (n // 2 + 1))
                for r, name in enumerate(("r", "i")):
                    t = ACC[f"{name}{n}"]
                    claim(t)
                    for c in range(NCH):
                        last = mm(acc[:, t % 2, c, 0:CH], WRI[:, n % 2, r, :], HB[:, n, c * CH:(c + 1) * CH], True, True)
                    last.then_inc(acc_done[t % 2], 1)

            project("xb0", "xb0", xn=SPLIT["norm2"])
            project("xb1", "xb1")
            for n in range(KT):
                gates(n)
                if n + 2 < KT:
                    project(f"xb{n + 2}", f"xb{n + 2}")
                else:
                    project(f"gate{n + 2 - KT}", f"gate{n + 2 - KT}")
            for n in range(2, KT):
                project(f"gate{n}", f"gate{n}")
            for m in range(KT):
                project(f"outo{m}", f"outo{m}", xn=SPLIT["mix"] if m == 0 else None)
            mlp(1, 3)
            norm(4)

        def last_down(layer, k):
            return f"mlp{layer}_{2 * HG + KT * (HG - 1) + k}"

        X_FROM = [None, lambda k: f"oute{k}", lambda k: last_down(0, k), lambda k: f"outo{k}", lambda k: last_down(1, k)]
        G_NORM = ["g_mix_even", "g_mlp0", "g_mix_odd", "g_mlp1", "g_final"]

        def sq_base(r):
            return KT * r + (4 if r else 0)

        @block.scalar
        def _(act):
            def norm(r):
                t, xs = ACC[f"norm{r}"], X0 if r == 0 else X
                for k in range(KT):
                    if r == 0:
                        act.wait_ge(x_in[k], 16)
                    else:
                        read_wait(act, X_FROM[r](k))
                    if k >= 2:
                        act.wait_ge(ssq_add, KT * r + k - 1)
                    act.activation(TT[:, k % 2, :], xs[:, k, :], ACT.Square).then_inc(sq_done, 1)
                done_wait(act, f"norm{r}")
                act.activation(cut(TT[:, 3, :]), bank(t), ACT.Sqrt, bias=few[:, 0:1], scale=1.0 / D)\
                   .then_inc(acc_read[t % 2], 1)
                if r < 4:
                    for k in range(KT):
                        act.wait_ge(xn_done, KT * r + k + 1)
                        act.activation(XH[:, k, :], TT[:, k % 2, :], ACT.Copy).then_inc(xh_done, 1)

            def read_ms(step, out, src):
                act.wait_ge(ms_done, MS[step] + 1)
                act.activation(out, src, ACT.Copy).then_inc(ms_read, 1)

            def read_a(q):
                read_ms(f"a{q}", WIN[:, :, :, :].rearrange("p r g n -> p r (g n)"), ms[:, :, :])

            def read_b(q):
                if q:
                    act.wait_ge(m_in, 16 * L * q)
                read_ms(f"b{q}", T7[:, :], ms[:, 0, 0:P])

            def read_cd(q, r):
                if r == 0 and q:
                    act.wait_ge(z_done, q)
                read_ms(("c", "d")[r] + str(q), VV[:, r, :, :].rearrange("p (b g) n -> p b (g n)", b=2),
                        ms[:, :, 0:2 * YW])

            def read_ef(q, half):
                read_ms(("e", "f")[half] + str(q),
                        G[:, half * 4 * YW:(half + 1) * 4 * YW].rearrange("p (q e n) -> p e q n", q=2, e=2),
                        ms[:, :, 0:2 * YW].rearrange("p e (q n) -> p e q n", q=2))

            def read_u(q):
                t = ACC[f"u{q}"]
                done_wait(act, f"u{q}")
                if q:
                    act.wait_ge(u_out, 16 * q)
                for c in range(NCH):
                    n = min(CH, SEQ - c * CH) // L
                    at = NB + c * (CH // L)
                    act.activation(UR[:, :, at:at + n].rearrange("p l n -> p n l"),
                                   acc[:, t % 2, c, 0:n * L].rearrange("p (n l) -> p n l", l=L), ACT.Copy)
                tail = acc[:, t % 2, 2, CH - NB * NS:CH].rearrange("p (n s) -> p n s", s=NS)
                act.activation(UR[:, 0:NS, 0:NB].rearrange("p l n -> p n l"), tail, ACT.Copy)
                act.activation(UR[:, L - NS:L, NB + NC:CW].rearrange("p l n -> p n l"), tail, ACT.Copy)\
                   .then_inc(acc_read[t % 2], 1)

            def read_plain(name, out, func=ACT.Copy, **more):
                t = ACC[name]
                done_wait(act, name)
                act.activation(cut(out), bank(t), func, **more).then_inc(acc_read[t % 2], 1)

            def gelu(q):
                act.wait_ge(zin_done, q + 1)
                if q:
                    act.wait_ge(z_out, 16 * q)
                act.activation(TT[:, 2, 0:SEQ].rearrange("p (n l) -> p l n", l=L), YR[:, :, NB:YW], ACT.Gelu_apprx_tanh)
                act.activation(TT[:, 2, SEQ:T].rearrange("p (n s) -> p s n", s=NS), YR[:, 0:NS, 0:NB],
                               ACT.Gelu_apprx_tanh).then_inc(z_done, 1)

            def decay(p):
                if p:
                    act.wait_ge(lg_dve, 2)
                read_plain(f"lg{p}", TT[:, 0, :], ACT.Identity, bias=p_col("b_a2", p))
                act.wait_ge(lg_dve, 2 * p + 1)
                act.activation(TT[:, 2, :], TT[:, 2, :], ACT.Exp).then_inc(act_step, 1)
                act.wait_ge(act_step, p + 1)
                act.activation(TT[:, 2, :], TT[:, 2, :], ACT.Ln, bias=1.0).then_inc(lg_act, 1)

            def read_g(h):
                if h >= 2:
                    act.wait_ge(g_out[h % 2], 16)
                read_plain(f"g{h}", TT[:, h % 2, :], ACT.Silu)
                read_wait(act, f"g{h}")
                act.dma_start(g_scr[h], TT[:, h % 2, :]).then_inc(g_out[h % 2], 16)

            act.wait_ge(const_ready, 1)
            norm(0)
            act.wait_ge(par5_in, 16)
            act.activation(sm[:, 0, :], p5c("log_dt"), ACT.Exp).then_inc(prep_act, 1)
            act.wait_ge(prep_dve, 1)
            act.activation(sm[:, 3, :], sm[:, 2, :], ACT.Exp)
            act.activation(sm[:, 4, :], sm[:, 2, :], ACT.Exp, scale=float(L)).then_inc(prep_act, 1)
            act.wait_ge(prep_dve, 2)
            act.activation(rot[:, 1, 0, :], sm[:, 6, :], ACT.Sin)
            act.activation(rot[:, 0, 0, :], sm[:, 7, :], ACT.Sin, bias=few[:, 1:2]).then_inc(prep_act, 1)
            act.wait_ge(ur_ready, 1)
            read_u(0)
            read_a(0)
            read_u(1)
            read_b(0)
            read_u(2)
            read_cd(0, 0)
            read_u(3)
            read_cd(0, 1)
            act.wait_ge(u_out, 16 * NG)
            t = ACC["alr"]
            done_wait(act, "alr")
            act.activation(cut(ALR), acc[0:16, t % 2, :, 0:CH], ACT.Copy).then_inc(acc_read[t % 2], 1)
            read_wait(act, "alr")
            act.nop().then_inc(alr_ready, 1)
            read_a(1)
            read_b(1)
            act.wait_ge(par_in, 16)
            decay(0)
            decay(1)
            read_plain("q0", Q[:, 0, :])
            read_ef(0, 0)
            read_ef(0, 1)
            gelu(0)
            read_plain("q1", Q[:, 1, :])
            read_cd(1, 0)
            read_cd(1, 1)
            read_plain("k0", K[:, 0, :])
            read_a(2)
            read_b(2)
            read_plain("k1", K[:, 1, :])
            read_ef(1, 0)
            read_ef(1, 1)
            gelu(1)
            read_g(0)
            read_cd(2, 0)
            read_cd(2, 1)
            read_g(1)
            read_a(3)
            read_b(3)
            read_g(2)
            read_ef(2, 0)
            read_ef(2, 1)
            gelu(2)
            read_g(3)
            read_cd(3, 0)
            read_cd(3, 1)
            read_ef(3, 0)
            read_ef(3, 1)
            gelu(3)
            act.wait_ge(z_done, NG)
            for j in range(3):
                t = ACC[f"v{j}"]
                done_wait(act, f"v{j}")
                if j < 2:
                    act.activation(V[:, 3 * j:3 * j + 3, :], acc[:, t % 2, :, :], ACT.Copy).then_inc(acc_read[t % 2], 1)
                else:
                    act.activation(V[:, 6:8, :], acc[:, t % 2, 0:2, :], ACT.Copy)
                    act.activation(V[0:32, NGC, :], acc[96:P, t % 2, 2, :], ACT.Copy).then_inc(acc_read[t % 2], 1)
            for k in range(4):
                act.wait_ge(z_in[k % 2], 16 * (k // 2 + 1))
                act.activation(XH[:, k, :], TT[:, k % 2, :], ACT.Copy).then_inc(xh_done, 1)
            for m in range(4):
                act.wait_ge(xl_done, SPLIT["z"] + 4 if m < 2 else SPLIT["zg"] + m - 1)
                read_plain(f"glu{m}", TT[:, 2 + m % 2, :], ACT.Sigmoid, bias=p_col("b_glu", m))
                act.wait_ge(gg_done, m + 1)
                act.activation(XH[:, 4 + m, :], TT[:, 2 + m % 2, :], ACT.Copy).then_inc(xh_done, 1)

            for p in range(2):
                g0 = 4 * p
                act.wait_ge(gd, g0 + 1)
                act.activation(TT[:, 0, :], TT[:, 3, :], ACT.Exp).then_inc(ga, 1)
                act.wait_ge(gd, g0 + 2)
                act.activation(TT[:, 0, :], TT[:, 3, :], ACT.Exp, scale=-1.0).then_inc(ga, 1)
                act.wait_ge(gd, g0 + 3)
                act.activation(TT[:, 0, :], TT[:, 0, :], ACT.Exp).then_inc(ga, 1)
                act.wait_ge(gd, g0 + 4)
                act.activation(gs[:, 2:5, :], gs[:, 2:5, :], ACT.Exp)
                act.activation(GB[:, :, :, :], GB[:, :, :, :], ACT.Exp).then_inc(ga, 1)

                def read_kt(it):
                    act.wait_ge(kt_done, it + 1)
                    if it >= 2:
                        act.wait_ge(kv_done, it - 1)
                    act.activation(KTR[:, it % 2, :], ms[:, it % 2, 0:P], ACT.Copy)\
                       .then_inc(kt_ready, 1)

                read_kt(NGC * p)
                for it in range(NGC * p, NGC * (p + 1)):
                    c, b = it % NGC, it % 2
                    if c + 1 < NGC:
                        read_kt(it + 1)
                    act.wait_ge(o_done, it + 1)
                    act.activation(Q[:, p, c * GC:(c + 1) * GC], glb[:, 2 + b, 0:GC], ACT.Copy)
                    act.activation(K[:, p, c * GC:(c + 1) * GC], glb[:, 2 + b, GC:2 * GC], ACT.Copy).then_inc(o_read, 1)
                act.wait_ge(so_done, p + 1)
                act.activation(Q[:, p, SEQ:T], glb[:, 2, 0:32], ACT.Copy)
                act.activation(K[:, p, SEQ:T], glb[:, 2, 32:64], ACT.Copy).then_inc(so_read, 1)
            act.wait_ge(so_read, 2)
            act.wait_ge(sst_ready, 2 * NB)
            for h in range(4):
                t = ACC[f"head{h}"]
                if h:
                    act.wait_ge(xl_done, SPLIT["o"] + h)
                act.activation(TT[:, 0, :], (Q, K)[h % 2][:, h // 2, :], ACT.Square).then_inc(sq_done, 1)
                done_wait(act, f"head{h}")
                act.activation(cut(TT[:, 1, :]), bank(t), ACT.Sqrt, bias=few[:, 0:1], scale=1.0 / P)\
                   .then_inc(acc_read[t % 2], 1)
                act.wait_ge(gg_done, 4 + h + 1)
                act.activation(XH[:, h, :], TT[:, 2, :], ACT.Copy).then_inc(xh_done, 1)

            def mlp_hidden(base_t, per5, hcount, u, first):
                t = base_t
                act.wait_ge(acc_done[t % 2], per5 + (t // 2 + 1))
                if not first:
                    act.wait_ge(h_ready, hcount - 1)
                act.activation(cut(TT[:, u % 2, :]), bank(t), ACT.Relu).then_inc(acc_read[t % 2], 1)
                act.wait_ge(acc_read[t % 2], per5 + (t // 2 + 1))
                act.activation(TT[:, 2 + u % 2, :], TT[:, u % 2, :], ACT.Square).then_inc(h_sq, 1)

            def mlp(layer):
                t0, h0 = ACC[f"mlp{layer}_0"], FT * layer
                for j in range(2):
                    mlp_hidden(t0 + j, 0, None, j, True)
                with act.Fori(0, HG // 2 - 1) as i:
                    for a in range(2):
                        for j in range(2):
                            mlp_hidden(t0 + 2 + 10 * a + j, i * 10, i * 4 + (h0 + 2 * (a + 1) + j), j, False)
                a = HG - 2
                for j in range(2):
                    mlp_hidden(t0 + 2 + 10 * a + j, 0, h0 + 2 * (a + 1) + j, j, False)
                act.wait_ge(h_ready, h0 + FT)

            norm(1)
            mlp(0)
            norm(2)
            act.wait_ge(tg_done, 1)
            act.activation(spt[:, :], spt[:, :], ACT.Exp).then_inc(act_step, 1)
            act.wait_ge(act_step, 3)
            act.activation(spt[:, :], spt[:, :], ACT.Ln, bias=1.0).then_inc(sp_act, 1)

            def load_ri(n):
                act.dma_start(WRI[:, n % 2, :, :], w_ri[n]).then_inc(wri_in[n % 2], 16)

            def read_xb(n):
                t = ACC[f"xb{n}"]
                done_wait(act, f"xb{n}")
                if n >= 2:
                    act.wait_ge(conv_done, n - 1)
                act.activation(XP[:, n % 2, 3:3 + 2 * CH].rearrange("p (c n) -> p c n", n=CH),
                               acc[:, t % 2, 0:2, 0:CH], ACT.Copy)
                act.activation(XP[:, n % 2, 3 + 2 * CH:3 + SEQ], acc[:, t % 2, 2, 0:SEQ - 2 * CH], ACT.Copy)
                smp = XP[:, n % 2, 3 + SEQ:].rearrange("p (b s) -> p b s", b=NB)
                act.activation(smp[:, :, 0:3], st_conv[:, n, :, :], ACT.Copy)
                act.activation(smp[:, :, 3:7], acc[:, t % 2, 2, SEQ - 2 * CH:CH].rearrange("p (b s) -> p b s", b=NB),
                               ACT.Copy).then_inc(acc_read[t % 2], 1)

            def gates(n):
                if n:
                    act.wait_ge(gt_done, n)
                if n == KT - 1:
                    act.wait_ge(hb_ready, 1)
                read_plain(f"r{n}", TT[:, 0, :], ACT.Sigmoid, bias=p_col("b_r", n))
                read_plain(f"i{n}", TT[:, 1, :], ACT.Sigmoid, bias=p_col("b_i", n))
                read_wait(act, f"r{n}")
                act.activation(TT[:, 0, :], TT[:, 0, :], ACT.Tanh, scale=sp4[:, n:n + 1]).then_inc(sig_done, 1)
                act.wait_ge(sig_done, 2 * n + 1)
                act.activation(TT[:, 3, :], TT[:, 0, :], ACT.Sqrt).then_inc(sig_done, 1)

            act.wait_ge(xl_done, SPLIT["norm2"] + KT)
            act.dma_start(st_lru[:, :, :], odd_lru).then_inc(odd_in, 16)
            act.dma_start(st_conv[:, :, :, :], odd_conv).then_inc(odd_in, 16)
            load_ri(0)
            load_ri(1)
            act.wait_ge(odd_in, 32)
            act.wait_ge(xp_ready, 1)
            read_xb(0)
            read_xb(1)
            act.wait_ge(tg_done, 2)
            for n in range(KT):
                gates(n)
                if n + 2 < KT:
                    load_ri(n + 2)
                    read_xb(n + 2)
                if n >= KT - 2:
                    m = n + 2 - KT
                    act.wait_ge(gt_done, n + 1)
                    read_plain(f"gate{m}", TT[:, m % 2, :], ACT.Gelu_apprx_tanh)
            for m in range(2, KT):
                act.wait_ge(hb_ready, m - 1)
                read_plain(f"gate{m}", TT[:, m % 2, :], ACT.Gelu_apprx_tanh)
            done_wait(act, f"gate{KT - 1}")
            act.dma_start(lru_out, LN[:, :, :]).then_inc(small_out, 16)
            act.dma_start(conv_out, CN[:, :, :]).then_inc(small_out, 16)
            act.dma_start(s5_out, SO[:, :, :, :]).then_inc(small_out, 16)
            for k in range(KT):
                act.wait_ge(hb_ready, k + 1)
                act.activation(XH[:, k, :], HB[:, k, :], ACT.Copy).then_inc(xh_done, 1)
            norm(3)
            mlp(1)
            norm(4)

        @block.vector
        def _(dve):
            step = Chain(dve, dve_step)
            link = step.link
            SP1 = slice(0, SEQ)

            def tt(out, a, b, op):
                return dve.tensor_tensor(out, a, b, op)

            def stt(out, a, scalar, b, op0, op1):
                return dve.scalar_tensor_tensor(out=out, in0=a, scalar=scalar, in1=b, op0=op0, op1=op1)

            def lo_part(dst, src, hi, want):
                dve.wait_ge(xh_done, want)
                tt(dst, src, hi.bitcast(F32), ALU.subtract).then_inc(xl_done, 1)

            def norm(r):
                xs, name, base = (X0 if r == 0 else X), G_NORM[r], KT * r
                at = SPLIT.get(f"norm{r}")
                for k in range(KT):
                    dve.wait_ge(sq_done, sq_base(r) + k + 1)
                    if k == 0:
                        dve.tensor_copy(TT[:, 2, :], TT[:, 0, :]).then_inc(ssq_add, 1)
                    else:
                        dve.wait_ge(ssq_add, base + k)
                        tt(TT[:, 2, :], TT[:, 2, :], TT[:, k % 2, :], ALU.add).then_inc(ssq_add, 1)
                if r == 0:
                    dve.wait_ge(par_in, 16)
                dve.wait_ge(ssq_add, base + KT)
                read_wait(dve, f"norm{r}")
                link(dve.reciprocal(TT[:, 3, :], TT[:, 3, :]))
                for k in range(KT):
                    g = p_col(name, k)
                    if r == 4:
                        stt(X[:, k, :], X[:, k, :], g, TT[:, 3, :], ALU.mult, ALU.mult).then_inc(xn_done, 1)
                        continue
                    if k >= 2:
                        dve.wait_ge(xl_done, at + k - 1)
                    stt(TT[:, k % 2, :], xs[:, k, :], g, TT[:, 3, :], ALU.mult, ALU.mult).then_inc(xn_done, 1)
                    if k:
                        dve.wait_ge(xn_done, base + k)
                        lo_part(XL[:, k - 1, :], TT[:, (k - 1) % 2, :], XH[:, k - 1, :], at + k)
                if r < 4:
                    dve.wait_ge(xn_done, base + KT)
                    lo_part(XL[:, KT - 1, :], TT[:, 1, :], XH[:, KT - 1, :], at + KT)

            def cmul(out, a, b, t, neg=False):
                link(tt(t[0], a[0], b[0], ALU.mult))
                link(tt(t[1], a[1], b[1], ALU.mult))
                tt(out[0], t[0], t[1], ALU.subtract).then_inc(dve_step, 1)
                step.n += 1
                step.wait()
                link(tt(t[0], a[0], b[1], ALU.mult))
                link(tt(t[1], a[1], b[0], ALU.mult))
                if neg:
                    return stt(out[1], t[0], -1.0, t[1], ALU.mult, ALU.subtract)
                return tt(out[1], t[0], t[1], ALU.add)

            dve.memset(ones[:, :], 1.0)
            dve.memset(few[:, 0:1], EPS)
            dve.memset(few[:, 1:2], 1.5707963267948966).then_inc(const_ready, 1)
            norm(0)

            dve.memset(UR[:, :, :], 0.0).then_inc(ur_ready, 1)
            dve.memset(M[:, :, :, :], 0.0)
            dve.memset(CB[:, :, :, :], 0.0)
            link(dve.memset(pw[:, :, 0, :], 0.0))
            link(dve.memset(pw[:, 0, 0, :], 1.0))
            dve.wait_ge(par5_in, 16)
            cb = [p5c(n).rearrange("p (g c) -> p g c", c=16) for n in ("c_re", "c_im")]
            bb = [p5c(n).rearrange("p (g c) -> p g c", c=16) for n in ("b_re", "b_im")]
            for e in range(2):
                h = slice(64 * e, 64 * e + 64)
                dve.tensor_copy(CB[h, 0, :, 16 * e:16 * e + 16], cb[0][h])
                link(dve.tensor_scalar(CB[h, 1, :, 16 * e:16 * e + 16], cb[1][h], -1.0, None, ALU.mult))
            dve.wait_ge(prep_act, 1)
            are, aim = p5c("a_re"), p5c("a_im")
            link(tt(sm[:, 1, :], sm[:, 0, :], aim, ALU.mult))
            tt(sm[:, 2, :], sm[:, 0, :], are, ALU.mult).then_inc(prep_dve, 1)
            link(dve.tensor_scalar(sm[:, 5, :], sm[:, 1, :], 0.15915494309189535, MAGIC, ALU.mult, ALU.add))
            link(dve.tensor_scalar(sm[:, 5, :], sm[:, 5, :], MAGIC, None, ALU.subtract))
            link(stt(sm[:, 6, :], sm[:, 5, :], -TWO_PI_1, sm[:, 1, :], ALU.mult, ALU.add))
            link(stt(sm[:, 6, :], sm[:, 5, :], -TWO_PI_2, sm[:, 6, :], ALU.mult, ALU.add))
            link(stt(sm[:, 6, :], sm[:, 5, :], -TWO_PI_3, sm[:, 6, :], ALU.mult, ALU.add))
            link(dve.tensor_scalar(sm[:, 6, :], sm[:, 6, :], 3.1415925, -3.1415925, ALU.min, ALU.max))
            stt(sm[:, 7, :], sm[:, 6, :], -1.0, sm[:, 6, :], ALU.mult, ALU.min).then_inc(prep_dve, 1)
            dve.wait_ge(prep_act, 3)
            sc2 = (sm[:, 8, :], sm[:, 9, :])
            a1 = (pw[:, 0, 1, :], pw[:, 1, 1, :])
            link(tt(a1[0], sm[:, 3, :], rot[:, 0, 0, :], ALU.mult))
            link(tt(a1[1], sm[:, 3, :], rot[:, 1, 0, :], ALU.mult))
            for k in range(2, 9):
                half = k // 2
                link(cmul((pw[:, 0, k, :], pw[:, 1, k, :]), (pw[:, 0, half, :], pw[:, 1, half, :]),
                          (pw[:, 0, k - half, :], pw[:, 1, k - half, :]), sc2))
            for k in range(1, 10):
                c, s = rot[:, 0, k, :], rot[:, 1, k, :]
                r0 = (rot[:, 0, k - 1, :], rot[:, 1, k - 1, :])
                link(cmul((c, s), r0, r0, sc2))
                link(tt(sc2[0], c, c, ALU.mult))
                link(tt(sc2[1], s, s, ALU.mult))
                link(tt(sc2[0], sc2[0], sc2[1], ALU.add))
                link(dve.tensor_scalar(sc2[0], sc2[0], -0.5, 1.5, ALU.mult, ALU.add))
                link(tt(c, c, sc2[0], ALU.mult))
                link(tt(s, s, sc2[0], ALU.mult))
            link(dve.tensor_scalar(sm[:, 5, :], a1[0], 1.0, None, ALU.subtract))
            link(tt(sm[:, 8, :], are, are, ALU.mult))
            link(tt(sm[:, 9, :], aim, aim, ALU.mult))
            link(tt(sm[:, 8, :], sm[:, 8, :], sm[:, 9, :], ALU.add))
            link(dve.reciprocal(sm[:, 10, :], sm[:, 8, :]))
            link(tt(sm[:, 8, :], sm[:, 5, :], are, ALU.mult))
            link(tt(sm[:, 9, :], a1[1], aim, ALU.mult))
            link(tt(sm[:, 8, :], sm[:, 8, :], sm[:, 9, :], ALU.add))
            link(tt(sm[:, 6, :], sm[:, 8, :], sm[:, 10, :], ALU.mult))
            link(tt(sm[:, 8, :], a1[1], are, ALU.mult))
            link(tt(sm[:, 9, :], sm[:, 5, :], aim, ALU.mult))
            link(tt(sm[:, 8, :], sm[:, 8, :], sm[:, 9, :], ALU.subtract))
            link(tt(sm[:, 7, :], sm[:, 8, :], sm[:, 10, :], ALU.mult))

            def over(ap, shape):
                return ap.broadcast_to(shape)

            g16 = [P, 16, 16]
            coef = [over(sm[:, 6 + r, :].unsqueeze(2), g16) for r in range(2)]
            tq = [TT[:, 3, 256 * n:256 * (n + 1)].rearrange("p (g c) -> p g c", c=16) for n in range(4)]
            link(tt(tq[0], coef[0], bb[0], ALU.mult))
            link(tt(tq[1], coef[1], bb[1], ALU.mult))
            link(tt(tq[2], coef[0], bb[1], ALU.mult))
            link(tt(tq[3], coef[1], bb[0], ALU.mult))
            link(tt(bb[0], tq[0], tq[1], ALU.subtract))
            link(tt(bb[1], tq[2], tq[3], ALU.add))

            shp = [P, PQ, L, 16]
            tx = [TT[:, 3, 512 * n:512 * (n + 1)].rearrange("p (g l c) -> p g l c", g=PQ, l=L) for n in range(2)]
            tn = [TT[:, 3, 512 * n:512 * (n + 1)].rearrange("p (g n) -> p g n", g=PQ) for n in range(2)]

            def power_rows(first, last, q):
                d = 1 if last > first else -1
                stop = last + d
                return [over(pw[:, r, first:(stop if stop >= 0 else None):d, PQ * q:PQ * (q + 1)]
                             .rearrange("p l g -> p g l").unsqueeze(3), shp) for r in range(2)]

            def build_xa(q):
                if q:
                    dve.wait_ge(ms_done, MS[f"b{q - 1}"] + 1)
                b = [over(bb[r][:, PQ * q:PQ * (q + 1), :].unsqueeze(2), shp) for r in range(2)]
                cmul((XA[:, 0], XA[:, 1]), power_rows(L - 1, 0, q), b, tx).then_inc(xa_ready, 1)
                dve.wait_ge(xa_ready, q + 1)

            def build_wo(q):
                if q:
                    dve.wait_ge(ms_done, MS[f"f{q - 1}"] + 1)
                c = [over(cb[r][:, PQ * q:PQ * (q + 1), :].unsqueeze(2), shp) for r in range(2)]
                cmul((WO[:, 0], WO[:, 1]), power_rows(1, L, q), c, tx, neg=True).then_inc(wo_ready, 1)
                dve.wait_ge(wo_ready, q + 1)

            def build_pt(q):
                link(dve.memset(PT[:, 0, :, 0:1], 1.0))
                link(dve.memset(PT[:, 1, :, 0:1], 0.0))
                for m in range(7):
                    s = 1 << m
                    turn = [over(rot[:, r, 3 + m, PQ * q:PQ * (q + 1)].unsqueeze(2), [P, PQ, s]) for r in range(2)]
                    link(cmul((PT[:, 0, :, s:2 * s], PT[:, 1, :, s:2 * s]), (PT[:, 0, :, 0:s], PT[:, 1, :, 0:s]),
                              turn, [t[:, :, 0:s] for t in tn]))

            def core(q):
                dve.wait_ge(ms_read, MS[f"d{q}"] + 1)
                if q:
                    dve.wait_ge(y_out, 16 * q)
                qs = slice(PQ * q, PQ * (q + 1))
                pr, pi = PT[:, 0], PT[:, 1]
                vr, vi = VV[:, 0, :, 0:NC], VV[:, 1, :, 0:NC]
                gr, gi = GV[:, 0], GV[:, 1]
                t = tn
                link(tt(t[0], pr, vr, ALU.mult))
                link(tt(t[1], pi, vi, ALU.mult))
                link(tt(gr, t[0], t[1], ALU.add))
                link(tt(t[0], pr, vi, ALU.mult))
                link(tt(t[1], pi, vr, ALU.mult))
                link(tt(gi, t[0], t[1], ALU.subtract))
                h0 = [p5c(n).rearrange("p (g b) -> p g b", b=NB)[:, qs, :] for n in ("h0_re", "h0_im")]
                a4 = [over(pw[:, r, NS, qs].unsqueeze(2), [P, PQ, NB]) for r in range(2)]
                ts = [x[:, :, 0:NB] for x in t]
                so = [SO[:, r, qs, 1:1 + NB] for r in range(2)]
                link(cmul(so, a4, h0, ts))
                for r in range(2):
                    link(tt(so[r], so[r], VV[:, r, :, NC:YW], ALU.add))
                link(dve.tensor_copy(t[0], over(sm[:, 4, qs].unsqueeze(2), [P, PQ, NC])))
                link(dve.memset(t[0][:, :, 0:1], 0.0))
                flat = t[0].rearrange("p g n -> p (g n)")
                for r in range(2):
                    g = GV[:, r].rearrange("p g n -> p (g n)")
                    link(dve.tensor_tensor_scan(g, flat, g, 0.0, ALU.mult, ALU.add))
                hv = [HV[:, r, :, NB + 1:NB + 1 + NC] for r in range(2)]
                link(cmul(hv, (gr, gi), (pr, pi), t))
                for r in range(2):
                    dve.memset(HV[:, r, :, NB:NB + 1], 0.0)
                    link(dve.tensor_copy(HV[:, r, :, 0:NB], h0[r]))
                    last = dve.tensor_copy(SO[:, r, qs, 0:1], HV[:, r, :, NB + NC:NB + NC + 1])
                    last.then_inc(st_ready, 1) if r else link(last)

            def z_in_sum(q):
                dve.wait_ge(y_in, 16 * GQ * (q + 1))
                dve.wait_ge(ud_in, 16 * (q + 1))
                u = U[:, q % 2, :, :].rearrange("p g w -> p (g w)").rearrange("p (l w) -> p l w", l=L)
                stt(YR, u[:, :, 0:YW], p_col("s5_d", q), YR, ALU.mult, ALU.add).then_inc(zin_done, 1)

            def decay(p):
                read_wait(dve, f"lg{p}")
                if p:
                    dve.wait_ge(lg_dve, 2)
                link(dve.tensor_scalar(TT[:, 1, :], TT[:, 0, :], 0.0, None, ALU.min))
                stt(TT[:, 2, :], TT[:, 1, :], 2.0, TT[:, 0, :], ALU.mult, ALU.subtract).then_inc(lg_dve, 1)
                dve.wait_ge(lg_act, p + 1)
                link(dve.tensor_scalar(TT[:, 2, :], TT[:, 2, :], 1.0 / 16, None, ALU.mult))
                stt(LA[:, p, :], TT[:, 1, :], 1.0 / 16, TT[:, 2, :], ALU.mult, ALU.subtract).then_inc(lg_dve, 1)

            build_xa(0)
            build_wo(0)
            build_pt(0)
            build_xa(1)
            core(0)
            decay(0)
            decay(1)
            for q in range(NG):
                if q + 1 < NG:
                    build_pt(q + 1)
                    build_wo(q + 1)
                if q + 2 < NG:
                    build_xa(q + 2)
                z_in_sum(q)
                if q + 1 < NG:
                    core(q + 1)

            for k in range(4):
                dve.wait_ge(z_in[k % 2], 16 * (k // 2 + 1))
                lo_part(XL[:, k, :], TT[:, k % 2, :], XH[:, k, :], SPLIT["z"] + k + 1)
            for m in range(4):
                dve.wait_ge(z_in[m % 2], 32 + 16 * (m // 2 + 1))
                read_wait(dve, f"glu{m}")
                row = TT[:, 2 + m % 2, :]
                tt(row, row, TT[:, m % 2, :], ALU.mult).then_inc(gg_done, 1)
                dve.wait_ge(gg_done, m + 1)
                lo_part(XL[:, 4 + m, :], row, XH[:, 4 + m, :], SPLIT["zg"] + m + 1)

            C16, E0, KE, KN = TT[:, 3, :], TT[:, 0, :], TT[:, 2, :], TT[:, 1, :]
            qp = QM[:, 0:2 * SEQ].rearrange("p (b e n) -> p e b n", e=2, n=BL)
            qc = QM[:, 0:2 * SEQ].rearrange("p (c i e n) -> p e c i n", i=NBL, e=2, n=BL)
            qi = QI[:, :].rearrange("p (c e i n) -> p e c i n", e=2, i=NBL, n=BL)
            qsm = QM[:, 2 * SEQ:2 * T].rearrange("p (e n) -> p e n", e=2)
            NBK = SEQ // BL
            link(dve.memset(QM[:, :], 0.0))
            dve.wait_ge(xl_done, SPLIT["o"])
            dve.wait_ge(z_out, 16 * NG)
            for p in range(2):
                g0 = 4 * p
                if p:
                    dve.wait_ge(sst_ready, NB)
                    dve.wait_ge(so_done, 1)
                mask = KX[:, 0, 0:T]
                link(dve.memset(mask, 1.0))
                link(dve.memset(mask[:, 0:SEQ].rearrange("p (b n) -> p b n", n=BL)[:, :, 0:1], 0.0))
                link(dve.memset(mask[:, SEQ:T].rearrange("p (b n) -> p b n", n=NS)[:, :, 0:1], 0.0))
                dve.tensor_tensor_scan(C16, mask, LA[:, p, :], 0.0, ALU.mult, ALU.add).then_inc(gd, 1)
                dve.wait_ge(gd, g0 + 1)
                link(dve.memset(gs[:, 5, :], 1.0))
                link(dve.memset(gs[:, 5, :].rearrange("p (c i) -> p c i", i=NBL)[:, :, 0:1], 0.0))
                link(dve.tensor_copy(gs[:, 0, :], C16[:, BL - 1:SEQ:BL]))
                link(dve.tensor_tensor_scan(gs[:, 1, :], gs[:, 5, :], gs[:, 0, :], 0.0, ALU.mult, ALU.add))
                link(tt(gs[:, 2, :], gs[:, 1, :], gs[:, 0, :], ALU.subtract))
                e3 = [gs[:, n, :].rearrange("p (c i) -> p c i", i=NBL) for n in range(4)]
                last = over(e3[1][:, :, NBL - 1:NBL], [P, NGC, NBL])
                link(tt(e3[3], last, e3[1], ALU.subtract))
                link(dve.memset(gs[:, 4, :], 0.0))
                link(dve.tensor_copy(gs[:, 4, 0:NGC], gs[:, 1, NBL - 1:NBK:NBL]))
                link(dve.tensor_copy(gs[:, 4, 8:8 + NB], C16[:, SEQ + NS - 1:T:NS]))
                g4 = [P, NGC, NBL, NBL]
                link(tt(GB[:, :, :, :], over(e3[2].unsqueeze(3), g4), over(e3[1].unsqueeze(2), g4), ALU.subtract))
                link(dve.tensor_scalar(GB[:, :, :, :], GB[:, :, :, :], 0.0, None, ALU.min))
                link(dve.tensor_copy(gs[:, 5, 0:NB], C16[:, SEQ + NS - 1:T:NS]))
                dve.wait_ge(ga, g0 + 1)
                for e in range(2):
                    h = slice(64 * e, 64 * e + 64)
                    stt(qp[h, e], Q[h, p, 0:SEQ].rearrange("p (b n) -> p b n", n=BL), 0.125,
                        E0[h, 0:SEQ].rearrange("p (b n) -> p b n", n=BL), ALU.mult, ALU.mult)
                    last = stt(qsm[h, e], Q[h, p, SEQ:T], 0.125, E0[h, SEQ:T], ALU.mult, ALU.mult)
                    last.then_inc(gd, 1) if e else link(last)
                dve.wait_ge(gd, g0 + 2)
                dve.wait_ge(ga, g0 + 2)
                link(tt(KN, K[:, p, :], E0, ALU.mult))
                link(tt(E0[:, 0:SEQ].rearrange("p (b n) -> p b n", n=BL), over(gs[:, 0, :].unsqueeze(2), [P, NBK, BL]),
                        C16[:, 0:SEQ].rearrange("p (b n) -> p b n", n=BL), ALU.subtract))
                tt(E0[:, SEQ:T].rearrange("p (b n) -> p b n", n=NS), over(gs[:, 5, 0:NB].unsqueeze(2), [P, NB, NS]),
                   C16[:, SEQ:T].rearrange("p (b n) -> p b n", n=NS), ALU.subtract).then_inc(gd, 1)
                dve.wait_ge(ga, g0 + 3)
                tt(KE, K[:, p, :], E0, ALU.mult).then_inc(gd, 1)
                dve.wait_ge(gd, g0 + 4)
                dve.wait_ge(ga, g0 + 4)
                link(tt(GB[:, :, :, :], GB[:, :, :, :],
                        over(c_("tri8").rearrange("p (i j) -> p i j", j=NBL).unsqueeze(1), g4), ALU.mult))
                for e in range(2):
                    link(tt(qi[:, e], qc[:, e], over(e3[2].unsqueeze(3), [P, NGC, NBL, BL]), ALU.mult))
                link(dve.tensor_copy(E0[:, SEQ:T], KE[:, SEQ:T]))
                tt(E0[:, 0:SEQ].rearrange("p (b n) -> p b n", n=BL), KE[:, 0:SEQ].rearrange("p (b n) -> p b n", n=BL),
                   over(gs[:, 3, :].unsqueeze(2), [P, NBK, BL]), ALU.mult).then_inc(pair_ready, 1)

                def key_blocks(it):
                    c, b = it % NGC, it % 2
                    if it >= 2:
                        dve.wait_ge(sc_done, it - 1)
                    dst = KX[:, b, 0:NBL * GC].rearrange("p (i j n) -> p i j n", i=NBL, j=NBL)
                    src = KE[:, c * GC:(c + 1) * GC].rearrange("p (j n) -> p j n", n=BL)
                    shape = [P, NBL, NBL, BL]
                    link(tt(dst, over(src.unsqueeze(1), shape), over(GB[:, c, :, :].unsqueeze(3), shape), ALU.mult))
                    own = KX[:, b, :].rearrange("p (i x) -> p i x", x=GC + BL)[:, :, 0:BL]
                    dve.tensor_copy(own, KN[:, c * GC:(c + 1) * GC].rearrange("p (j n) -> p j n", n=BL))\
                       .then_inc(kx_ready, 1)

                key_blocks(NGC * p)
                for it in range(NGC * p, NGC * (p + 1)):
                    c, b = it % NGC, it % 2
                    if c + 1 < NGC:
                        key_blocks(it + 1)
                    dve.wait_ge(sc_done, it + 1)
                    if it >= 2:
                        dve.wait_ge(o_done, it - 1)
                    tt(SC[:, b, :].rearrange("p (e i n) -> p i e n", e=2, n=BL),
                       glb[:, b, 0:2 * GC].rearrange("p (i e n) -> p i e n", e=2, n=BL),
                       over(tri.unsqueeze(2), [P, NBL, 2, BL]), ALU.mult).then_inc(sc_ready, 1)
                    dve.wait_ge(kv_done, it + 1)
                    if c == 0:
                        dve.tensor_copy(S[:, p, :], glb[:, 5, 0:P]).then_inc(s_ready, 1)
                    else:
                        dve.wait_ge(s_ready, it)
                        stt(S[:, p, :], S[:, p, :], gs[:, 4, c:c + 1], glb[:, 5, 0:P], ALU.mult, ALU.add)\
                            .then_inc(s_ready, 1)
                dve.wait_ge(sm_done, 2 * p + 2)
                dve.wait_ge(o_done, NGC * (p + 1))
                tt(SC[0:32, 0, 0:64].rearrange("p (e n) -> p e n", e=2), glb[0:32, 0, 0:64].rearrange("p (e n) -> p e n", e=2),
                   over(c_("smask")[0:32, :].unsqueeze(1), [32, 2, 32]), ALU.mult).then_inc(smc_ready, 1)
                kts = KX[0:32, :, :].rearrange("p a n -> p (a n)")[:, 0:NB * P].rearrange("p (s n) -> p s n", s=NB)
                tt(kts, over(glb[0:32, 4, 0:P].unsqueeze(1), [32, NB, P]),
                   over(c_("bmask")[0:32, :].unsqueeze(2), [32, NB, P]), ALU.mult).then_inc(smk_ready, 1)
                dve.wait_ge(skv_done, p + 1)
                for s in range(NB):
                    stt(SS[:, s, :], SS[:, s, :], gs[:, 4, 8 + s:9 + s], glb[:, 5 if s < 4 else 1, (s % 4) * P:(s % 4 + 1) * P],
                        ALU.mult, ALU.add).then_inc(sst_ready, 1)

            for h in range(4):
                read_wait(dve, f"head{h}")
                if h == 0:
                    dve.wait_ge(so_read, 2)
                link(dve.reciprocal(TT[:, 1, :], TT[:, 1, :]))
                link(stt(TT[:, 1, :], TT[:, 1, :], p_col("g_head", h), (Q, K)[h % 2][:, h // 2, :], ALU.mult, ALU.mult))
                dve.wait_ge(g_in, 16 * (h + 1))
                if h:
                    dve.wait_ge(xl_done, SPLIT["o"] + h)
                tt(TT[:, 2, :], TT[:, 1, :], TT[:, 3, :], ALU.mult).then_inc(gg_done, 1)
                dve.wait_ge(gg_done, 4 + h + 1)
                lo_part(XL[:, h, :], TT[:, 2, :], XH[:, h, :], SPLIT["o"] + h + 1)
            dve.wait_ge(xr_in, 16 * KT)

            def add_to_residual(m, t, per5=0, before=None):
                dve.wait_ge(acc_done[t % 2], per5 + (t // 2 + 1))
                if before is not None:
                    dve.wait_ge(acc_read[t % 2], before)
                tt(cut(X[:, m, :]), cut(X[:, m, :]), bank(t), ALU.add).then_inc(acc_read[t % 2], 1)

            def mlp(layer):
                t0, h0 = ACC[f"mlp{layer}_0"], FT * layer

                def hidden(t, per5, hcount, slot, u):
                    dve.wait_ge(acc_read[t % 2], per5 + (t // 2 + 1))
                    link(tt(HH[:, slot, :], TT[:, u, :], TT[:, u, :], ALU.mult))
                    dve.wait_ge(h_sq, hcount + 1)
                    tt(HL[:, slot, :], TT[:, 2 + u, :], HH[:, slot, :].bitcast(F32), ALU.subtract).then_inc(h_ready, 1)

                for j in range(2):
                    hidden(t0 + j, 0, h0 + j, j, j)
                step.loop(None, 0)
                with dve.Fori(0, HG // 2 - 1) as i:
                    step.loop(i, 4)
                    for a in range(2):
                        for j in range(2):
                            hidden(t0 + 2 + 10 * a + j, i * 10, i * 4 + (h0 + 2 * (a + 1) + j), (2 * (a + 1) + j) % 4, j)
                        for m in range(KT):
                            t = t0 + 4 + 10 * a + m
                            add_to_residual(m, t, i * 10, i * 10 + (t // 2 - 4))
                    step.end(HG // 2 - 1)
                a = HG - 2
                for j in range(2):
                    hidden(t0 + 2 + 10 * a + j, 0, h0 + 2 * (a + 1) + j, (2 * (a + 1) + j) % 4, j)
                for a, at in ((HG - 2, t0 + 4 + 10 * a), (HG - 1, t0 + 12 + 10 * a)):
                    for m in range(KT):
                        add_to_residual(m, at + m, 0, (at + m) // 2 - 3)

            for m in range(KT):
                add_to_residual(m, ACC[f"oute{m}"])
            norm(1)
            mlp(0)
            norm(2)
            link(dve.memset(XP[:, :, 0:3], 0.0))
            link(dve.tensor_scalar(spt[:, :], par[:, PAR["lam"][0]:PAR["lam"][1]], 0.0, None, ALU.min))
            stt(spt[:, :], spt[:, :], 2.0, par[:, PAR["lam"][0]:PAR["lam"][1]], ALU.mult, ALU.subtract).then_inc(tg_done, 1)
            dve.nop().then_inc(xp_ready, 1)
            dve.wait_ge(sp_act, 1)
            dve.wait_ge(tg_done, 1)
            link(dve.tensor_scalar(sp4[:, :], par[:, PAR["lam"][0]:PAR["lam"][1]], 0.0, -1.0, ALU.min, ALU.mult))
            link(tt(sp4[:, :], sp4[:, :], spt[:, :], ALU.add))
            dve.tensor_scalar(sp4[:, :], sp4[:, :], 4.0, None, ALU.mult).then_inc(tg_done, 1)
            dve.wait_ge(odd_in, 32)

            def conv(n):
                read_wait(dve, f"xb{n}")
                smp = XP[:, n % 2, 3 + SEQ:].rearrange("p (b s) -> p b s", b=NB)
                outs = HB[:, n, 0:SEQ], HB[:, n, SEQ:T].rearrange("p (b s) -> p b s", b=NB)
                for j in range(4):
                    w = par[:, PAR["conv_w"][0] + 4 * n + j:PAR["conv_w"][0] + 4 * n + j + 1]
                    for out, x in zip(outs, (XP[:, n % 2, j:j + SEQ], smp[:, :, j:j + NS])):
                        if j == 0:
                            link(dve.tensor_scalar(out, x, w, p_col("conv_b", n), ALU.mult, ALU.add))
                        elif j < 3:
                            link(stt(out, x, w, out, ALU.mult, ALU.add))
                        else:
                            step.run(stt(out, x, w, out, ALU.mult, ALU.add))
                dve.tensor_copy(CN[:, n, 0:3], XP[:, n % 2, SEQ:SEQ + 3])
                dve.tensor_copy(CN[:, n, 3:].rearrange("p (b s) -> p b s", b=NB), smp[:, :, NS:NS + 3]).then_inc(conv_done, 1)
                dve.wait_ge(conv_done, n + 1)

            def recur(n):
                dve.wait_ge(sig_done, 2 * n + 1)
                link(dve.tensor_scalar(TT[:, 2, :], TT[:, 0, :], 1.0, None, ALU.add))
                link(dve.reciprocal(TT[:, 2, :], TT[:, 2, :]))
                link(tt(TT[:, 1, :], TT[:, 1, :], HB[:, n, :], ALU.mult))
                dve.wait_ge(sig_done, 2 * n + 2)
                link(stt(TT[:, 3, :], TT[:, 3, :], 2.0, TT[:, 2, :], ALU.mult, ALU.mult))
                link(tt(TT[:, 3, :], TT[:, 3, :], TT[:, 1, :], ALU.mult))
                link(dve.tensor_scalar(TT[:, 2, :], TT[:, 2, :], 2.0, -1.0, ALU.mult, ALU.add))
                a0, b0 = TT[:, 2, SEQ:T:NS], TT[:, 3, SEQ:T:NS]
                link(tt(spt[:, 0:NB], a0, st_lru[:, n, :], ALU.mult))
                link(tt(b0, b0, spt[:, 0:NB], ALU.add))
                link(dve.memset(a0, 0.0))
                dve.tensor_tensor_scan(HB[:, n, :], TT[:, 2, :], TT[:, 3, :], 0.0, ALU.mult, ALU.add).then_inc(gt_done, 1)
                dve.wait_ge(gt_done, n + 1)
                dve.tensor_copy(LN[:, n, 0:1], HB[:, n, SEQ - 1:SEQ])
                link(dve.tensor_copy(LN[:, n, 1:], HB[:, n, SEQ + NS - 1:T:NS]))

            def apply_gate(m):
                read_wait(dve, f"gate{m}")
                tt(HB[:, m, :], HB[:, m, :], TT[:, m % 2, :], ALU.mult).then_inc(hb_ready, 1)

            conv(0)
            for n in range(KT):
                if n + 1 < KT:
                    conv(n + 1)
                recur(n)
                if n >= KT - 2:
                    apply_gate(n + 2 - KT)
            for m in range(2, KT):
                apply_gate(m)
            for k in range(KT):
                dve.wait_ge(hb_ready, k + 1)
                lo_part(XL[:, k, :], HB[:, k, :], XH[:, k, :], SPLIT["mix"] + k + 1)
            for m in range(KT):
                add_to_residual(m, ACC[f"outo{m}"])
            norm(3)
            mlp(1)
            norm(4)


def tiles(w, m):
    k = w.shape[0] // P
    return w.reshape(k, P, m, P).transpose(2, 1, 0, 3).reshape(m, P, k * P)


def kernel(**inputs):
    import numpy as np
    import concourse.bacc as bacc
    from concourse.bass_utils import run_bass_kernel_spmd as run

    x = {k: np.asarray(v) for k, v in inputs.items()}
    f32 = np.float32
    tok = np.concatenate([x["x_prompt"].reshape(SEQ, D), x["x_sample"].reshape(NB * NS, D)])
    x_t = np.ascontiguousarray(tok.T).reshape(KT, P, T)

    w = x["w_in_even"][0]
    wv = w[:, 512:1024].reshape(4, 2, P, 512).transpose(0, 2, 1, 3).reshape(4, P, 1024)
    walr = np.zeros((D, P), f32)
    walr[:, :16] = w[:, 1536:1552]
    glu = tiles(x["s5_w_glu"][0], 4).reshape(2, 2, P, 512).transpose(0, 2, 1, 3).reshape(2, P, 1024)

    def mlp_tiles(layer):
        up = tiles(x["w_up"][layer], FT)
        down = x["w_down"][layer].reshape(FT, P, D)
        order = [up[0:2]]
        for a in range(1, HG):
            order += [up[2 * a:2 * a + 2], down[2 * a - 2:2 * a]]
        return np.concatenate(order + [down[FT - 2:FT]])

    w_odd = x["w_in_odd"][0]
    w_stream = np.concatenate([
        tiles(w[:, 1552:], 4), tiles(walr, 1), tiles(w[:, 0:256], 2), tiles(w[:, 256:512], 2),
        tiles(w[:, 1024:1536], 4), wv, glu, tiles(x["w_out_even"][0], KT), mlp_tiles(0),
        tiles(w_odd[:, D:], KT), tiles(w_odd[:, :D], KT), tiles(x["w_out_odd"][0], KT), mlp_tiles(1)])
    assert w_stream.shape == (NT, P, 1024)

    def cols(v):
        return v.reshape(-1, P).T

    par = np.concatenate([
        cols(x["norm_mix_even"][0]), cols(x["norm_mlp"][0]), cols(x["norm_mix_odd"][0]), cols(x["norm_mlp"][1]),
        cols(x["norm_final"]), cols(x["gla_norm"][0]), cols(x["gla_b_a2"][0]), cols(x["s5_d"][0].reshape(-1)),
        cols(x["s5_b_glu"][0]), x["conv_w"][0].reshape(4, KT, P).transpose(2, 1, 0).reshape(P, 32),
        cols(x["conv_b"][0]), cols(x["lru_b_r"][0]), cols(x["lru_b_i"][0]), cols(x["lru_lam"][0])], axis=1)

    def states(v):
        v = v.reshape((16, 2, 64) + v.shape[2:])
        return np.moveaxis(v, 0, 2).reshape(P, -1)

    dt = np.broadcast_to(x["s5_log_dt"][0][:, None], (32, 64))
    par5 = np.concatenate([
        states(x["s5_a_re"][0]), states(x["s5_a_im"][0]), states(dt), states(x["s5_b_re"][0]), states(x["s5_b_im"][0]),
        states(x["s5_c_re"][0].transpose(0, 2, 1)), states(x["s5_c_im"][0].transpose(0, 2, 1)),
        states(x["state_s5_re"][0].transpose(1, 2, 0)), states(x["state_s5_im"][0].transpose(1, 2, 0))], axis=1)

    cst = np.zeros((P, NCST), f32)
    i = np.arange(P)
    cst[:, 0:128] = np.eye(P)
    cst[:, 128:256] = i[:, None] <= i[None, :]
    j = np.arange(32)
    cst[0:32, 256:288] = (j[:, None] <= j[None, :]) & (j[:, None] // NS == j[None, :] // NS)
    cst[0:32, 288:296] = j[:, None] // NS == np.arange(NB)[None, :]
    b = np.arange(NBL)
    cst[:, 296:360] = (b[None, :] < b[:, None]).reshape(1, -1)

    w_ri = np.stack([x["lru_w_r"][0], x["lru_w_i"][0]], axis=1).transpose(0, 2, 1, 3)
    st_gla = x["state_gla"][0].reshape(NB, 2, P, P).transpose(1, 2, 0, 3)
    odd_lru = x["state_lru"][0].reshape(NB, KT, P).transpose(2, 1, 0)
    odd_conv = x["state_conv"][0].reshape(NB, 3, KT, P).transpose(3, 2, 0, 1)

    nc = bacc.Bacc("TRN2", target_bir_lowering=False, num_devices=1)
    arrays, args = {}, []
    for name, a in (("x_t", x_t), ("w_stream", w_stream), ("par", par), ("par5", par5), ("cst", cst),
                    ("w_a2", x["gla_w_a2"][0]), ("w_ri", w_ri), ("st_gla", st_gla), ("odd_lru", odd_lru),
                    ("odd_conv", odd_conv)):
        arrays[f"in_{name}"] = np.ascontiguousarray(a)
        args.append(nc.dram_tensor(f"in_{name}", a.shape, F32, kind="ExternalInput").ap())
    for name, shape in (("y_t", (KT, P, T)), ("s5_out", (P, 2, 16, 1 + NB)), ("lru_out", (P, KT, 1 + NB)),
                        ("conv_out", (P, KT, 3 * (1 + NB))), ("gla_p", (P, 2, P)), ("gla_s", (2, P, NB, P))):
        args.append(nc.dram_tensor(f"out_{name}", shape, F32, kind="ExternalOutput").ap())
    trunk_kernel(nc, *args)
    r = run(nc, [arrays], core_ids=[0]).results[0]
    r = {k.removeprefix("out_"): np.asarray(v) for k, v in r.items()}

    y = r["y_t"].reshape(D, T).T
    s5 = r["s5_out"].reshape(2, 64, 2, 16, 1 + NB).transpose(2, 4, 3, 0, 1).reshape(2, 1 + NB, 32, 64)
    lru = r["lru_out"].transpose(2, 1, 0).reshape(1 + NB, D)
    conv = r["conv_out"].reshape(P, KT, 1 + NB, 3).transpose(2, 3, 1, 0).reshape(1 + NB, 3, D)
    gla_prompt = r["gla_p"].reshape(2, 64, 2, P).transpose(2, 0, 1, 3).reshape(1, 1, 4, 64, P)
    gla_sample = r["gla_s"].reshape(2, 2, 64, NB, P).transpose(3, 0, 1, 2, 4).reshape(1, NB, 4, 64, P)
    c = np.ascontiguousarray
    return (c(y[:SEQ]).reshape(1, SEQ, D), c(y[SEQ:]).reshape(NB, NS, D),
            c(gla_prompt), c(s5[0, :1])[None], c(s5[1, :1])[None], c(lru[:1])[None], c(conv[:1])[None],
            c(gla_sample), c(s5[0, 1:])[None], c(s5[1, 1:])[None], c(lru[1:])[None], c(conv[1:])[None])
```

```python
from contextlib import ExitStack

import concourse.bass as bass
from concourse import mybir

F32 = mybir.dt.float32
F32R = mybir.dt.float32r
ALU = mybir.AluOpType
ACT = mybir.ActivationFunctionType

P = 128
D = 1024
KT = D // P
SEQ = 1024
NB, NS = 8, 4
T = SEQ + NB * NS
CH = 352
NCH = T // CH
FT = 4 * D // P
EPS = 1e-6

PAR = {}
_at = 0
for _name, _n in (("g_mix_even", 8), ("g_mlp0", 8), ("g_mix_odd", 8), ("g_mlp1", 8), ("g_final", 8),
                  ("g_head", 4), ("b_a2", 2), ("s5_d", 4), ("b_glu", 4), ("conv_w", 32), ("conv_b", 8),
                  ("b_r", 8), ("b_i", 8), ("lam", 8)):
    PAR[_name] = (_at, _at + _n)
    _at += _n
NPAR = _at
PAR5 = {}
_at = 0
for _name, _n in (("a_re", 16), ("a_im", 16), ("log_dt", 16), ("b_re", 256), ("b_im", 256),
                  ("c_re", 256), ("c_im", 256), ("h0_re", 128), ("h0_im", 128)):
    PAR5[_name] = (_at, _at + _n)
    _at += _n
NPAR5 = _at
CST = {"ident": (0, 128), "tri": (128, 256), "smask": (256, 288), "bmask": (288, 296), "tri8": (296, 360),
       "count": (360, 488)}
NCST = 488


class Chain:

    def __init__(self, eng, sem):
        self.eng, self.sem, self.n, self.var, self.per = eng, sem, 0, None, 0

    def run(self, ins):
        self.n += 1
        return ins.then_inc(self.sem, 1)

    def value(self):
        return self.n if self.var is None else self.var * self.per + self.n

    def wait(self):
        self.eng.wait_ge(self.sem, self.value())

    def link(self, ins):
        self.run(ins)
        self.wait()

    def loop(self, var, per):
        self.var, self.per, self.first = var, per, self.n

    def end(self, trips):
        assert self.n - self.first == self.per, (self.n - self.first, self.per)
        self.var, self.n = None, self.first + self.per * trips


def index(names):
    return {name: n for n, name in enumerate(names)}


HG = FT // 2
MLP_TILES = 2 * FT
STREAM = index(["u0", "u1", "u2", "u3", "q0", "q1", "g0", "g1", "g2", "g3", "k0", "k1", "alr",
                "v0", "v1", "v2", "v3", "glu0", "glu1"] + [f"oute{m}" for m in range(KT)]
               + [f"mlp0_{n}" for n in range(MLP_TILES)]
               + [f"xb{n}" for n in range(KT)] + [f"gate{n}" for n in range(KT)]
               + [f"outo{m}" for m in range(KT)] + [f"mlp1_{n}" for n in range(MLP_TILES)])
NT = len(STREAM)
RAW, SLOTS = 2, 4
POOL_LOADS = 20

_odd = ["xb0", "xb1"]
for _n in range(KT):
    _odd += [f"r{_n}", f"i{_n}"] + ([f"xb{_n + 2}"] if _n + 2 < KT else [f"gate{_n + 2 - KT}"])
_odd += [f"gate{_n}" for _n in range(2, KT)]
ACC = index(["norm0", "u0", "u1", "u2", "u3", "q0", "q1", "g0", "g1", "g2", "g3",
        "k0", "k1", "alr", "lg0", "lg1", "v0", "v1", "v2", "glu0", "glu1", "glu2", "glu3",
             "head0", "head1", "head2", "head3"] + [f"oute{m}" for m in range(KT)]
            + ["norm1"] + [f"mlp0_{n}" for n in range(HG * (2 + KT))]
            + ["norm2"] + _odd + [f"outo{m}" for m in range(KT)]
            + ["norm3"] + [f"mlp1_{n}" for n in range(HG * (2 + KT))] + ["norm4"])

SPLIT = {}
_at = 0
for _name, _n in (("norm0", NCH * KT), ("z", 4), ("zg", 4), ("o", 4), ("norm1", NCH * KT), ("norm2", NCH * KT), ("mix", 8), ("norm3", NCH * KT)):
    SPLIT[_name] = _at
    _at += _n

SSQ_N = KT - 1 + NCH
L = 8
NC = SEQ // L
PQ = 4
GQ = 8
NG = 4
CW = NC + 2 * NB
YW = NC + NB
GC = 128
NGC = SEQ // GC
BL = 16
NBL = GC // BL
MAGIC = 1.5 * 2.0 ** 23
CUT12 = 1.5 * 2.0 ** 13
TWO_PI_1, TWO_PI_2, TWO_PI_3 = 6.28125, 0.0019350051879882812, 3.0199159819567e-07


def trunk_kernel(nc, x_t, w_stream, par_d, par5_d, cst_d, w_a2, w_ri, st_gla, odd_lru, odd_conv,
                 y_t, s5_out, lru_out, conv_out, gla_p, gla_s):
    u_scr = nc.dram_tensor("u_scratch", (NG, P, L, CW), F32, kind="Internal").ap()
    y_scr = nc.dram_tensor("y_scratch", (NG, P, GQ, YW), F32, kind="Internal").ap()
    z_scr = nc.dram_tensor("z_scratch", (NG, P, T), F32, kind="Internal").ap()
    g_scr = nc.dram_tensor("g_scratch", (NG, P, T), F32, kind="Internal").ap()

    with ExitStack() as ctx:
        def sem(name):
            return ctx.enter_context(nc.semaphore(name))

        def sb(stack, name, shape, dt=F32):
            return stack.enter_context(nc.sbuf_tensor(name, shape, dt))

        XH = sb(ctx, "XH", [P, KT, T], F32R)
        XL = sb(ctx, "XL", [P, KT, T], F32R)
        WR = sb(ctx, "WR", [P, RAW, 1024])
        WH = sb(ctx, "WH", [P, SLOTS, 1024], F32R)
        WL = sb(ctx, "WL", [P, SLOTS, 1024], F32R)
        TT = sb(ctx, "TT", [P, 4, T])
        par = sb(ctx, "par", [P, NPAR])
        cst = sb(ctx, "cst", [P, NCST])
        ones = sb(ctx, "ones", [P, P])
        few = sb(ctx, "few", [P, 4])
        sp4 = sb(ctx, "sp4", [P, KT])
        spt = sb(ctx, "spt", [P, KT])
        SO = sb(ctx, "SO", [P, 2, 16, 1 + NB])
        with ExitStack() as area:
            X0 = sb(area, "X0", [P, KT, T])
        with ExitStack() as area:
            Q = sb(area, "Q", [P, 2, T])
            with ExitStack() as s5b:
                PTR = sb(s5b, "PTR", [P, 2, 12, NC])
                VH1 = sb(s5b, "VH1", [P, 2 * PQ * 144])
            K = sb(area, "K", [P, 2, T])
            LA = sb(area, "LA", [P, 2, T])
            with ExitStack() as s5a:
                XA = sb(s5a, "XA", [P, 2, PQ, L, 16])
                WIN = sb(s5a, "WIN", [P, 2, PQ, P])
                WO = sb(s5a, "WO", [P, 2, PQ, L, 16])
                M = sb(s5a, "M", [P, GQ, L, 16])
                T7 = sb(s5a, "T7", [P, GQ * 16])
                PT0 = sb(s5a, "PT0", [P, 2, PQ, NC])
                U = sb(s5a, "U", [P, 2, GQ, CW])
                VH0 = sb(s5a, "VH0", [P, 2 * PQ * 144])
                G = sb(s5a, "G", [P, GQ * YW])
                UR = sb(s5a, "UR", [P, L, CW])
                p5 = sb(s5a, "p5", [P, NPAR5])
                pw = sb(s5a, "pw", [P, 2, 9, 16])
                rot = sb(s5a, "rot", [P, 2, 16])
                sm = sb(s5a, "sm", [P, 14, 16])
                CB = sb(s5a, "CB", [P, 2, 16, 32])
                wa2 = sb(s5a, "wa2", [16, 2 * P])
            with ExitStack() as gla:
                V = sb(gla, "V", [P, NGC + 1, 512])
                QM = sb(gla, "QM", [P, 2 * T])
                QI = sb(gla, "QI", [P, 2 * SEQ])
                KX = sb(gla, "KX", [P, 2, 1152])
                SC = sb(gla, "SC", [P, 2, 256])
                KTR = sb(gla, "KTR", [P, 2, P])
                S = sb(gla, "S", [P, 2, P])
                GB = sb(gla, "GB", [P, NGC, NBL, NBL])
                gs = sb(gla, "gs", [P, 6, 64])
                SS = sb(gla, "SS", [P, NB, P])
        X = sb(ctx, "X", [P, KT, T])
        with ExitStack() as area:
            HH = sb(area, "HH", [P, 4, T], F32R)
            HL = sb(area, "HL", [P, 4, T], F32R)
        HB = sb(ctx, "HB", [P, KT, T])
        XP = sb(ctx, "XP", [P, 2, 3 + SEQ + 7 * NB])
        WRI = sb(ctx, "WRI", [P, 2, 2, P])
        st_lru = sb(ctx, "st_lru", [P, KT, NB])
        st_conv = sb(ctx, "st_conv", [P, KT, NB, 3])
        LN = sb(ctx, "LN", [P, KT, 1 + NB])
        CN = sb(ctx, "CN", [P, KT, 3 * (1 + NB)])
        acc = ctx.enter_context(nc.psum_tensor("acc", [P, 2, NCH, 512], F32))
        ms = ctx.enter_context(nc.psum_tensor("ms", [P, 2, 512], F32))
        glb = acc[:, :, :, :].rearrange("p s c n -> p (s c) n")

        par_in, par5_in, cst_in, wa2_in = sem("par_in"), sem("par5_in"), sem("cst_in"), sem("wa2_in")
        x_in = [sem(f"x_in{c}") for c in range(NCH)]
        xr_in = sem("xr_in")
        w_first = [sem(f"w_first{r}") for r in range(RAW)]
        w_in = [sem(f"w_in{r}") for r in range(RAW)]
        u_out, m_in, y_out, y_in, ud_in = sem("u_out"), sem("m_in"), sem("y_out"), sem("y_in"), sem("ud_in")
        u_in = [sem("u_in0"), sem("u_in1")]
        z_out, g_out = sem("z_out"), [sem("g_out0"), sem("g_out1")]
        z_in = [sem("z_in0"), sem("z_in1")]
        g_in = [sem("g_in0"), sem("g_in1")]
        ss_in, ss_out, s_out = sem("ss_in"), sem("ss_out"), sem("s_out")
        odd_in, wri_in = sem("odd_in"), [sem("wri_in0"), sem("wri_in1")]
        y_sent, small_out = sem("y_sent"), sem("small_out")
        w_hi, w_ready, w_used = sem("w_hi"), sem("w_ready"), sem("w_used")
        acc_done = [sem("acc_done0"), sem("acc_done1")]
        acc_read = [sem("acc_read0"), sem("acc_read1")]
        sq_done, ssq_add, rs_done, xn_done = sem("sq_done"), sem("ssq_add"), sem("rs_done"), sem("xn_done")
        sq_used, res_part, norm_sum, ln_done = sem("sq_used"), sem("res_part"), sem("norm_sum"), sem("ln_done")
        head_g, head_rs = sem("head_g"), sem("head_rs")
        xh_done, xl_done = sem("xh_done"), sem("xl_done")
        h_sq, h_ready = sem("h_sq"), sem("h_ready")
        ms_done, ms_read = sem("ms_done"), sem("ms_read")
        prep_act, prep_dve, const_ready = sem("prep_act"), sem("prep_dve"), sem("const_ready")
        angle_ready, pt_ready = sem("angle_ready"), sem("pt_ready")
        ur_ready, xa_ready, wo_ready, st_ready, zin_done, z_done = (sem("ur_ready"), sem("xa_ready"), sem("wo_ready"),
                                                                    sem("st_ready"), sem("zin_done"), sem("z_done"))
        alr_ready, lg_dve, lg_act, g_done = sem("alr_ready"), sem("lg_dve"), sem("lg_act"), sem("g_done")
        z_ready, gg_done = sem("z_ready"), sem("gg_done")
        ga, gd, pair_ready = sem("ga"), sem("gd"), sem("pair_ready")
        kx_ready, sc_done, sc_ready, kt_done, kt_ready = (sem("kx_ready"), sem("sc_done"), sem("sc_ready"),
                                                          sem("kt_done"), sem("kt_ready"))
        o_done, o_read, kv_done, s_ready = sem("o_done"), sem("o_read"), sem("kv_done"), sem("s_ready")
        sm_done, smk_ready, smc_ready, so_done, so_read, skv_done, sst_ready = (
            sem("sm_done"), sem("smk_ready"), sem("smc_ready"), sem("so_done"), sem("so_read"), sem("skv_done"),
            sem("sst_ready"))
        xp_ready, conv_done, sig_done, gt_done, hb_ready = (sem("xp_ready"), sem("conv_done"), sem("sig_done"),
                                                            sem("gt_done"), sem("hb_ready"))
        tg_done, sp_act = sem("tg_done"), sem("sp_act")
        dve_step, act_step = sem("dve_step"), sem("act_step")

        def p_col(name, n):
            return par[:, PAR[name][0] + n:PAR[name][0] + n + 1]

        def p5c(name):
            return p5[:, PAR5[name][0]:PAR5[name][1]]

        def c_(name):
            return cst[:, CST[name][0]:CST[name][1]]

        def cut(ap):
            return ap.rearrange("p (c n) -> p c n", n=CH)

        def bank(t):
            return acc[:, t % 2, :, 0:CH]

        def cols_of(c):
            return slice(c * CH, (c + 1) * CH)

        def done_wait(eng, name):
            t = ACC[name]
            eng.wait_ge(acc_done[t % 2], t // 2 + 1)

        def read_wait(eng, name):
            t = ACC[name]
            eng.wait_ge(acc_read[t % 2], t // 2 + 1)

        MS = index("a0 b0 c0 d0 a1 b1 c1 d1 e0 f0 a2 b2 e1 f1 c2 d2 a3 b3 e2 f2 c3 d3 e3 f3".split())
        ident, tri = c_("ident"), c_("tri").rearrange("p (i n) -> p i n", i=NBL)
        def VV(q):
            return (VH0, VH1)[q % 2][:, 0:2 * PQ * YW].rearrange("p (r q n) -> p r q n", r=2, q=PQ)

        def HV(q):
            return (VH0, VH1)[q % 2][:, :].rearrange("p (r q n) -> p r q n", r=2, q=PQ)

        def YR(q):
            return (VH0, VH1)[q % 2][:, 0:L * YW].rearrange("p (l n) -> p l n", l=L)

        def GV(q):
            flat = G if q == 0 else UR[:, :, :].rearrange("p l n -> p (l n)")
            return flat[:, 0:2 * PQ * NC].rearrange("p (r q n) -> p r q n", r=2, q=PQ)

        YG = G[:, :].rearrange("p (g n) -> p g n", g=GQ)
        ALR = UR[:, :, :].rearrange("p l n -> p (l n)")[0:16, 0:T]
        block = ctx.enter_context(nc.Block())

        @block.sync
        def _(sp):
            sp.dma_start(par[:, :], par_d).then_inc(par_in, 16)
            for c in range(NCH):
                sp.dma_start(X0[:, :, cols_of(c)], x_t.rearrange("k p t -> p k t")[:, :, cols_of(c)]).then_inc(x_in[c], 16)
            sp.dma_start(cst[:, :], cst_d).then_inc(cst_in, 16)
            sp.dma_start(p5[:, :], par5_d).then_inc(par5_in, 16)
            sp.dma_start(wa2[:, :], w_a2).then_inc(wa2_in, 16)

            def store_u(q):
                read_wait(sp, f"u{q}")
                sp.dma_start(u_scr[q], UR[:, :, :]).then_inc(u_out, 16)

            def load_u(q):
                sp.wait_ge(u_out, 16 * (q + 1))
                if q >= 2:
                    sp.wait_ge(zin_done, q - 1)
                src = u_scr[q].rearrange("(g c) l w -> l c g w", g=GQ)
                for j in range(L):
                    sp.dma_start(U[16 * j:16 * j + 16, q % 2, :, :], src[j]).then_inc(u_in[q % 2], 16)

            def load_m(q):
                sp.wait_ge(ms_read, MS[f"b{q}"] + 1)
                if q >= 1:
                    sp.wait_ge(ms_done, MS[f"f{q - 1}"] + 1)
                for i in range(L):
                    sp.dma_start(M[0:16 * (i + 1), :, i, :],
                                 T7[16 * (L - 1 - i):P, :].rearrange("p (g c) -> p g c", c=16)).then_inc(m_in, 16)

            def turn_y(q):
                sp.wait_ge(ms_read, MS[f"f{q}"] + 1)
                sp.dma_start(y_scr[q], YG).then_inc(y_out, 16)
                sp.wait_ge(y_out, 16 * (q + 1))
                src = y_scr[q].rearrange("(i c) g n -> g c i n", i=L)
                for g in range(GQ):
                    sp.dma_start(YR(q)[16 * g:16 * g + 16], src[g]).then_inc(y_in, 16)
                sp.dma_start(U[:, q % 2, :, :].rearrange("p g w -> p (g w)"),
                             u_scr[q].rearrange("p l w -> p (l w)")).then_inc(ud_in, 16)

            store_u(0)
            load_u(0)
            store_u(1)
            load_u(1)
            store_u(2)
            sp.wait_ge(u_out, 48)
            store_u(3)
            load_m(0)
            for q in range(NG):
                if q + 1 < NG:
                    load_m(q + 1)
                turn_y(q)
                if q + 2 < NG:
                    load_u(q + 2)
                sp.wait_ge(z_done, q + 1)
                sp.dma_start(z_scr[q], TT[:, 2, :]).then_inc(z_out, 16)
            sp.wait_ge(z_out, 16 * NG)
            for r in range(2):
                sp.wait_ge(g_out[r], 32)
            sp.wait_ge(lg_dve, 4)
            for k in range(NG):
                if k >= 2:
                    sp.wait_ge(xl_done, SPLIT["z"] + k - 1)
                sp.dma_start(TT[:, k % 2, :], z_scr[k]).then_inc(z_in[k % 2], 16)
            for k in range(NG):
                sp.wait_ge(xl_done, (SPLIT["z"] + k + 3) if k < 2 else (SPLIT["zg"] + k - 1))
                sp.dma_start(TT[:, k % 2, :], z_scr[k]).then_inc(z_in[k % 2], 16)
            def load_w(n, r, first=False):
                sp.wait_ge(w_ready, n - (RAW - 1))
                sp.dma_start(WR[:, r, :], w_stream[n]).then_inc(w_in[r], 16)

            gla_w = STREAM["glu0"] + 6
            for n in range(POOL_LOADS, gla_w):
                load_w(n, n % RAW)
            for p in range(2):
                if p:
                    sp.wait_ge(ss_out, 16)
                sp.dma_start(SS[:, :, :], st_gla[p]).then_inc(ss_in, 16)
                sp.wait_ge(sst_ready, NB * (p + 1))
                sp.dma_start(gla_s[p], SS[:, :, :]).then_inc(ss_out, 16)
            sp.dma_start(gla_p, S[:, :, :]).then_inc(s_out, 16)
            for h in range(4):
                sp.wait_ge(sst_ready, 2 * NB)
                if h >= 2:
                    sp.wait_ge(head_g, h - 1)
                sp.dma_start(TT[:, 2 + h % 2, :], g_scr[h]).then_inc(g_in[h % 2], 16)
            sp.wait_ge(xl_done, SPLIT["o"] + 4)
            sp.wait_ge(s_out, 16)
            sp.wait_ge(ss_out, 32)
            for k in range(KT):
                sp.dma_start(X[:, k, :], x_t[k]).then_inc(xr_in, 16)
            at = gla_w
            while (NT - at) % 4:
                load_w(at, at % RAW)
                at += 1
            with sp.Fori(0, (NT - at) // 4) as i:
                for j in range(4):
                    n = at + j
                    sp.wait_ge(w_ready, i * 4 + (n - (RAW - 1)))
                    sp.dma_start(WR[:, n % RAW, :], w_stream[i * 4 + n]).then_inc(w_in[n % RAW], 16)
            for c in range(NCH):
                sp.wait_ge(xn_done, 4 * NCH * KT + (c + 1) * KT)
                sp.dma_start(y_t.rearrange("k p t -> p k t")[:, :, cols_of(c)], X[:, :, cols_of(c)]).then_inc(y_sent, 16)
            sp.wait_ge(y_sent, 16 * NCH)
            sp.wait_ge(small_out, 3 * 16)

        @block.gpsimd
        def _(pool):
            def split(r, s, loaded, used, count):
                pool.wait_ge(*loaded)
                if used is not None:
                    pool.wait_ge(w_used, used)
                pool.tensor_tensor(WH[:, s, :], WR[:, r, :], ones[:, 0:1].broadcast_to([P, 1024]), ALU.mult).then_inc(w_hi, 1)
                pool.wait_ge(w_hi, count)
                pool.tensor_tensor(WL[:, s, :], WR[:, r, :], WH[:, s, :].bitcast(F32), ALU.subtract).then_inc(w_ready, 1)

            for n in range(RAW):
                pool.dma_start(WR[:, n, :], w_stream[n]).then_inc(w_first[n], 16)
            pool.wait_ge(const_ready, 1)
            at = POOL_LOADS
            while (NT - at) % 4:
                at += 1
            for n in range(at):
                loaded = ((w_first[n % RAW], 16 * (n // RAW + 1)) if n < POOL_LOADS else
                          (w_in[n % RAW], 16 * ((n - POOL_LOADS) // RAW + 1)))
                split(n % RAW, n % SLOTS, loaded, n - SLOTS + 1 if n >= SLOTS else None, n + 1)
                if n + RAW < POOL_LOADS:
                    pool.wait_ge(w_ready, n + 1)
                    pool.dma_start(WR[:, n % RAW, :], w_stream[n + RAW]).then_inc(w_first[n % RAW], 16)
            with pool.Fori(0, (NT - at) // 4) as i:
                for j in range(4):
                    n = at + j
                    split(n % RAW, n % SLOTS, (w_in[n % RAW], i * 32 + 16 * ((n - POOL_LOADS) // RAW + 1)), i * 4 + (n - SLOTS + 1), i * 4 + (n + 1))

        @block.tensor
        def _(pe):
            held = [0]

            def mm(out, lhs, rhs, start, stop):
                ins = pe.matmul(out, lhs, rhs, start=start, stop=stop)
                if held[0]:
                    held[0] -= 1
                    ins.then_inc(w_used, 1)
                return ins

            PASSES = ((WH, 0), (WH, 1), (WL, 0))

            def claim(t, prev=None):
                if prev is not None or t >= 2:
                    pe.wait_ge(acc_read[t % 2], t // 2 if prev is None else prev)

            def product(t, slots, cols, ops, nk=KT, xn=None, last_w=False, ks=None):
                ks = ks or range(nk)
                for k in ks:
                    if xn is not None and (ks[0] == 0 or k < ks[0]):
                        pe.wait_ge(xl_done, xn + k + 1)
                    if last_w and k:
                        held[0] += 1
                    s, col = slots(k), cols(k)
                    for c in range(NCH):
                        for i, (w, x) in enumerate(PASSES):
                            last = mm(acc[:, t % 2, c, 0:CH], w[:, s, col:col + P],
                                      ops[x](k)[:, cols_of(c)], k == ks[0] and i == 0, k == ks[-1] and i == 2)
                last.then_inc(acc_done[t % 2], 1)

            XOPS = (lambda k: XH[:, k, :], lambda k: XL[:, k, :])

            def project(name, acc_name, xn=None, ks=None):
                n, t = STREAM[name], ACC[acc_name]
                pe.wait_ge(w_ready, n + 1)
                claim(t)
                product(t, lambda k: n % SLOTS, lambda k: k * P, XOPS, xn=xn, ks=ks)
                held[0] += 1

            def norm(r):
                t = ACC[f"norm{r}"]
                claim(t)
                for c in range(NCH):
                    if r == 0:
                        for k in range(KT):
                            n = c * KT + k
                            pe.wait_ge(sq_done, n + 1)
                            pe.matmul(acc[:, t % 2, c, 0:CH], ones[:, :], TT[:, 2, cols_of(n % NCH)],
                                      start=(k == 0), stop=(k == KT - 1))\
                              .then_inc(acc_done[t % 2] if n == NCH * KT - 1 else sq_used, 1)
                        continue
                    pe.wait_ge(ssq_add, SSQ_N * (r - 1) + KT + c)
                    if c == 0:
                        mm(acc[:, t % 2, 0, 0:CH // 2], ones[:, :], TT[:, 2, 0:CH // 2], True, True)
                        last = mm(acc[:, t % 2, 0, CH // 2:CH], ones[:, :], TT[:, 2, CH // 2:CH], True, True)
                    else:
                        last = mm(acc[:, t % 2, c, 0:CH], ones[:, :], TT[:, 2, cols_of(c)], True, True)
                    last.then_inc(acc_done[t % 2] if c == NCH - 1 else norm_sum, 1)

            def project_pair(names, acc_names, xn):
                n, t = STREAM[names[0]], ACC[acc_names[0]]
                claim(t)
                claim(t + 1)
                for c in range(NCH):
                    for k in range(KT):
                        pe.wait_ge(xl_done, xn + c * KT + k + 1)
                        for j in range(2):
                            if c == k == 0:
                                pe.wait_ge(w_ready, n + j + 1)
                            for i, (w, x) in enumerate(PASSES):
                                last = mm(acc[:, (t + j) % 2, c, 0:CH], w[:, (n + j) % SLOTS, k * P:(k + 1) * P],
                                          XOPS[x](k)[:, cols_of(c)], k == 0 and i == 0, k == KT - 1 and i == 2)
                            if c == NCH - 1 and k == KT - 1:
                                last.then_inc(acc_done[(t + j) % 2], 1)
                                held[0] += 1

            def ms_claim(step):
                if MS[step]:
                    pe.wait_ge(ms_read, MS[step])

            def step_a(q):
                pe.wait_ge(xa_ready, q + 1)
                ms_claim(f"a{q}")
                for r in range(2):
                    for g in range(PQ):
                        last = pe.transpose(ms[:, r, g * P:(g + 1) * P],
                                            XA[:, r, g, :, :].rearrange("p l c -> p (l c)"), ident)
                last.then_inc(ms_done, 1)

            def step_b(q):
                ms_claim(f"b{q}")
                for g in range(PQ):
                    for r in range(2):
                        last = pe.matmul(ms[:, 0, g * 32:(g + 1) * 32], XA[:, r, g, :, :].rearrange("p l c -> p (l c)"),
                                         CB[:, r, PQ * q + g, :], start=(r == 0), stop=(r == 1))
                last.then_inc(ms_done, 1)

            def step_cd(q, r):
                if r == 0:
                    pe.wait_ge(u_in[q % 2], 16 * L * (q // 2 + 1))
                ms_claim(("c", "d")[r] + str(q))
                for g in range(GQ):
                    h = 64 * (g % 2)
                    last = pe.matmul(ms[h:h + 64, g // 4, (g // 2 % 2) * YW:(g // 2 % 2 + 1) * YW],
                                     WIN[:, r, g // 2, h:h + 64], U[:, q % 2, g, NB:NB + YW], start=True, stop=True)
                last.then_inc(ms_done, 1)

            def step_ef(q, half):
                if half == 0:
                    pe.wait_ge(m_in, 16 * L * (q + 1))
                    pe.wait_ge(st_ready, q + 1)
                    pe.wait_ge(wo_ready, q + 1)
                ms_claim(("e", "f")[half] + str(q))
                for g in range(4 * half, 4 * half + 4):
                    h = 64 * (g % 2)
                    out = ms[:, g % 2, (g // 2 % 2) * YW:(g // 2 % 2 + 1) * YW]
                    pe.matmul(out, M[:, g, :, :].rearrange("p l c -> p (l c)"), U[:, q % 2, g, 0:YW], start=True, stop=False)
                    for r in range(2):
                        last = pe.matmul(out, WO[h:h + 64, r, g // 2, :, :].rearrange("p l c -> p (l c)"),
                                         HV(q)[h:h + 64, r, g // 2, 0:YW], start=False, stop=(r == 1))
                last.then_inc(ms_done, 1)

            def logits(p):
                t = ACC[f"lg{p}"]
                claim(t)
                for c in range(NCH):
                    last = mm(acc[:, t % 2, c, 0:CH], wa2[0:16, p * P:(p + 1) * P], ALR[:, c * CH:(c + 1) * CH], True, True)
                last.then_inc(acc_done[t % 2], 1)

            def values():
                n = STREAM["v0"]
                for j in range(3):
                    t = ACC[f"v{j}"]
                    claim(t)
                    for b in range(3):
                        at = min((3 * j + b) * GC, T - GC)
                        for k in range(KT):
                            if j == b == k % 2 == 0:
                                pe.wait_ge(w_ready, n + k // 2 + 1)
                            if j == b == 2 and k % 2 == 0 and k:
                                held[0] += 1
                            s, col = (n + k // 2) % SLOTS, (k % 2) * 512
                            for i, (w, x) in enumerate(((WH, XH), (WL, XH), (WH, XL))):
                                last = mm(acc[:, t % 2, b, :], x[:, k, at:at + GC], w[:, s, col:col + 512],
                                          k == 0 and i == 0, k == KT - 1 and i == 2)
                    last.then_inc(acc_done[t % 2], 1)
                held[0] += 1

            pe.wait_ge(const_ready, 1)
            norm(0)
            project_pair(("u0", "u1"), ("u0", "u1"), SPLIT["norm0"])
            project("u2", "u2")
            project("u3", "u3")
            pe.wait_ge(cst_in, 16)
            step_a(0)
            step_b(0)
            project("q0", "q0")
            step_cd(0, 0)
            step_cd(0, 1)
            step_a(1)
            step_b(1)
            project("q1", "q1")
            step_cd(1, 0)
            step_cd(1, 1)
            step_ef(0, 0)
            step_ef(0, 1)
            project("g0", "g0")
            step_a(2)
            step_b(2)
            step_ef(1, 0)
            step_ef(1, 1)
            step_cd(2, 0)
            step_cd(2, 1)
            project("g1", "g1")
            step_a(3)
            step_b(3)
            step_ef(2, 0)
            step_ef(2, 1)
            project("g2", "g2")
            step_cd(3, 0)
            step_cd(3, 1)
            project("g3", "g3")
            step_ef(3, 0)
            step_ef(3, 1)
            project("k0", "k0")
            project("k1", "k1")
            project("alr", "alr")
            pe.wait_ge(alr_ready, 1)
            pe.wait_ge(wa2_in, 16)
            logits(0)
            logits(1)
            values()
            for m in range(4):
                n, t = STREAM["glu0"] + m // 2, ACC[f"glu{m}"]
                pe.wait_ge(w_ready, n + 1)
                claim(t)
                product(t, lambda k: n % SLOTS, lambda k: (m % 2) * 512 + k * P, XOPS, nk=4,
                        xn=SPLIT["z"] if m == 0 else None)
                if m % 2:
                    held[0] += 1
            read_wait(pe, "glu2")
            read_wait(pe, "glu3")
            vs = V[0:32, NGC, :]

            def gla_front(it):
                p, c, b = it // NGC, it % NGC, it % 2
                pe.wait_ge(pair_ready, p + 1)
                if it == 0:
                    pe.wait_ge(ms_read, len(MS))
                if it >= 2:
                    pe.wait_ge(kt_ready, it - 1)
                pe.transpose(ms[:, b, 0:P], TT[:, 0, c * GC:(c + 1) * GC], ident).then_inc(kt_done, 1)
                pe.wait_ge(kx_ready, it + 1)
                if it >= 2:
                    pe.wait_ge(sc_ready, it - 1)
                for i in range(NBL):
                    at = (c * NBL + i) * 2 * BL
                    last = pe.matmul(glb[:, b, i * 2 * BL:(i + 1) * 2 * BL], KX[:, b, i * GC:(i + 1) * GC],
                                     QM[:, at:at + 2 * BL], start=True, stop=True)
                last.then_inc(sc_done, 1)

            def gla_back(it):
                p, c, b = it // NGC, it % NGC, it % 2
                pe.wait_ge(sc_ready, it + 1)
                if it >= 2:
                    pe.wait_ge(o_read, it - 1)
                if c:
                    pe.wait_ge(s_ready, it)
                    pe.matmul(glb[:, 2 + b, 0:2 * GC], S[:, p, :], QI[:, c * 2 * GC:(c + 1) * 2 * GC],
                              start=True, stop=False)
                for e in range(2):
                    h = 2 * p + e
                    last = pe.matmul(glb[:, 2 + b, e * GC:(e + 1) * GC], V[:, c, h * P:(h + 1) * P],
                                     SC[:, b, e * GC:(e + 1) * GC], start=(c == 0), stop=(c == 0 or e == 1))
                last.then_inc(o_done, 1)
                pe.wait_ge(kt_ready, it + 1)
                if it:
                    pe.wait_ge(s_ready, it)
                for e in range(2):
                    h = 2 * p + e
                    last = pe.matmul(glb[64 * e:64 * e + 64, 5, 0:P], KTR[:, b, 64 * e:64 * e + 64],
                                     V[:, c, h * P:(h + 1) * P], start=True, stop=True)
                last.then_inc(kv_done, 1)

            def gla_sample(p):
                pe.wait_ge(kt_ready, NGC * (p + 1))
                pe.wait_ge(sc_ready, NGC * (p + 1))
                pe.transpose(glb[0:32, 4, 0:P], TT[:, 0, SEQ:T], ident).then_inc(sm_done, 1)
                qs = QM[:, 2 * SEQ:2 * T]
                pe.matmul(glb[0:32, 0, 0:64], TT[:, 1, SEQ:T], qs, start=True, stop=True).then_inc(sm_done, 1)
                pe.wait_ge(smc_ready, p + 1)
                pe.wait_ge(ss_in, 16 * (p + 1))
                pe.wait_ge(o_read, NGC * (p + 1))
                for e in range(2):
                    h = 2 * p + e
                    pe.matmul(glb[:, 2, e * 32:(e + 1) * 32], vs[:, h * P:(h + 1) * P], SC[0:32, 0, e * 32:(e + 1) * 32],
                              start=(e == 0), stop=False, skip_group_check=True)
                two = glb[:, 2, 0:64].rearrange("p (e n) -> p e n", e=2)
                qs2 = qs.rearrange("p (e n) -> p e n", e=2)
                for s in range(NB):
                    last = pe.matmul(two[:, :, s * NS:(s + 1) * NS], SS[:, s, :], qs2[:, :, s * NS:(s + 1) * NS],
                                     start=False, stop=(s == NB - 1), skip_group_check=True)
                last.then_inc(so_done, 1)
                pe.wait_ge(smk_ready, p + 1)
                pe.wait_ge(s_ready, NGC * (p + 1))
                kts = KX[0:32, :, :].rearrange("p a n -> p (a n)")
                for s in range(NB):
                    for e in range(2):
                        h = 2 * p + e
                        last = pe.matmul(glb[64 * e:64 * e + 64, 5 if s < 4 else 1, (s % 4) * P:(s % 4 + 1) * P],
                                         kts[:, s * P + 64 * e:s * P + 64 * e + 64], vs[:, h * P:(h + 1) * P],
                                         start=True, stop=True)
                last.then_inc(skv_done, 1)

            for p in range(2):
                if p:
                    pe.wait_ge(sst_ready, NB)
                    pe.wait_ge(so_read, 1)
                gla_front(NGC * p)
                for it in range(NGC * p, NGC * (p + 1)):
                    if it + 1 < NGC * (p + 1):
                        gla_front(it + 1)
                    gla_back(it)
                gla_sample(p)
            pe.wait_ge(sst_ready, 2 * NB)
            pe.wait_ge(so_read, 2)
            for h in range(4):
                t = ACC[f"head{h}"]
                pe.wait_ge(sq_done, NCH * KT + h + 1)
                claim(t)
                for c in range(NCH):
                    last = mm(acc[:, t % 2, c, 0:CH], ones[:, :], TT[:, h % 2, cols_of(c)], True, True)
                last.then_inc(acc_done[t % 2], 1)
            for m in range(KT):
                project(f"oute{m}", f"oute{m}", xn=SPLIT["o"] if m == 0 else None, ks=(4, 5, 6, 7, 0, 1, 2, 3))

            def mlp(layer, r):
                norm(r)
                w0, t0, xn = STREAM[f"mlp{layer}_0"], ACC[f"mlp{layer}_0"], SPLIT[f"norm{r}"]
                h0 = FT * layer

                def up(a, par_a, base_w, base_t, per):
                    for j in range(2):
                        n, t = base_w + j, base_t + j
                        pe.wait_ge(w_ready, per(4) + (n + 1))
                        pe.wait_ge(acc_read[t % 2], per(5) + t // 2)
                        product(t, lambda k: n % SLOTS, lambda k: k * P, XOPS)
                        held[0] += 1

                def down(hready, par_a, base_w, base_t, per):
                    pe.wait_ge(w_ready, per(4) + (base_w + 2))
                    pe.wait_ge(h_ready, hready)
                    ops = (lambda k: HH[:, 2 * par_a + k, :], lambda k: HL[:, 2 * par_a + k, :])
                    for m in range(KT):
                        t = base_t + m
                        pe.wait_ge(acc_read[t % 2], per(5) + t // 2)
                        product(t, lambda k: (base_w + k) % SLOTS, lambda k: m * P, ops, nk=2,
                                last_w=(m == KT - 1))
                    held[0] += 1

                project_pair((f"mlp{layer}_0", f"mlp{layer}_1"), (f"mlp{layer}_0", f"mlp{layer}_1"), xn)
                with pe.Fori(0, HG // 2 - 1) as i:
                    for j in range(2):
                        per = lambda x: i * (2 * x)
                        up(None, (j + 1) % 2, w0 + 2 + 4 * j, t0 + 2 + 10 * j, per)
                        down(i * 4 + (h0 + 2 * j + 2), j, w0 + 4 + 4 * j, t0 + 4 + 10 * j, per)
                a = HG - 2
                flat = lambda x: 0
                up(a + 1, 1, w0 + 2 + 4 * a, t0 + 2 + 10 * a, flat)
                down(h0 + 2 * a + 2, 0, w0 + 4 + 4 * a, t0 + 4 + 10 * a, flat)
                down(h0 + 2 * a + 4, 1, w0 + 6 + 4 * a, t0 + 12 + 10 * a, flat)

            mlp(0, 1)
            norm(2)

            def gates(n):
                pe.wait_ge(conv_done, n + 1)
                pe.wait_ge(wri_in[n % 2], 16 * (n // 2 + 1))
                for r, name in enumerate(("r", "i")):
                    t = ACC[f"{name}{n}"]
                    claim(t)
                    for c in range(NCH):
                        last = mm(acc[:, t % 2, c, 0:CH], WRI[:, n % 2, r, :], HB[:, n, c * CH:(c + 1) * CH], True, True)
                    last.then_inc(acc_done[t % 2], 1)

            project_pair(("xb0", "xb1"), ("xb0", "xb1"), SPLIT["norm2"])
            for n in range(KT):
                gates(n)
                if n + 2 < KT:
                    project(f"xb{n + 2}", f"xb{n + 2}")
                else:
                    project(f"gate{n + 2 - KT}", f"gate{n + 2 - KT}")
            for n in range(2, KT):
                project(f"gate{n}", f"gate{n}")
            for m in range(KT):
                project(f"outo{m}", f"outo{m}", xn=SPLIT["mix"] if m == 0 else None)
            mlp(1, 3)
            norm(4)

        def last_down(layer, k):
            return f"mlp{layer}_{2 * HG + KT * (HG - 1) + k}"

        X_FROM = [None, lambda k: f"oute{k}", lambda k: last_down(0, k), lambda k: f"outo{k}", lambda k: last_down(1, k)]
        G_NORM = ["g_mix_even", "g_mlp0", "g_mix_odd", "g_mlp1", "g_final"]

        def sq_base(r):
            return NCH * KT + 4 + SSQ_N * (r - 1)

        @block.scalar
        def _(act):
            def norm(r):
                t = ACC[f"norm{r}"]

                def first_square(c, k):
                    n = c * KT + k
                    act.wait_ge(x_in[c], 16)
                    if n >= NCH:
                        act.wait_ge(sq_used, n - NCH + 1)
                    act.activation(TT[:, 2, cols_of(n % NCH)], X0[:, k, cols_of(c)], ACT.Square).then_inc(sq_done, 1)

                def log(c):
                    if c == NCH - 1:
                        done_wait(act, f"norm{r}")
                    elif r == 0:
                        act.wait_ge(sq_used, KT * (c + 1))
                    else:
                        act.wait_ge(norm_sum, (NCH - 1) * (r - 1) + c + 1)
                    ins = act.activation(TT[:, 3, cols_of(c)], acc[:, t % 2, c, 0:CH], ACT.Ln, bias=few[:, 0:1],
                                         scale=1.0 / D)
                    ins.then_inc(ln_done if c < NCH - 1 else acc_read[t % 2], 1)

                def root(c):
                    if c < NCH - 1:
                        act.wait_ge(ln_done, (NCH - 1) * r + c + 1)
                    else:
                        read_wait(act, f"norm{r}")
                    act.activation(TT[:, 3, cols_of(c)], TT[:, 3, cols_of(c)], ACT.Exp, scale=-0.5).then_inc(rs_done, 1)

                if r == 0:
                    for k in range(KT):
                        first_square(0, k)
                else:
                    for k in range(KT - 1):
                        read_wait(act, X_FROM[r](k))
                        if k >= 2:
                            act.wait_ge(ssq_add, SSQ_N * (r - 1) + k - 1)
                        act.activation(TT[:, k % 2, :], X[:, k, :], ACT.Square).then_inc(sq_done, 1)
                    act.wait_ge(ssq_add, SSQ_N * (r - 1) + KT - 2)
                    for c in range(NCH):
                        if c < NCH - 1:
                            act.wait_ge(res_part, (NCH - 1) * (r - 1) + c + 1)
                        else:
                            read_wait(act, X_FROM[r](KT - 1))
                        act.activation(TT[:, (KT - 1) % 2, cols_of(c)], X[:, KT - 1, cols_of(c)], ACT.Square)\
                           .then_inc(sq_done, 1)
                if r == 0:
                    log(0)
                    root(0)
                else:
                    for c in range(NCH):
                        log(c)
                    for c in range(NCH):
                        root(c)
                for c in range(NCH if r < 4 else 0):
                    for k in range(KT):
                        act.wait_ge(xn_done, (NCH * r + c) * KT + k + 1)
                        act.activation(XH[:, k, cols_of(c)], TT[:, k % 2, cols_of(c)], ACT.Copy).then_inc(xh_done, 1)
                        if r == 0 and c + 1 < NCH:
                            first_square(c + 1, k)
                    if r == 0 and c + 1 < NCH:
                        log(c + 1)
                        root(c + 1)

            def read_ms(step, out, src):
                act.wait_ge(ms_done, MS[step] + 1)
                act.activation(out, src, ACT.Copy).then_inc(ms_read, 1)

            def read_a(q):
                read_ms(f"a{q}", WIN[:, :, :, :].rearrange("p r g n -> p r (g n)"), ms[:, :, :])

            def read_b(q):
                if q:
                    act.wait_ge(m_in, 16 * L * q)
                read_ms(f"b{q}", T7[:, :], ms[:, 0, 0:P])

            def read_cd(q, r):
                if r == 0 and q >= 2:
                    act.wait_ge(z_done, q - 1)
                read_ms(("c", "d")[r] + str(q), VV(q)[:, r, :, :].rearrange("p (b g) n -> p b (g n)", b=2),
                        ms[:, :, 0:2 * YW])

            def read_ef(q, half):
                if q and half == 0:
                    act.wait_ge(y_out, 16 * q)
                read_ms(("e", "f")[half] + str(q),
                        G[:, half * 4 * YW:(half + 1) * 4 * YW].rearrange("p (q e n) -> p e q n", q=2, e=2),
                        ms[:, :, 0:2 * YW].rearrange("p e (q n) -> p e q n", q=2))

            def read_u(q):
                t = ACC[f"u{q}"]
                done_wait(act, f"u{q}")
                if q:
                    act.wait_ge(u_out, 16 * q)
                for c in range(NCH):
                    n = min(CH, SEQ - c * CH) // L
                    at = NB + c * (CH // L)
                    act.activation(UR[:, :, at:at + n].rearrange("p l n -> p n l"),
                                   acc[:, t % 2, c, 0:n * L].rearrange("p (n l) -> p n l", l=L), ACT.Copy)
                tail = acc[:, t % 2, 2, CH - NB * NS:CH].rearrange("p (n s) -> p n s", s=NS)
                act.activation(UR[:, 0:NS, 0:NB].rearrange("p l n -> p n l"), tail, ACT.Copy)
                act.activation(UR[:, L - NS:L, NB + NC:CW].rearrange("p l n -> p n l"), tail, ACT.Copy)\
                   .then_inc(acc_read[t % 2], 1)

            def read_plain(name, out, func=ACT.Copy, **more):
                t = ACC[name]
                done_wait(act, name)
                act.activation(cut(out), bank(t), func, **more).then_inc(acc_read[t % 2], 1)

            def gelu(q):
                act.wait_ge(zin_done, q + 1)
                if q:
                    act.wait_ge(z_out, 16 * q)
                act.activation(TT[:, 2, 0:SEQ].rearrange("p (n l) -> p l n", l=L), YR(q)[:, :, NB:YW], ACT.Gelu_apprx_tanh)
                act.activation(TT[:, 2, SEQ:T].rearrange("p (n s) -> p s n", s=NS), YR(q)[:, 0:NS, 0:NB],
                               ACT.Gelu_apprx_tanh).then_inc(z_done, 1)

            def decay(p):
                if p:
                    act.wait_ge(lg_dve, 2)
                read_plain(f"lg{p}", TT[:, 0, :], ACT.Identity, bias=p_col("b_a2", p))
                act.wait_ge(lg_dve, 2 * p + 1)
                act.activation(TT[:, 2, :], TT[:, 2, :], ACT.Exp).then_inc(act_step, 1)
                act.wait_ge(act_step, p + 1)
                act.activation(TT[:, 2, :], TT[:, 2, :], ACT.Ln, bias=1.0).then_inc(lg_act, 1)

            def read_g(h):
                if h >= 2:
                    act.wait_ge(g_out[h % 2], 16)
                read_plain(f"g{h}", TT[:, h % 2, :], ACT.Silu)
                read_wait(act, f"g{h}")
                act.dma_start(g_scr[h], TT[:, h % 2, :]).then_inc(g_out[h % 2], 16)

            act.wait_ge(const_ready, 1)
            norm(0)
            act.wait_ge(par5_in, 16)
            act.activation(sm[:, 0, :], p5c("log_dt"), ACT.Exp).then_inc(prep_act, 1)
            act.wait_ge(prep_dve, 1)
            act.activation(sm[:, 3, :], sm[:, 2, :], ACT.Exp)
            act.activation(sm[:, 4, :], sm[:, 2, :], ACT.Exp, scale=float(L)).then_inc(prep_act, 1)
            act.wait_ge(prep_dve, 2)
            act.activation(rot[:, 1, :], sm[:, 6, :], ACT.Sin)
            act.activation(rot[:, 0, :], sm[:, 7, :], ACT.Sin, bias=few[:, 1:2]).then_inc(prep_act, 1)

            def turn_table(n):
                table = (PT0, PTR)[n]
                act.wait_ge(angle_ready, n + 1)
                act.activation(table[:, 1, :, :], table[:, 1, :, :], ACT.Sin)
                act.activation(table[:, 0, :, :], table[:, 0, :, :], ACT.Sin, bias=few[:, 1:2]).then_inc(pt_ready, 1)

            act.wait_ge(ur_ready, 1)
            for q in range(NG):
                read_u(q)
            read_a(0)
            read_b(0)
            turn_table(0)
            read_plain("q0", Q[:, 0, :])
            read_cd(0, 0)
            read_cd(0, 1)
            read_a(1)
            read_b(1)
            read_plain("q1", Q[:, 1, :])
            read_cd(1, 0)
            read_cd(1, 1)
            read_ef(0, 0)
            read_ef(0, 1)
            turn_table(1)
            read_g(0)
            read_a(2)
            read_b(2)
            gelu(0)
            read_ef(1, 0)
            read_ef(1, 1)
            read_cd(2, 0)
            read_cd(2, 1)
            read_g(1)
            read_a(3)
            read_b(3)
            gelu(1)
            read_ef(2, 0)
            read_ef(2, 1)
            read_g(2)
            read_cd(3, 0)
            read_cd(3, 1)
            read_g(3)
            gelu(2)
            read_ef(3, 0)
            read_ef(3, 1)
            act.wait_ge(st_ready, NG)
            read_plain("k0", K[:, 0, :])
            gelu(3)
            read_plain("k1", K[:, 1, :])
            t = ACC["alr"]
            done_wait(act, "alr")
            act.activation(cut(ALR), acc[0:16, t % 2, :, 0:CH], ACT.Copy).then_inc(acc_read[t % 2], 1)
            read_wait(act, "alr")
            act.nop().then_inc(alr_ready, 1)
            act.wait_ge(g_out[0], 32)
            decay(0)
            decay(1)
            act.wait_ge(z_done, NG)
            for j in range(3):
                t = ACC[f"v{j}"]
                done_wait(act, f"v{j}")
                if j < 2:
                    act.activation(V[:, 3 * j:3 * j + 3, :], acc[:, t % 2, :, :], ACT.Copy).then_inc(acc_read[t % 2], 1)
                else:
                    act.activation(V[:, 6:8, :], acc[:, t % 2, 0:2, :], ACT.Copy)
                    act.activation(V[0:32, NGC, :], acc[96:P, t % 2, 2, :], ACT.Copy).then_inc(acc_read[t % 2], 1)
            for k in range(4):
                act.wait_ge(z_in[k % 2], 16 * (k // 2 + 1))
                act.activation(XH[:, k, :], TT[:, k % 2, :], ACT.Copy).then_inc(xh_done, 1)
            for m in range(4):
                act.wait_ge(xl_done, SPLIT["z"] + 4 if m < 2 else SPLIT["zg"] + m - 1)
                read_plain(f"glu{m}", TT[:, 2 + m % 2, :], ACT.Sigmoid, bias=p_col("b_glu", m))
                act.wait_ge(gg_done, m + 1)
                act.activation(XH[:, 4 + m, :], TT[:, 2 + m % 2, :], ACT.Copy).then_inc(xh_done, 1)

            for p in range(2):
                g0 = 4 * p
                act.wait_ge(gd, g0 + 1)
                act.activation(TT[:, 0, :], TT[:, 3, :], ACT.Exp).then_inc(ga, 1)
                act.wait_ge(gd, g0 + 2)
                act.activation(TT[:, 0, :], TT[:, 3, :], ACT.Exp, scale=-1.0).then_inc(ga, 1)
                act.wait_ge(gd, g0 + 3)
                act.activation(TT[:, 0, :], TT[:, 0, :], ACT.Exp).then_inc(ga, 1)
                act.wait_ge(gd, g0 + 4)
                act.activation(gs[:, 2:5, :], gs[:, 2:5, :], ACT.Exp)
                act.activation(GB[:, :, :, :], GB[:, :, :, :], ACT.Exp).then_inc(ga, 1)

                def read_kt(it):
                    act.wait_ge(kt_done, it + 1)
                    if it >= 2:
                        act.wait_ge(kv_done, it - 1)
                    act.activation(KTR[:, it % 2, :], ms[:, it % 2, 0:P], ACT.Copy)\
                       .then_inc(kt_ready, 1)

                read_kt(NGC * p)
                for it in range(NGC * p, NGC * (p + 1)):
                    c, b = it % NGC, it % 2
                    if c + 1 < NGC:
                        read_kt(it + 1)
                    act.wait_ge(o_done, it + 1)
                    act.activation(Q[:, p, c * GC:(c + 1) * GC], glb[:, 2 + b, 0:GC], ACT.Copy)
                    act.activation(K[:, p, c * GC:(c + 1) * GC], glb[:, 2 + b, GC:2 * GC], ACT.Copy).then_inc(o_read, 1)
                act.wait_ge(so_done, p + 1)
                act.activation(Q[:, p, SEQ:T], glb[:, 2, 0:32], ACT.Copy)
                act.activation(K[:, p, SEQ:T], glb[:, 2, 32:64], ACT.Copy).then_inc(so_read, 1)
            act.wait_ge(so_read, 2)
            act.wait_ge(sst_ready, 2 * NB)
            def head_square(h):
                if h >= 2:
                    act.wait_ge(gg_done, 4 + h - 1)
                act.activation(TT[:, h % 2, :], (Q, K)[h % 2][:, h // 2, :], ACT.Square).then_inc(sq_done, 1)

            def head_hi(h):
                act.wait_ge(gg_done, 4 + h + 1)
                act.activation(XH[:, h, :], (Q, K)[h % 2][:, h // 2, :], ACT.Copy).then_inc(xh_done, 1)

            for h in (0, 1):
                head_square(h)
            for first in (0, 2):
                for h in (first, first + 1):
                    t = ACC[f"head{h}"]
                    done_wait(act, f"head{h}")
                    act.activation(cut(TT[:, h % 2, :]), bank(t), ACT.Ln, bias=few[:, 0:1], scale=1.0 / P)\
                       .then_inc(acc_read[t % 2], 1)
                for h in (first, first + 1):
                    read_wait(act, f"head{h}")
                    act.activation(TT[:, h % 2, :], TT[:, h % 2, :], ACT.Exp, scale=-0.5).then_inc(head_rs, 1)
                if first == 0:
                    for h in (2, 3):
                        head_square(h)
                        head_hi(h - 2)
            head_hi(2)
            head_hi(3)

            def mlp_hidden(base_t, per5, hcount, u, first):
                t = base_t
                act.wait_ge(acc_done[t % 2], per5 + (t // 2 + 1))
                if not first:
                    act.wait_ge(h_ready, hcount - 1)
                act.activation(cut(TT[:, u % 2, :]), bank(t), ACT.Relu).then_inc(acc_read[t % 2], 1)
                act.wait_ge(acc_read[t % 2], per5 + (t // 2 + 1))
                act.activation(TT[:, 2 + u % 2, :], TT[:, u % 2, :], ACT.Square).then_inc(h_sq, 1)

            def mlp(layer):
                t0, h0 = ACC[f"mlp{layer}_0"], FT * layer
                for j in range(2):
                    mlp_hidden(t0 + j, 0, None, j, True)
                with act.Fori(0, HG // 2 - 1) as i:
                    for a in range(2):
                        for j in range(2):
                            mlp_hidden(t0 + 2 + 10 * a + j, i * 10, i * 4 + (h0 + 2 * (a + 1) + j), j, False)
                a = HG - 2
                for j in range(2):
                    mlp_hidden(t0 + 2 + 10 * a + j, 0, h0 + 2 * (a + 1) + j, j, False)
                act.wait_ge(h_ready, h0 + FT)

            norm(1)
            mlp(0)
            norm(2)
            act.wait_ge(tg_done, 1)
            act.activation(spt[:, :], spt[:, :], ACT.Exp).then_inc(act_step, 1)
            act.wait_ge(act_step, 3)
            act.activation(spt[:, :], spt[:, :], ACT.Ln, bias=1.0).then_inc(sp_act, 1)

            def load_ri(n):
                act.dma_start(WRI[:, n % 2, :, :], w_ri[n]).then_inc(wri_in[n % 2], 16)

            def read_xb(n):
                t = ACC[f"xb{n}"]
                done_wait(act, f"xb{n}")
                if n >= 2:
                    act.wait_ge(conv_done, n - 1)
                act.activation(XP[:, n % 2, 3:3 + 2 * CH].rearrange("p (c n) -> p c n", n=CH),
                               acc[:, t % 2, 0:2, 0:CH], ACT.Copy)
                act.activation(XP[:, n % 2, 3 + 2 * CH:3 + SEQ], acc[:, t % 2, 2, 0:SEQ - 2 * CH], ACT.Copy)
                smp = XP[:, n % 2, 3 + SEQ:].rearrange("p (b s) -> p b s", b=NB)
                act.activation(smp[:, :, 0:3], st_conv[:, n, :, :], ACT.Copy)
                act.activation(smp[:, :, 3:7], acc[:, t % 2, 2, SEQ - 2 * CH:CH].rearrange("p (b s) -> p b s", b=NB),
                               ACT.Copy).then_inc(acc_read[t % 2], 1)

            def gates(n):
                if n:
                    act.wait_ge(gt_done, n)
                if n == KT - 1:
                    act.wait_ge(hb_ready, 1)
                read_plain(f"r{n}", TT[:, 0, :], ACT.Sigmoid, bias=p_col("b_r", n))
                read_plain(f"i{n}", TT[:, 1, :], ACT.Sigmoid, bias=p_col("b_i", n))
                read_wait(act, f"r{n}")
                act.activation(TT[:, 0, :], TT[:, 0, :], ACT.Tanh, scale=sp4[:, n:n + 1]).then_inc(sig_done, 1)
                act.wait_ge(sig_done, 3 * n + 1)
                act.activation(TT[:, 3, :], TT[:, 0, :], ACT.Sqrt)
                act.activation(TT[:, 2, :], TT[:, 0, :], ACT.Ln, bias=1.0).then_inc(sig_done, 1)
                act.wait_ge(sig_done, 3 * n + 2)
                act.activation(TT[:, 2, :], TT[:, 2, :], ACT.Exp, scale=-1.0).then_inc(sig_done, 1)

            act.wait_ge(xl_done, SPLIT["norm2"] + NCH * KT)
            act.dma_start(st_lru[:, :, :], odd_lru).then_inc(odd_in, 16)
            act.dma_start(st_conv[:, :, :, :], odd_conv).then_inc(odd_in, 16)
            load_ri(0)
            load_ri(1)
            act.wait_ge(odd_in, 32)
            act.wait_ge(xp_ready, 1)
            read_xb(0)
            read_xb(1)
            act.wait_ge(tg_done, 2)
            for n in range(KT):
                gates(n)
                if n + 2 < KT:
                    load_ri(n + 2)
                    read_xb(n + 2)
                if n >= KT - 2:
                    m = n + 2 - KT
                    act.wait_ge(gt_done, n + 1)
                    read_plain(f"gate{m}", TT[:, m % 2, :], ACT.Gelu_apprx_tanh)
            for m in range(2, KT):
                act.wait_ge(hb_ready, m - 1)
                read_plain(f"gate{m}", TT[:, m % 2, :], ACT.Gelu_apprx_tanh)
            done_wait(act, f"gate{KT - 1}")
            act.dma_start(lru_out, LN[:, :, :]).then_inc(small_out, 16)
            act.dma_start(conv_out, CN[:, :, :]).then_inc(small_out, 16)
            act.dma_start(s5_out, SO[:, :, :, :]).then_inc(small_out, 16)
            for k in range(KT):
                act.wait_ge(hb_ready, k + 1)
                act.activation(XH[:, k, :], HB[:, k, :], ACT.Copy).then_inc(xh_done, 1)
            norm(3)
            mlp(1)
            norm(4)

        @block.vector
        def _(dve):
            step = Chain(dve, dve_step)
            link = step.link
            SP1 = slice(0, SEQ)

            def tt(out, a, b, op):
                return dve.tensor_tensor(out, a, b, op)

            def stt(out, a, scalar, b, op0, op1):
                return dve.scalar_tensor_tensor(out=out, in0=a, scalar=scalar, in1=b, op0=op0, op1=op1)

            def lo_part(dst, src, hi, want):
                dve.wait_ge(xh_done, want)
                tt(dst, src, hi.bitcast(F32), ALU.subtract).then_inc(xl_done, 1)

            def add_square(r, k):
                dve.wait_ge(sq_done, sq_base(r) + k + 1)
                if k == 0:
                    dve.tensor_copy(TT[:, 2, :], TT[:, 0, :]).then_inc(ssq_add, 1)
                else:
                    dve.wait_ge(ssq_add, SSQ_N * (r - 1) + k)
                    tt(TT[:, 2, :], TT[:, 2, :], TT[:, k % 2, :], ALU.add).then_inc(ssq_add, 1)

            def norm(r):
                xs, at = (X0 if r == 0 else X), SPLIT.get(f"norm{r}")
                if r == 0:
                    dve.wait_ge(par_in, 16)
                else:
                    dve.wait_ge(ssq_add, SSQ_N * (r - 1) + KT - 1)
                    for c in range(NCH):
                        dve.wait_ge(sq_done, sq_base(r) + KT + c)
                        tt(TT[:, 2, cols_of(c)], TT[:, 2, cols_of(c)], TT[:, (KT - 1) % 2, cols_of(c)], ALU.add)\
                            .then_inc(ssq_add, 1)

                def lo(n):
                    c, k = n // KT, n % KT
                    dve.wait_ge(xn_done, NCH * KT * r + n + 1)
                    lo_part(XL[:, k, cols_of(c)], TT[:, k % 2, cols_of(c)], XH[:, k, cols_of(c)], at + n + 1)

                for n in range(NCH * KT):
                    c, k = n // KT, n % KT
                    if k == 0:
                        dve.wait_ge(rs_done, NCH * r + c + 1)
                    g = p_col(G_NORM[r], k)
                    if r == 4:
                        stt(X[:, k, cols_of(c)], X[:, k, cols_of(c)], g, TT[:, 3, cols_of(c)], ALU.mult, ALU.mult)\
                            .then_inc(xn_done, 1)
                        continue
                    if n >= 2:
                        dve.wait_ge(xl_done, at + n - 1)
                    stt(TT[:, k % 2, cols_of(c)], xs[:, k, cols_of(c)], g, TT[:, 3, cols_of(c)], ALU.mult, ALU.mult)\
                        .then_inc(xn_done, 1)
                    if n:
                        lo(n - 1)
                if r < 4:
                    lo(NCH * KT - 1)

            def cmul(out, a, b, t, neg=False):
                link(tt(t[0], a[0], b[0], ALU.mult))
                link(tt(t[1], a[1], b[1], ALU.mult))
                tt(out[0], t[0], t[1], ALU.subtract).then_inc(dve_step, 1)
                step.n += 1
                step.wait()
                link(tt(t[0], a[0], b[1], ALU.mult))
                link(tt(t[1], a[1], b[0], ALU.mult))
                if neg:
                    return stt(out[1], t[0], -1.0, t[1], ALU.mult, ALU.subtract)
                return tt(out[1], t[0], t[1], ALU.add)

            dve.memset(ones[:, :], 1.0)
            dve.memset(few[:, 0:1], EPS)
            dve.memset(few[:, 1:2], 1.5707963267948966).then_inc(const_ready, 1)
            dve.memset(UR[:, :, :], 0.0).then_inc(ur_ready, 1)
            dve.memset(M[:, :, :, :], 0.0)
            link(dve.memset(CB[:, :, :, :], 0.0))
            norm(0)

            link(dve.memset(pw[:, :, 0, :], 0.0))
            link(dve.memset(pw[:, 0, 0, :], 1.0))
            dve.wait_ge(par5_in, 16)
            cb = [p5c(n).rearrange("p (g c) -> p g c", c=16) for n in ("c_re", "c_im")]
            bb = [p5c(n).rearrange("p (g c) -> p g c", c=16) for n in ("b_re", "b_im")]
            for e in range(2):
                h = slice(64 * e, 64 * e + 64)
                dve.tensor_copy(CB[h, 0, :, 16 * e:16 * e + 16], cb[0][h])
                link(dve.tensor_scalar(CB[h, 1, :, 16 * e:16 * e + 16], cb[1][h], -1.0, None, ALU.mult))
            dve.wait_ge(prep_act, 1)
            are, aim = p5c("a_re"), p5c("a_im")
            link(tt(sm[:, 1, :], sm[:, 0, :], aim, ALU.mult))
            tt(sm[:, 2, :], sm[:, 0, :], are, ALU.mult).then_inc(prep_dve, 1)

            def reduce(x, t, near=None):
                link(dve.tensor_scalar(t, x if near is None else near, 0.15915494309189535, MAGIC, ALU.mult, ALU.add))
                link(dve.tensor_scalar(t, t, MAGIC, None, ALU.subtract))
                for part in (TWO_PI_1, TWO_PI_2, TWO_PI_3):
                    link(stt(x, t, -part, x, ALU.mult, ALU.add))

            def clamp(x):
                return dve.tensor_scalar(x, x, 3.1415925, -3.1415925, ALU.min, ALU.max)

            link(dve.tensor_scalar(sm[:, 12, :], sm[:, 1, :], float(L), None, ALU.mult))
            link(dve.tensor_copy(sm[:, 6, :], sm[:, 1, :]))
            reduce(sm[:, 6, :], sm[:, 5, :])
            link(clamp(sm[:, 6, :]))
            stt(sm[:, 7, :], sm[:, 6, :], -1.0, sm[:, 6, :], ALU.mult, ALU.min).then_inc(prep_dve, 1)
            reduce(sm[:, 12, :], sm[:, 5, :])
            link(dve.tensor_scalar(sm[:, 11, :], sm[:, 12, :], CUT12, None, ALU.add))
            link(dve.tensor_scalar(sm[:, 11, :], sm[:, 11, :], CUT12, None, ALU.subtract))
            link(tt(sm[:, 13, :], sm[:, 12, :], sm[:, 11, :], ALU.subtract))
            dve.wait_ge(prep_act, 3)
            sc2 = (sm[:, 8, :], sm[:, 9, :])
            a1 = (pw[:, 0, 1, :], pw[:, 1, 1, :])
            link(tt(a1[0], sm[:, 3, :], rot[:, 0, :], ALU.mult))
            link(tt(a1[1], sm[:, 3, :], rot[:, 1, :], ALU.mult))
            for n in (1, 2, 4):
                t = [TT[:, 3, 64 * r:64 * r + 16 * n].rearrange("p (k g) -> p k g", g=16) for r in range(2)]
                link(cmul([pw[:, r, n + 1:2 * n + 1, :] for r in range(2)], [pw[:, r, 1:n + 1, :] for r in range(2)],
                          [pw[:, r, n, :].unsqueeze(1).broadcast_to([P, n, 16]) for r in range(2)], t))
            link(dve.tensor_scalar(sm[:, 5, :], a1[0], 1.0, None, ALU.subtract))
            link(tt(sm[:, 8, :], are, are, ALU.mult))
            link(tt(sm[:, 9, :], aim, aim, ALU.mult))
            link(tt(sm[:, 8, :], sm[:, 8, :], sm[:, 9, :], ALU.add))
            link(dve.reciprocal(sm[:, 10, :], sm[:, 8, :]))
            link(tt(sm[:, 8, :], sm[:, 5, :], are, ALU.mult))
            link(tt(sm[:, 9, :], a1[1], aim, ALU.mult))
            link(tt(sm[:, 8, :], sm[:, 8, :], sm[:, 9, :], ALU.add))
            link(tt(sm[:, 6, :], sm[:, 8, :], sm[:, 10, :], ALU.mult))
            link(tt(sm[:, 8, :], a1[1], are, ALU.mult))
            link(tt(sm[:, 9, :], sm[:, 5, :], aim, ALU.mult))
            link(tt(sm[:, 8, :], sm[:, 8, :], sm[:, 9, :], ALU.subtract))
            link(tt(sm[:, 7, :], sm[:, 8, :], sm[:, 10, :], ALU.mult))

            def over(ap, shape):
                return ap.broadcast_to(shape)

            g16 = [P, 16, 16]
            coef = [over(sm[:, 6 + r, :].unsqueeze(2), g16) for r in range(2)]
            tq = [TT[:, 3, 256 * n:256 * (n + 1)].rearrange("p (g c) -> p g c", c=16) for n in range(4)]
            link(tt(tq[0], coef[0], bb[0], ALU.mult))
            link(tt(tq[1], coef[1], bb[1], ALU.mult))
            link(tt(tq[2], coef[0], bb[1], ALU.mult))
            link(tt(tq[3], coef[1], bb[0], ALU.mult))
            link(tt(bb[0], tq[0], tq[1], ALU.subtract))
            link(tt(bb[1], tq[2], tq[3], ALU.add))

            shp = [P, PQ, L, 16]
            tx = [TT[:, 3, 512 * n:512 * (n + 1)].rearrange("p (g l c) -> p g l c", g=PQ, l=L) for n in range(2)]
            tn = [TT[:, 3, 512 * n:512 * (n + 1)].rearrange("p (g n) -> p g n", g=PQ) for n in range(2)]

            def power_rows(first, last, q):
                d = 1 if last > first else -1
                stop = last + d
                return [over(pw[:, r, first:(stop if stop >= 0 else None):d, PQ * q:PQ * (q + 1)]
                             .rearrange("p l g -> p g l").unsqueeze(3), shp) for r in range(2)]

            def build_xa(q):
                if q:
                    dve.wait_ge(ms_done, MS[f"b{q - 1}"] + 1)
                b = [over(bb[r][:, PQ * q:PQ * (q + 1), :].unsqueeze(2), shp) for r in range(2)]
                cmul((XA[:, 0], XA[:, 1]), power_rows(L - 1, 0, q), b, tx).then_inc(xa_ready, 1)
                dve.wait_ge(xa_ready, q + 1)

            def build_wo(q):
                if q:
                    dve.wait_ge(ms_done, MS[f"f{q - 1}"] + 1)
                c = [over(cb[r][:, PQ * q:PQ * (q + 1), :].unsqueeze(2), shp) for r in range(2)]
                cmul((WO[:, 0], WO[:, 1]), power_rows(1, L, q), c, tx, neg=True).then_inc(wo_ready, 1)
                dve.wait_ge(wo_ready, q + 1)

            def build_angles(table, g0, g1):
                shape = [P, g1 - g0, NC]
                x = table[:, 1, :, :]
                t, rest = [TT[:, 2 * r:2 * r + 2, :].rearrange("p a n -> p (a n)")[:, 0:(g1 - g0) * NC]
                           .rearrange("p (g n) -> p g n", n=NC) for r in range(2)]
                count = over(c_("count").unsqueeze(1), shape)
                link(tt(x, count, over(sm[:, 11, g0:g1].unsqueeze(2), shape), ALU.mult))
                link(tt(rest, count, over(sm[:, 13, g0:g1].unsqueeze(2), shape), ALU.mult))
                link(tt(t, x, rest, ALU.add))
                reduce(x, t, t)
                link(tt(x, x, rest, ALU.add))
                link(clamp(x))
                stt(table[:, 0, :, :], x, -1.0, x, ALU.mult, ALU.min).then_inc(angle_ready, 1)

            def core(q):
                dve.wait_ge(ms_read, MS[f"d{q}"] + 1)
                dve.wait_ge(pt_ready, 2 if q else 1)
                qs = slice(PQ * q, PQ * (q + 1))
                pr, pi = [(PTR[:, r, PQ * (q - 1):PQ * q, :] if q else PT0[:, r, :, :]) for r in range(2)]
                vv, gv, h = VV(q), GV(q), HV(q)
                vr, vi = vv[:, 0, :, 0:NC], vv[:, 1, :, 0:NC]
                gr, gi = gv[:, 0], gv[:, 1]
                t = tn
                link(tt(t[0], pr, vr, ALU.mult))
                link(tt(t[1], pi, vi, ALU.mult))
                link(tt(gr, t[0], t[1], ALU.add))
                link(tt(t[0], pr, vi, ALU.mult))
                link(tt(t[1], pi, vr, ALU.mult))
                link(tt(gi, t[0], t[1], ALU.subtract))
                h0 = [p5c(n).rearrange("p (g b) -> p g b", b=NB)[:, qs, :] for n in ("h0_re", "h0_im")]
                a4 = [over(pw[:, r, NS, qs].unsqueeze(2), [P, PQ, NB]) for r in range(2)]
                ts = [x[:, :, 0:NB] for x in t]
                so = [SO[:, r, qs, 1:1 + NB] for r in range(2)]
                link(cmul(so, a4, h0, ts))
                for r in range(2):
                    link(tt(so[r], so[r], vv[:, r, :, NC:YW], ALU.add))
                link(dve.tensor_copy(t[0], over(sm[:, 4, qs].unsqueeze(2), [P, PQ, NC])))
                link(dve.memset(t[0][:, :, 0:1], 0.0))
                flat = t[0].rearrange("p g n -> p (g n)")
                for r in range(2):
                    g = gv[:, r].rearrange("p g n -> p (g n)")
                    link(dve.tensor_tensor_scan(g, flat, g, 0.0, ALU.mult, ALU.add))
                hv = [h[:, r, :, NB + 1:NB + 1 + NC] for r in range(2)]
                link(cmul(hv, (gr, gi), (pr, pi), t))
                for r in range(2):
                    dve.memset(h[:, r, :, NB:NB + 1], 0.0)
                    link(dve.tensor_copy(h[:, r, :, 0:NB], h0[r]))
                    last = dve.tensor_copy(SO[:, r, qs, 0:1], h[:, r, :, NB + NC:NB + NC + 1])
                    last.then_inc(st_ready, 1) if r else link(last)

            def z_in_sum(q):
                dve.wait_ge(y_in, 16 * GQ * (q + 1))
                dve.wait_ge(ud_in, 16 * (q + 1))
                u = U[:, q % 2, :, :].rearrange("p g w -> p (g w)").rearrange("p (l w) -> p l w", l=L)
                stt(YR(q), u[:, :, 0:YW], p_col("s5_d", q), YR(q), ALU.mult, ALU.add).then_inc(zin_done, 1)

            def decay(p):
                read_wait(dve, f"lg{p}")
                if p:
                    dve.wait_ge(lg_dve, 2)
                link(dve.tensor_scalar(TT[:, 1, :], TT[:, 0, :], 0.0, None, ALU.min))
                stt(TT[:, 2, :], TT[:, 1, :], 2.0, TT[:, 0, :], ALU.mult, ALU.subtract).then_inc(lg_dve, 1)
                dve.wait_ge(lg_act, p + 1)
                link(dve.tensor_scalar(TT[:, 2, :], TT[:, 2, :], 1.0 / 16, None, ALU.mult))
                stt(LA[:, p, :], TT[:, 1, :], 1.0 / 16, TT[:, 2, :], ALU.mult, ALU.subtract).then_inc(lg_dve, 1)

            build_xa(0)
            dve.wait_ge(cst_in, 16)
            build_angles(PT0, 0, PQ)
            build_wo(0)
            build_xa(1)
            core(0)
            build_angles(PTR, PQ, 16)
            for q in range(NG):
                if q + 2 < NG:
                    build_xa(q + 2)
                if q + 1 < NG:
                    core(q + 1)
                z_in_sum(q)
                if q + 1 < NG:
                    build_wo(q + 1)
            dve.wait_ge(g_out[1], 32)
            dve.wait_ge(z_out, 16 * NG)
            decay(0)
            decay(1)

            for k in range(4):
                dve.wait_ge(z_in[k % 2], 16 * (k // 2 + 1))
                lo_part(XL[:, k, :], TT[:, k % 2, :], XH[:, k, :], SPLIT["z"] + k + 1)
            for m in range(4):
                dve.wait_ge(z_in[m % 2], 32 + 16 * (m // 2 + 1))
                read_wait(dve, f"glu{m}")
                row = TT[:, 2 + m % 2, :]
                tt(row, row, TT[:, m % 2, :], ALU.mult).then_inc(gg_done, 1)
                dve.wait_ge(gg_done, m + 1)
                lo_part(XL[:, 4 + m, :], row, XH[:, 4 + m, :], SPLIT["zg"] + m + 1)

            C16, E0, KE, KN = TT[:, 3, :], TT[:, 0, :], TT[:, 2, :], TT[:, 1, :]
            qp = QM[:, 0:2 * SEQ].rearrange("p (b e n) -> p e b n", e=2, n=BL)
            qc = QM[:, 0:2 * SEQ].rearrange("p (c i e n) -> p e c i n", i=NBL, e=2, n=BL)
            qi = QI[:, :].rearrange("p (c e i n) -> p e c i n", e=2, i=NBL, n=BL)
            qsm = QM[:, 2 * SEQ:2 * T].rearrange("p (e n) -> p e n", e=2)
            NBK = SEQ // BL
            link(dve.memset(QM[:, :], 0.0))
            dve.wait_ge(xl_done, SPLIT["o"])
            dve.wait_ge(z_out, 16 * NG)
            for p in range(2):
                g0 = 4 * p
                if p:
                    dve.wait_ge(sst_ready, NB)
                    dve.wait_ge(so_done, 1)
                mask = KX[:, 0, 0:T]
                link(dve.memset(mask, 1.0))
                link(dve.memset(mask[:, 0:SEQ].rearrange("p (b n) -> p b n", n=BL)[:, :, 0:1], 0.0))
                link(dve.memset(mask[:, SEQ:T].rearrange("p (b n) -> p b n", n=NS)[:, :, 0:1], 0.0))
                dve.tensor_tensor_scan(C16, mask, LA[:, p, :], 0.0, ALU.mult, ALU.add).then_inc(gd, 1)
                dve.wait_ge(gd, g0 + 1)
                link(dve.memset(gs[:, 5, :], 1.0))
                link(dve.memset(gs[:, 5, :].rearrange("p (c i) -> p c i", i=NBL)[:, :, 0:1], 0.0))
                link(dve.tensor_copy(gs[:, 0, :], C16[:, BL - 1:SEQ:BL]))
                link(dve.tensor_tensor_scan(gs[:, 1, :], gs[:, 5, :], gs[:, 0, :], 0.0, ALU.mult, ALU.add))
                link(tt(gs[:, 2, :], gs[:, 1, :], gs[:, 0, :], ALU.subtract))
                e3 = [gs[:, n, :].rearrange("p (c i) -> p c i", i=NBL) for n in range(4)]
                last = over(e3[1][:, :, NBL - 1:NBL], [P, NGC, NBL])
                link(tt(e3[3], last, e3[1], ALU.subtract))
                link(dve.memset(gs[:, 4, :], 0.0))
                link(dve.tensor_copy(gs[:, 4, 0:NGC], gs[:, 1, NBL - 1:NBK:NBL]))
                link(dve.tensor_copy(gs[:, 4, 8:8 + NB], C16[:, SEQ + NS - 1:T:NS]))
                g4 = [P, NGC, NBL, NBL]
                link(tt(GB[:, :, :, :], over(e3[2].unsqueeze(3), g4), over(e3[1].unsqueeze(2), g4), ALU.subtract))
                link(dve.tensor_scalar(GB[:, :, :, :], GB[:, :, :, :], 0.0, None, ALU.min))
                link(dve.tensor_copy(gs[:, 5, 0:NB], C16[:, SEQ + NS - 1:T:NS]))
                dve.wait_ge(ga, g0 + 1)
                for e in range(2):
                    h = slice(64 * e, 64 * e + 64)
                    stt(qp[h, e], Q[h, p, 0:SEQ].rearrange("p (b n) -> p b n", n=BL), 0.125,
                        E0[h, 0:SEQ].rearrange("p (b n) -> p b n", n=BL), ALU.mult, ALU.mult)
                    last = stt(qsm[h, e], Q[h, p, SEQ:T], 0.125, E0[h, SEQ:T], ALU.mult, ALU.mult)
                    last.then_inc(gd, 1) if e else link(last)
                dve.wait_ge(gd, g0 + 2)
                dve.wait_ge(ga, g0 + 2)
                link(tt(KN, K[:, p, :], E0, ALU.mult))
                link(tt(E0[:, 0:SEQ].rearrange("p (b n) -> p b n", n=BL), over(gs[:, 0, :].unsqueeze(2), [P, NBK, BL]),
                        C16[:, 0:SEQ].rearrange("p (b n) -> p b n", n=BL), ALU.subtract))
                tt(E0[:, SEQ:T].rearrange("p (b n) -> p b n", n=NS), over(gs[:, 5, 0:NB].unsqueeze(2), [P, NB, NS]),
                   C16[:, SEQ:T].rearrange("p (b n) -> p b n", n=NS), ALU.subtract).then_inc(gd, 1)
                dve.wait_ge(ga, g0 + 3)
                tt(KE, K[:, p, :], E0, ALU.mult).then_inc(gd, 1)
                dve.wait_ge(gd, g0 + 4)
                dve.wait_ge(ga, g0 + 4)
                link(tt(GB[:, :, :, :], GB[:, :, :, :],
                        over(c_("tri8").rearrange("p (i j) -> p i j", j=NBL).unsqueeze(1), g4), ALU.mult))
                for e in range(2):
                    link(tt(qi[:, e], qc[:, e], over(e3[2].unsqueeze(3), [P, NGC, NBL, BL]), ALU.mult))
                link(dve.tensor_copy(E0[:, SEQ:T], KE[:, SEQ:T]))
                tt(E0[:, 0:SEQ].rearrange("p (b n) -> p b n", n=BL), KE[:, 0:SEQ].rearrange("p (b n) -> p b n", n=BL),
                   over(gs[:, 3, :].unsqueeze(2), [P, NBK, BL]), ALU.mult).then_inc(pair_ready, 1)

                def key_blocks(it):
                    c, b = it % NGC, it % 2
                    if it >= 2:
                        dve.wait_ge(sc_done, it - 1)
                    dst = KX[:, b, 0:NBL * GC].rearrange("p (i j n) -> p i j n", i=NBL, j=NBL)
                    src = KE[:, c * GC:(c + 1) * GC].rearrange("p (j n) -> p j n", n=BL)
                    shape = [P, NBL, NBL, BL]
                    link(tt(dst, over(src.unsqueeze(1), shape), over(GB[:, c, :, :].unsqueeze(3), shape), ALU.mult))
                    own = KX[:, b, :].rearrange("p (i x) -> p i x", x=GC + BL)[:, :, 0:BL]
                    dve.tensor_copy(own, KN[:, c * GC:(c + 1) * GC].rearrange("p (j n) -> p j n", n=BL))\
                       .then_inc(kx_ready, 1)

                key_blocks(NGC * p)
                key_blocks(NGC * p + 1)
                for it in range(NGC * p, NGC * (p + 1)):
                    c, b = it % NGC, it % 2
                    dve.wait_ge(sc_done, it + 1)
                    if it >= 2:
                        dve.wait_ge(o_done, it - 1)
                    tt(SC[:, b, :].rearrange("p (e i n) -> p i e n", e=2, n=BL),
                       glb[:, b, 0:2 * GC].rearrange("p (i e n) -> p i e n", e=2, n=BL),
                       over(tri.unsqueeze(2), [P, NBL, 2, BL]), ALU.mult).then_inc(sc_ready, 1)
                    if c + 2 < NGC:
                        key_blocks(it + 2)
                    dve.wait_ge(kv_done, it + 1)
                    if c == 0:
                        dve.tensor_copy(S[:, p, :], glb[:, 5, 0:P]).then_inc(s_ready, 1)
                    else:
                        dve.wait_ge(s_ready, it)
                        stt(S[:, p, :], S[:, p, :], gs[:, 4, c:c + 1], glb[:, 5, 0:P], ALU.mult, ALU.add)\
                            .then_inc(s_ready, 1)
                dve.wait_ge(sm_done, 2 * p + 2)
                dve.wait_ge(o_done, NGC * (p + 1))
                tt(SC[0:32, 0, 0:64].rearrange("p (e n) -> p e n", e=2), glb[0:32, 0, 0:64].rearrange("p (e n) -> p e n", e=2),
                   over(c_("smask")[0:32, :].unsqueeze(1), [32, 2, 32]), ALU.mult).then_inc(smc_ready, 1)
                kts = KX[0:32, :, :].rearrange("p a n -> p (a n)")[:, 0:NB * P].rearrange("p (s n) -> p s n", s=NB)
                tt(kts, over(glb[0:32, 4, 0:P].unsqueeze(1), [32, NB, P]),
                   over(c_("bmask")[0:32, :].unsqueeze(2), [32, NB, P]), ALU.mult).then_inc(smk_ready, 1)
                dve.wait_ge(skv_done, p + 1)
                for s in range(NB):
                    stt(SS[:, s, :], SS[:, s, :], gs[:, 4, 8 + s:9 + s], glb[:, 5 if s < 4 else 1, (s % 4) * P:(s % 4 + 1) * P],
                        ALU.mult, ALU.add).then_inc(sst_ready, 1)

            def head_gate(h):
                o = (Q, K)[h % 2][:, h // 2, :]
                dve.wait_ge(g_in[h % 2], 16 * (h // 2 + 1))
                dve.wait_ge(sq_done, NCH * KT + h + 1)
                stt(o, o, p_col("g_head", h), TT[:, 2 + h % 2, :], ALU.mult, ALU.mult).then_inc(head_g, 1)

            def head_norm(h):
                o = (Q, K)[h % 2][:, h // 2, :]
                dve.wait_ge(head_rs, h + 1)
                dve.wait_ge(head_g, h + 1)
                tt(o, o, TT[:, h % 2, :], ALU.mult).then_inc(gg_done, 1)

            def head_lo(h):
                dve.wait_ge(gg_done, 4 + h + 1)
                lo_part(XL[:, h, :], (Q, K)[h % 2][:, h // 2, :], XH[:, h, :], SPLIT["o"] + h + 1)

            head_gate(0)
            head_gate(1)
            head_norm(0)
            head_norm(1)
            head_gate(2)
            head_lo(0)
            head_gate(3)
            head_lo(1)
            head_norm(2)
            head_norm(3)
            head_lo(2)
            head_lo(3)
            dve.wait_ge(xr_in, 16 * KT)

            def add_to_residual(m, t, per5=0, before=None):
                dve.wait_ge(acc_done[t % 2], per5 + (t // 2 + 1))
                if before is not None:
                    dve.wait_ge(acc_read[t % 2], before)
                tt(cut(X[:, m, :]), cut(X[:, m, :]), bank(t), ALU.add).then_inc(acc_read[t % 2], 1)

            def residual_of_norm(r, m, t, before=None):
                if m < KT - 1:
                    add_to_residual(m, t, 0, before)
                    if m:
                        add_square(r, m - 1)
                    return
                add_square(r, m - 1)
                dve.wait_ge(acc_done[t % 2], t // 2 + 1)
                if before is not None:
                    dve.wait_ge(acc_read[t % 2], before)
                for c in range(NCH):
                    tt(X[:, m, cols_of(c)], X[:, m, cols_of(c)], acc[:, t % 2, c, 0:CH], ALU.add)\
                        .then_inc(res_part if c < NCH - 1 else acc_read[t % 2], 1)

            def mlp(layer):
                t0, h0 = ACC[f"mlp{layer}_0"], FT * layer

                def hidden(t, per5, hcount, slot, u):
                    dve.wait_ge(acc_read[t % 2], per5 + (t // 2 + 1))
                    link(tt(HH[:, slot, :], TT[:, u, :], TT[:, u, :], ALU.mult))
                    dve.wait_ge(h_sq, hcount + 1)
                    tt(HL[:, slot, :], TT[:, 2 + u, :], HH[:, slot, :].bitcast(F32), ALU.subtract).then_inc(h_ready, 1)

                for j in range(2):
                    hidden(t0 + j, 0, h0 + j, j, j)
                step.loop(None, 0)
                with dve.Fori(0, HG // 2 - 1) as i:
                    step.loop(i, 4)
                    for a in range(2):
                        for j in range(2):
                            hidden(t0 + 2 + 10 * a + j, i * 10, i * 4 + (h0 + 2 * (a + 1) + j), (2 * (a + 1) + j) % 4, j)
                        for m in range(KT):
                            t = t0 + 4 + 10 * a + m
                            add_to_residual(m, t, i * 10, i * 10 + (t // 2 - 4))
                    step.end(HG // 2 - 1)
                a = HG - 2
                for j in range(2):
                    hidden(t0 + 2 + 10 * a + j, 0, h0 + 2 * (a + 1) + j, (2 * (a + 1) + j) % 4, j)
                for a, at in ((HG - 2, t0 + 4 + 10 * a), (HG - 1, t0 + 12 + 10 * a)):
                    for m in range(KT):
                        if a == HG - 1:
                            residual_of_norm(2 * layer + 2, m, at + m, (at + m) // 2 - 3)
                        else:
                            add_to_residual(m, at + m, 0, (at + m) // 2 - 3)

            for m in range(KT):
                residual_of_norm(1, m, ACC[f"oute{m}"])
            norm(1)
            mlp(0)
            norm(2)
            link(dve.memset(XP[:, :, 0:3], 0.0))
            link(dve.tensor_scalar(spt[:, :], par[:, PAR["lam"][0]:PAR["lam"][1]], 0.0, None, ALU.min))
            stt(spt[:, :], spt[:, :], 2.0, par[:, PAR["lam"][0]:PAR["lam"][1]], ALU.mult, ALU.subtract).then_inc(tg_done, 1)
            dve.nop().then_inc(xp_ready, 1)
            dve.wait_ge(sp_act, 1)
            dve.wait_ge(tg_done, 1)
            link(dve.tensor_scalar(sp4[:, :], par[:, PAR["lam"][0]:PAR["lam"][1]], 0.0, -1.0, ALU.min, ALU.mult))
            link(tt(sp4[:, :], sp4[:, :], spt[:, :], ALU.add))
            dve.tensor_scalar(sp4[:, :], sp4[:, :], 4.0, None, ALU.mult).then_inc(tg_done, 1)
            dve.wait_ge(odd_in, 32)

            def conv(n):
                read_wait(dve, f"xb{n}")
                smp = XP[:, n % 2, 3 + SEQ:].rearrange("p (b s) -> p b s", b=NB)
                outs = HB[:, n, 0:SEQ], HB[:, n, SEQ:T].rearrange("p (b s) -> p b s", b=NB)
                for j in range(4):
                    w = par[:, PAR["conv_w"][0] + 4 * n + j:PAR["conv_w"][0] + 4 * n + j + 1]
                    for out, x in zip(outs, (XP[:, n % 2, j:j + SEQ], smp[:, :, j:j + NS])):
                        if j == 0:
                            link(dve.tensor_scalar(out, x, w, p_col("conv_b", n), ALU.mult, ALU.add))
                        elif j < 3:
                            link(stt(out, x, w, out, ALU.mult, ALU.add))
                        else:
                            step.run(stt(out, x, w, out, ALU.mult, ALU.add))
                dve.tensor_copy(CN[:, n, 0:3], XP[:, n % 2, SEQ:SEQ + 3])
                dve.tensor_copy(CN[:, n, 3:].rearrange("p (b s) -> p b s", b=NB), smp[:, :, NS:NS + 3]).then_inc(conv_done, 1)
                dve.wait_ge(conv_done, n + 1)

            def recur(n):
                dve.wait_ge(sig_done, 3 * n + 1)
                link(tt(TT[:, 1, :], TT[:, 1, :], HB[:, n, :], ALU.mult))
                dve.wait_ge(sig_done, 3 * n + 3)
                link(stt(TT[:, 3, :], TT[:, 3, :], 2.0, TT[:, 2, :], ALU.mult, ALU.mult))
                link(tt(TT[:, 3, :], TT[:, 3, :], TT[:, 1, :], ALU.mult))
                link(dve.tensor_scalar(TT[:, 2, :], TT[:, 2, :], 2.0, -1.0, ALU.mult, ALU.add))
                a0, b0 = TT[:, 2, SEQ:T:NS], TT[:, 3, SEQ:T:NS]
                link(tt(spt[:, 0:NB], a0, st_lru[:, n, :], ALU.mult))
                link(tt(b0, b0, spt[:, 0:NB], ALU.add))
                link(dve.memset(a0, 0.0))
                dve.tensor_tensor_scan(HB[:, n, :], TT[:, 2, :], TT[:, 3, :], 0.0, ALU.mult, ALU.add).then_inc(gt_done, 1)
                dve.wait_ge(gt_done, n + 1)
                dve.tensor_copy(LN[:, n, 0:1], HB[:, n, SEQ - 1:SEQ])
                link(dve.tensor_copy(LN[:, n, 1:], HB[:, n, SEQ + NS - 1:T:NS]))

            def apply_gate(m):
                read_wait(dve, f"gate{m}")
                tt(HB[:, m, :], HB[:, m, :], TT[:, m % 2, :], ALU.mult).then_inc(hb_ready, 1)

            conv(0)
            for n in range(KT):
                if n + 1 < KT:
                    conv(n + 1)
                recur(n)
                if n >= KT - 2:
                    apply_gate(n + 2 - KT)
            for m in range(2, KT):
                apply_gate(m)
            for k in range(KT):
                dve.wait_ge(hb_ready, k + 1)
                lo_part(XL[:, k, :], HB[:, k, :], XH[:, k, :], SPLIT["mix"] + k + 1)
            for m in range(KT):
                residual_of_norm(3, m, ACC[f"outo{m}"])
            norm(3)
            mlp(1)
            norm(4)


def tiles(w, m):
    k = w.shape[0] // P
    return w.reshape(k, P, m, P).transpose(2, 1, 0, 3).reshape(m, P, k * P)


def kernel(**inputs):
    import numpy as np
    import concourse.bacc as bacc
    from concourse.bass_utils import run_bass_kernel_spmd as run

    x = {k: np.asarray(v) for k, v in inputs.items()}
    f32 = np.float32
    tok = np.concatenate([x["x_prompt"].reshape(SEQ, D), x["x_sample"].reshape(NB * NS, D)])
    x_t = np.ascontiguousarray(tok.T).reshape(KT, P, T)

    w = x["w_in_even"][0]
    wv = w[:, 512:1024].reshape(4, 2, P, 512).transpose(0, 2, 1, 3).reshape(4, P, 1024)
    walr = np.zeros((D, P), f32)
    walr[:, :16] = w[:, 1536:1552]
    glu = tiles(x["s5_w_glu"][0], 4).reshape(2, 2, P, 512).transpose(0, 2, 1, 3).reshape(2, P, 1024)

    def mlp_tiles(layer):
        up = tiles(x["w_up"][layer], FT)
        down = x["w_down"][layer].reshape(FT, P, D)
        order = [up[0:2]]
        for a in range(1, HG):
            order += [up[2 * a:2 * a + 2], down[2 * a - 2:2 * a]]
        return np.concatenate(order + [down[FT - 2:FT]])

    w_odd = x["w_in_odd"][0]
    w_stream = np.concatenate([
        tiles(w[:, 1552:], 4), tiles(w[:, 0:256], 2), tiles(w[:, 1024:1536], 4), tiles(w[:, 256:512], 2),
        tiles(walr, 1), wv, glu, tiles(x["w_out_even"][0], KT), mlp_tiles(0),
        tiles(w_odd[:, D:], KT), tiles(w_odd[:, :D], KT), tiles(x["w_out_odd"][0], KT), mlp_tiles(1)])
    assert w_stream.shape == (NT, P, 1024)

    def cols(v):
        return v.reshape(-1, P).T

    par = np.concatenate([
        cols(x["norm_mix_even"][0]), cols(x["norm_mlp"][0]), cols(x["norm_mix_odd"][0]), cols(x["norm_mlp"][1]),
        cols(x["norm_final"]), cols(x["gla_norm"][0]), cols(x["gla_b_a2"][0]), cols(x["s5_d"][0].reshape(-1)),
        cols(x["s5_b_glu"][0]), x["conv_w"][0].reshape(4, KT, P).transpose(2, 1, 0).reshape(P, 32),
        cols(x["conv_b"][0]), cols(x["lru_b_r"][0]), cols(x["lru_b_i"][0]), cols(x["lru_lam"][0])], axis=1)

    def states(v):
        v = v.reshape((16, 2, 64) + v.shape[2:])
        return np.moveaxis(v, 0, 2).reshape(P, -1)

    dt = np.broadcast_to(x["s5_log_dt"][0][:, None], (32, 64))
    par5 = np.concatenate([
        states(x["s5_a_re"][0]), states(x["s5_a_im"][0]), states(dt), states(x["s5_b_re"][0]), states(x["s5_b_im"][0]),
        states(x["s5_c_re"][0].transpose(0, 2, 1)), states(x["s5_c_im"][0].transpose(0, 2, 1)),
        states(x["state_s5_re"][0].transpose(1, 2, 0)), states(x["state_s5_im"][0].transpose(1, 2, 0))], axis=1)

    cst = np.zeros((P, NCST), f32)
    i = np.arange(P)
    cst[:, 0:128] = np.eye(P)
    cst[:, 128:256] = i[:, None] <= i[None, :]
    j = np.arange(32)
    cst[0:32, 256:288] = (j[:, None] <= j[None, :]) & (j[:, None] // NS == j[None, :] // NS)
    cst[0:32, 288:296] = j[:, None] // NS == np.arange(NB)[None, :]
    b = np.arange(NBL)
    cst[:, 296:360] = (b[None, :] < b[:, None]).reshape(1, -1)
    cst[:, 360:488] = np.arange(NC)[None, :]

    w_ri = np.stack([x["lru_w_r"][0], x["lru_w_i"][0]], axis=1).transpose(0, 2, 1, 3)
    st_gla = x["state_gla"][0].reshape(NB, 2, P, P).transpose(1, 2, 0, 3)
    odd_lru = x["state_lru"][0].reshape(NB, KT, P).transpose(2, 1, 0)
    odd_conv = x["state_conv"][0].reshape(NB, 3, KT, P).transpose(3, 2, 0, 1)

    nc = bacc.Bacc("TRN2", target_bir_lowering=False, num_devices=1)
    arrays, args = {}, []
    for name, a in (("x_t", x_t), ("w_stream", w_stream), ("par", par), ("par5", par5), ("cst", cst),
                    ("w_a2", x["gla_w_a2"][0]), ("w_ri", w_ri), ("st_gla", st_gla), ("odd_lru", odd_lru),
                    ("odd_conv", odd_conv)):
        arrays[f"in_{name}"] = np.ascontiguousarray(a)
        args.append(nc.dram_tensor(f"in_{name}", a.shape, F32, kind="ExternalInput").ap())
    for name, shape in (("y_t", (KT, P, T)), ("s5_out", (P, 2, 16, 1 + NB)), ("lru_out", (P, KT, 1 + NB)),
                        ("conv_out", (P, KT, 3 * (1 + NB))), ("gla_p", (P, 2, P)), ("gla_s", (2, P, NB, P))):
        args.append(nc.dram_tensor(f"out_{name}", shape, F32, kind="ExternalOutput").ap())
    trunk_kernel(nc, *args)
    r = run(nc, [arrays], core_ids=[0]).results[0]
    r = {k.removeprefix("out_"): np.asarray(v) for k, v in r.items()}

    y = r["y_t"].reshape(D, T).T
    s5 = r["s5_out"].reshape(2, 64, 2, 16, 1 + NB).transpose(2, 4, 3, 0, 1).reshape(2, 1 + NB, 32, 64)
    lru = r["lru_out"].transpose(2, 1, 0).reshape(1 + NB, D)
    conv = r["conv_out"].reshape(P, KT, 1 + NB, 3).transpose(2, 3, 1, 0).reshape(1 + NB, 3, D)
    gla_prompt = r["gla_p"].reshape(2, 64, 2, P).transpose(2, 0, 1, 3).reshape(1, 1, 4, 64, P)
    gla_sample = r["gla_s"].reshape(2, 2, 64, NB, P).transpose(3, 0, 1, 2, 4).reshape(1, NB, 4, 64, P)
    c = np.ascontiguousarray
    return (c(y[:SEQ]).reshape(1, SEQ, D), c(y[SEQ:]).reshape(NB, NS, D),
            c(gla_prompt), c(s5[0, :1])[None], c(s5[1, :1])[None], c(lru[:1])[None], c(conv[:1])[None],
            c(gla_sample), c(s5[0, 1:])[None], c(s5[1, 1:])[None], c(lru[1:])[None], c(conv[1:])[None])
```

```python
from contextlib import ExitStack

import concourse.bass as bass
from concourse import mybir

F32 = mybir.dt.float32
F32R = mybir.dt.float32r
ALU = mybir.AluOpType
ACT = mybir.ActivationFunctionType

P = 128
D = 1024
KT = D // P
SEQ = 1024
NB, NS = 8, 4
T = SEQ + NB * NS
CH = 352
NCH = T // CH
FT = 4 * D // P
EPS = 1e-6

PAR = {}
_at = 0
for _name, _n in (("g_mix_even", 8), ("g_mlp0", 8), ("g_mix_odd", 8), ("g_mlp1", 8), ("g_final", 8),
                  ("g_head", 4), ("b_a2", 2), ("s5_d", 4), ("b_glu", 4), ("conv_w", 32), ("conv_b", 8),
                  ("b_r", 8), ("b_i", 8), ("lam", 8)):
    PAR[_name] = (_at, _at + _n)
    _at += _n
NPAR = _at
PAR5 = {}
_at = 0
for _name, _n in (("a_re", 16), ("a_im", 16), ("log_dt", 16), ("b_re", 256), ("b_im", 256),
                  ("c_re", 256), ("c_im", 256), ("h0_re", 128), ("h0_im", 128)):
    PAR5[_name] = (_at, _at + _n)
    _at += _n
NPAR5 = _at
CST = {"ident": (0, 128), "tri": (128, 256), "smask": (256, 288), "bmask": (288, 296), "tri8": (296, 360),
       "count": (360, 488)}
NCST = 488


class Chain:

    def __init__(self, eng, sem):
        self.eng, self.sem, self.n, self.var, self.per = eng, sem, 0, None, 0

    def run(self, ins):
        self.n += 1
        return ins.then_inc(self.sem, 1)

    def value(self):
        return self.n if self.var is None else self.var * self.per + self.n

    def wait(self):
        self.eng.wait_ge(self.sem, self.value())

    def link(self, ins):
        self.run(ins)
        self.wait()

    def loop(self, var, per):
        self.var, self.per, self.first = var, per, self.n

    def end(self, trips):
        assert self.n - self.first == self.per, (self.n - self.first, self.per)
        self.var, self.n = None, self.first + self.per * trips


def index(names):
    return {name: n for n, name in enumerate(names)}


HG = FT // 2
MLP_TILES = 2 * FT
STREAM = index(["u0", "u1", "u2", "u3", "q0", "q1", "g0", "g1", "g2", "g3", "k0", "k1", "alr",
                "v0", "v1", "v2", "v3", "glu0", "glu1"] + [f"oute{m}" for m in range(KT)]
               + [f"mlp0_{n}" for n in range(MLP_TILES)]
               + [f"xb{n}" for n in range(KT)] + [f"gate{n}" for n in range(KT)]
               + [f"outo{m}" for m in range(KT)] + [f"mlp1_{n}" for n in range(MLP_TILES)])
NT = len(STREAM)
RAW, SLOTS = 2, 4
POOL_LOADS = 20

_odd = ["xb0", "xb1"]
for _n in range(KT):
    _odd += [f"r{_n}", f"i{_n}"] + ([f"xb{_n + 2}"] if _n + 2 < KT else [f"gate{_n + 2 - KT}"])
_odd += [f"gate{_n}" for _n in range(2, KT)]
ACC = index(["norm0", "u0", "u1", "u2", "u3", "q0", "q1", "g0", "g1", "g2", "g3",
        "k0", "k1", "alr", "lg0", "lg1", "v0", "v1", "v2", "glu0", "glu1", "glu2", "glu3",
             "head0", "head1", "head2", "head3"] + [f"oute{m}" for m in range(KT)]
            + ["norm1"] + [f"mlp0_{n}" for n in range(HG * (2 + KT))]
            + ["norm2"] + _odd + [f"outo{m}" for m in range(KT)]
            + ["norm3"] + [f"mlp1_{n}" for n in range(HG * (2 + KT))] + ["norm4"])

SPLIT = {}
_at = 0
for _name, _n in (("norm0", NCH * KT), ("z", 4), ("zg", 4), ("o", 4), ("norm1", NCH * KT), ("norm2", NCH * KT),
                   ("mix", 8), ("norm3", NCH * KT)):
    SPLIT[_name] = _at
    _at += _n

SSQ_N = KT - 1 + NCH
L = 8
NC = SEQ // L
PQ = 4
GQ = 8
NG = 4
CW = NC + 2 * NB
YW = NC + NB
GC = 128
NGC = SEQ // GC
BL = 16
NBL = GC // BL
MAGIC = 1.5 * 2.0 ** 23
CUT12 = 1.5 * 2.0 ** 13
TWO_PI_1, TWO_PI_2, TWO_PI_3 = 6.28125, 0.0019350051879882812, 3.0199159819567e-07


def trunk_kernel(nc, x_t, w_stream, par_d, par5_d, cst_d, w_a2, w_ri, st_gla, odd_lru, odd_conv,
                 y_t, s5_out, lru_out, conv_out, gla_p, gla_s):
    u_scr = nc.dram_tensor("u_scratch", (NG, P, L, CW), F32, kind="Internal").ap()
    y_scr = nc.dram_tensor("y_scratch", (NG, P, GQ, YW), F32, kind="Internal").ap()
    z_scr = nc.dram_tensor("z_scratch", (NG, P, T), F32, kind="Internal").ap()
    g_scr = nc.dram_tensor("g_scratch", (NG, P, T), F32, kind="Internal").ap()

    with ExitStack() as ctx:
        def sem(name):
            return ctx.enter_context(nc.semaphore(name))

        def sb(stack, name, shape, dt=F32):
            return stack.enter_context(nc.sbuf_tensor(name, shape, dt))

        with ExitStack() as spare:
            QM1 = sb(spare, "QM1", [P, 2 * T])
            QI1 = sb(spare, "QI1", [P, 2 * SEQ])
        XH = sb(ctx, "XH", [P, KT, T], F32R)
        with ExitStack() as spare:
            E1 = sb(spare, "E1", [P, T])
            KN1 = sb(spare, "KN1", [P, T])
            KE1 = sb(spare, "KE1", [P, T])
            GB1 = sb(spare, "GB1", [P, NGC, NBL, NBL])
            gs1 = sb(spare, "gs1", [P, 6, 64])
        XL = sb(ctx, "XL", [P, KT, T], F32R)
        WR = sb(ctx, "WR", [P, RAW, 1024])
        WH = sb(ctx, "WH", [P, SLOTS, 1024], F32R)
        WL = sb(ctx, "WL", [P, SLOTS, 1024], F32R)
        TT = sb(ctx, "TT", [P, 4, T])
        par = sb(ctx, "par", [P, NPAR])
        cst = sb(ctx, "cst", [P, NCST])
        ones = sb(ctx, "ones", [P, P])
        few = sb(ctx, "few", [P, 8])
        sp4 = sb(ctx, "sp4", [P, KT])
        sp8 = sb(ctx, "sp8", [P, KT])
        spt = sb(ctx, "spt", [P, KT])
        SO = sb(ctx, "SO", [P, 2, 16, 1 + NB])
        with ExitStack() as area:
            X0 = sb(area, "X0", [P, KT, T])
        with ExitStack() as area:
            Q = sb(area, "Q", [P, 2, T])
            with ExitStack() as s5b:
                PTR = sb(s5b, "PTR", [P, 2, 12, NC])
                VH1 = sb(s5b, "VH1", [P, 2 * PQ * 144])
            K = sb(area, "K", [P, 2, T])
            LA = sb(area, "LA", [P, 2, T])
            with ExitStack() as s5a:
                XA = sb(s5a, "XA", [P, 2, PQ, L, 16])
                WIN = sb(s5a, "WIN", [P, 2, PQ, P])
                WO = sb(s5a, "WO", [P, 2, PQ, L, 16])
                M = sb(s5a, "M", [P, GQ, L, 16])
                T7 = sb(s5a, "T7", [P, GQ * 16])
                PT0 = sb(s5a, "PT0", [P, 2, PQ, NC])
                U = sb(s5a, "U", [P, 2, GQ, CW])
                VH0 = sb(s5a, "VH0", [P, 2 * PQ * 144])
                G = sb(s5a, "G", [P, GQ * YW])
                UR = sb(s5a, "UR", [P, L, CW])
                p5 = sb(s5a, "p5", [P, NPAR5])
                pw = sb(s5a, "pw", [P, 2, 9, 16])
                rot = sb(s5a, "rot", [P, 2, 16])
                sm = sb(s5a, "sm", [P, 14, 16])
                CB = sb(s5a, "CB", [P, 2, 16, 32])
                wa2 = sb(s5a, "wa2", [16, 2 * P])
            with ExitStack() as gla:
                V = sb(gla, "V", [P, NGC + 1, 512])
                QM0 = sb(gla, "QM0", [P, 2 * T])
                QI0 = sb(gla, "QI0", [P, 2 * SEQ])
                KX = sb(gla, "KX", [P, 2, 1152])
                SC = sb(gla, "SC", [P, 2, 256])
                KTR = sb(gla, "KTR", [P, 2, P])
                S = sb(gla, "S", [P, 2, P])
                GB0 = sb(gla, "GB0", [P, NGC, NBL, NBL])
                gs0 = sb(gla, "gs0", [P, 6, 64])
                SS0 = sb(gla, "SS0", [P, NB, P])
        X = sb(ctx, "X", [P, KT, T])
        with ExitStack() as area:
            HH = sb(area, "HH", [P, 4, T], F32R)
            HL = sb(area, "HL", [P, 4, T], F32R)
        HB = sb(ctx, "HB", [P, KT, T])
        XP = sb(ctx, "XP", [P, 2, 3 + SEQ + 7 * NB])
        WRI = sb(ctx, "WRI", [P, 2, 2, P])
        st_lru = sb(ctx, "st_lru", [P, KT, NB])
        st_conv = sb(ctx, "st_conv", [P, KT, NB, 3])
        LN = sb(ctx, "LN", [P, KT, 1 + NB])
        CN = sb(ctx, "CN", [P, KT, 3 * (1 + NB)])
        acc = ctx.enter_context(nc.psum_tensor("acc", [P, 2, NCH, 512], F32))
        ms = ctx.enter_context(nc.psum_tensor("ms", [P, 2, 512], F32))
        QM, QI, GB, gs = (QM0, QM1), (QI0, QI1), (GB0, GB1), (gs0, gs1)
        EE = (TT[:, 0, :], E1[:, :])
        KN = (TT[:, 1, :], KN1[:, :])
        KE = (TT[:, 2, :], KE1[:, :])
        SS = (SS0[:, :, :], LA[:, 0, 0:NB * P].rearrange("p (s n) -> p s n", s=NB))
        EX = (KX[:, 0, 0:T], E1[:, :])
        EI = (KX[:, 1, 0:T], TT[:, 3, :])
        glb = acc[:, :, :, :].rearrange("p s c n -> p (s c) n")

        par_in, par5_in, cst_in, wa2_in = sem("par_in"), sem("par5_in"), sem("cst_in"), sem("wa2_in")
        x_in = [sem(f"x_in{c}") for c in range(NCH)]
        xr_in = sem("xr_in")
        w_first = [sem(f"w_first{r}") for r in range(RAW)]
        w_in = [sem(f"w_in{r}") for r in range(RAW)]
        u_out, m_in, y_out, y_in, ud_in = sem("u_out"), sem("m_in"), sem("y_out"), sem("y_in"), sem("ud_in")
        u_in = [sem("u_in0"), sem("u_in1")]
        z_out, g_out = sem("z_out"), [sem("g_out0"), sem("g_out1")]
        z_in = [sem("z_in0"), sem("z_in1")]
        g_in = [sem("g_in0"), sem("g_in1")]
        ss_in, ss_out, s_out = [sem("ss_in0"), sem("ss_in1")], sem("ss_out"), sem("s_out")
        odd_in, wri_in = sem("odd_in"), [sem("wri_in0"), sem("wri_in1")]
        y_sent, small_out = sem("y_sent"), sem("small_out")
        w_hi, w_ready, w_used = sem("w_hi"), sem("w_ready"), sem("w_used")
        acc_done = [sem("acc_done0"), sem("acc_done1")]
        acc_read = [sem("acc_read0"), sem("acc_read1")]
        sq_done, ssq_add, sq_used = sem("sq_done"), sem("ssq_add"), sem("sq_used")
        res_part, norm_sum, ln_done, rs_done = sem("res_part"), sem("norm_sum"), sem("ln_done"), sem("rs_done")
        xn_done, xh_done, xl_done = sem("xn_done"), sem("xh_done"), sem("xl_done")
        h_sq, h_ready = sem("h_sq"), sem("h_ready")
        prep_act, prep_dve, const_ready = sem("prep_act"), sem("prep_dve"), sem("const_ready")
        phi_ready, pool_angles = sem("phi_ready"), sem("pool_angles")
        angle_ready, pt_ready = sem("angle_ready"), sem("pt_ready")
        ms_done, ms_read = sem("ms_done"), sem("ms_read")
        ur_ready, xa_ready, wo_ready = sem("ur_ready"), sem("xa_ready"), sem("wo_ready")
        st_ready, zin_done, z_done = sem("st_ready"), sem("zin_done"), sem("z_done")
        alr_ready, lg_dve, lg_act = sem("alr_ready"), sem("lg_dve"), sem("lg_act")
        gg_done = sem("gg_done")
        pair_exps, pair_sums, pair_ready = sem("pair_exps"), sem("pair_sums"), sem("pair_ready")
        qm_zero = sem("qm_zero")
        kx_ready, sc_done, sc_ready = sem("kx_ready"), sem("sc_done"), sem("sc_ready")
        kt_done, kt_ready = sem("kt_done"), sem("kt_ready")
        o_done, o_read, kv_done, s_ready = sem("o_done"), sem("o_read"), sem("kv_done"), sem("s_ready")
        sm_done, smc_ready, smk_ready = sem("sm_done"), sem("smc_ready"), sem("smk_ready")
        so_done, so_read, skv_done, sst_ready = sem("so_done"), sem("so_read"), sem("skv_done"), sem("sst_ready")
        head_g, head_rs = sem("head_g"), sem("head_rs")
        lam_dve, lam_act = sem("lam_dve"), sem("lam_act")
        xp_ready, conv_done, gates_done = sem("xp_ready"), sem("conv_done"), sem("gates_done")
        states_done, hb_ready = sem("states_done"), sem("hb_ready")
        dve_step, act_step = sem("dve_step"), sem("act_step")

        def p_col(name, n):
            return par[:, PAR[name][0] + n:PAR[name][0] + n + 1]

        def p5c(name):
            return p5[:, PAR5[name][0]:PAR5[name][1]]

        def c_(name):
            return cst[:, CST[name][0]:CST[name][1]]

        def cut(ap):
            return ap.rearrange("p (c n) -> p c n", n=CH)

        def bank(t):
            return acc[:, t % 2, :, 0:CH]

        def cols_of(c):
            return slice(c * CH, (c + 1) * CH)

        def done_wait(eng, name):
            t = ACC[name]
            eng.wait_ge(acc_done[t % 2], t // 2 + 1)

        def read_wait(eng, name):
            t = ACC[name]
            eng.wait_ge(acc_read[t % 2], t // 2 + 1)

        MS = index("a0 b0 c0 d0 a1 b1 c1 d1 e0 f0 a2 b2 e1 f1 c2 d2 a3 b3 e2 f2 c3 d3 e3 f3".split())
        ident, tri = c_("ident"), c_("tri").rearrange("p (i n) -> p i n", i=NBL)
        def VV(q):
            return (VH0, VH1)[q % 2][:, 0:2 * PQ * YW].rearrange("p (r q n) -> p r q n", r=2, q=PQ)

        def HV(q):
            return (VH0, VH1)[q % 2][:, :].rearrange("p (r q n) -> p r q n", r=2, q=PQ)

        def YR(q):
            return (VH0, VH1)[q % 2][:, 0:L * YW].rearrange("p (l n) -> p l n", l=L)

        def GV(q):
            flat = G if q == 0 else UR[:, :, :].rearrange("p l n -> p (l n)")
            return flat[:, 0:2 * PQ * NC].rearrange("p (r q n) -> p r q n", r=2, q=PQ)

        YG = G[:, :].rearrange("p (g n) -> p g n", g=GQ)
        ALR = UR[:, :, :].rearrange("p l n -> p (l n)")[0:16, 0:T]
        block = ctx.enter_context(nc.Block())

        @block.sync
        def _(sp):
            sp.dma_start(par[:, :], par_d).then_inc(par_in, 16)
            for c in range(NCH):
                sp.dma_start(X0[:, :, cols_of(c)], x_t.rearrange("k p t -> p k t")[:, :, cols_of(c)]).then_inc(x_in[c], 16)
            sp.dma_start(cst[:, :], cst_d).then_inc(cst_in, 16)
            sp.dma_start(p5[:, :], par5_d).then_inc(par5_in, 16)
            sp.dma_start(wa2[:, :], w_a2).then_inc(wa2_in, 16)

            def store_u(q):
                read_wait(sp, f"u{q}")
                sp.dma_start(u_scr[q], UR[:, :, :]).then_inc(u_out, 16)

            def load_u(q):
                sp.wait_ge(u_out, 16 * (q + 1))
                if q >= 2:
                    sp.wait_ge(zin_done, q - 1)
                src = u_scr[q].rearrange("(g c) l w -> l c g w", g=GQ)
                for j in range(L):
                    sp.dma_start(U[16 * j:16 * j + 16, q % 2, :, :], src[j]).then_inc(u_in[q % 2], 16)

            def load_m(q):
                sp.wait_ge(ms_read, MS[f"b{q}"] + 1)
                if q >= 1:
                    sp.wait_ge(ms_done, MS[f"f{q - 1}"] + 1)
                for i in range(L):
                    sp.dma_start(M[0:16 * (i + 1), :, i, :],
                                 T7[16 * (L - 1 - i):P, :].rearrange("p (g c) -> p g c", c=16)).then_inc(m_in, 16)

            def turn_y(q):
                sp.wait_ge(ms_read, MS[f"f{q}"] + 1)
                sp.dma_start(y_scr[q], YG).then_inc(y_out, 16)
                sp.wait_ge(y_out, 16 * (q + 1))
                src = y_scr[q].rearrange("(i c) g n -> g c i n", i=L)
                for g in range(GQ):
                    sp.dma_start(YR(q)[16 * g:16 * g + 16], src[g]).then_inc(y_in, 16)
                sp.dma_start(U[:, q % 2, :, :].rearrange("p g w -> p (g w)"),
                             u_scr[q].rearrange("p l w -> p (l w)")).then_inc(ud_in, 16)

            store_u(0)
            load_u(0)
            store_u(1)
            load_u(1)
            store_u(2)
            sp.wait_ge(u_out, 48)
            store_u(3)
            load_m(0)
            for q in range(NG):
                if q + 1 < NG:
                    load_m(q + 1)
                turn_y(q)
                if q + 2 < NG:
                    load_u(q + 2)
                sp.wait_ge(z_done, q + 1)
                sp.dma_start(z_scr[q], TT[:, 2, :]).then_inc(z_out, 16)
            sp.wait_ge(z_out, 16 * NG)
            for r in range(2):
                sp.wait_ge(g_out[r], 32)
            sp.wait_ge(lg_dve, 4)
            for k in range(NG):
                if k >= 2:
                    sp.wait_ge(xl_done, SPLIT["z"] + k - 1)
                sp.dma_start(TT[:, k % 2, :], z_scr[k]).then_inc(z_in[k % 2], 16)
            for k in range(NG):
                sp.wait_ge(xl_done, (SPLIT["z"] + k + 3) if k < 2 else (SPLIT["zg"] + k - 1))
                sp.dma_start(TT[:, k % 2, :], z_scr[k]).then_inc(z_in[k % 2], 16)
            def load_w(n, r, first=False):
                sp.wait_ge(w_ready, n - (RAW - 1))
                sp.dma_start(WR[:, r, :], w_stream[n]).then_inc(w_in[r], 16)

            gla_w = STREAM["glu0"] + 6
            for n in range(POOL_LOADS, gla_w):
                load_w(n, n % RAW)
            for p in range(2):
                if p:
                    sp.wait_ge(pair_ready, 1)
                sp.dma_start(SS[p], st_gla[p]).then_inc(ss_in[p], 16)
            sp.wait_ge(kx_ready, NGC + 1)
            for h in range(2):
                sp.dma_start(TT[:, 2 + h, :], g_scr[h]).then_inc(g_in[h], 16)
            for p in range(2):
                sp.wait_ge(sst_ready, NB * (p + 1))
                sp.dma_start(gla_s[p], SS[p]).then_inc(ss_out, 16)
            sp.dma_start(gla_p, S[:, :, :]).then_inc(s_out, 16)
            for h in range(2, 4):
                sp.wait_ge(head_g, h - 1)
                sp.dma_start(TT[:, 2 + h % 2, :], g_scr[h]).then_inc(g_in[h % 2], 16)
            sp.wait_ge(xl_done, SPLIT["o"] + 4)
            sp.wait_ge(s_out, 16)
            sp.wait_ge(ss_out, 32)
            for k in range(KT):
                sp.dma_start(X[:, k, :], x_t[k]).then_inc(xr_in, 16)
            at = gla_w
            while (NT - at) % 4:
                load_w(at, at % RAW)
                at += 1
            with sp.Fori(0, (NT - at) // 4) as i:
                for j in range(4):
                    n = at + j
                    sp.wait_ge(w_ready, i * 4 + (n - (RAW - 1)))
                    sp.dma_start(WR[:, n % RAW, :], w_stream[i * 4 + n]).then_inc(w_in[n % RAW], 16)
            for c in range(NCH):
                for k in range(0, KT, 2):
                    sp.wait_ge(xn_done, (4 * NCH + c) * KT + k + 2)
                    sp.dma_start(y_t.rearrange("k p t -> p k t")[:, k:k + 2, cols_of(c)], X[:, k:k + 2, cols_of(c)])\
                      .then_inc(y_sent, 16)
            sp.wait_ge(y_sent, 16 * NCH * KT // 2)
            sp.wait_ge(small_out, 3 * 16)

        @block.gpsimd
        def _(pool):
            def split(r, s, loaded, used, count):
                pool.wait_ge(*loaded)
                if used is not None:
                    pool.wait_ge(w_used, used)
                pool.tensor_tensor(WH[:, s, :], WR[:, r, :], ones[:, 0:1].broadcast_to([P, 1024]), ALU.mult)\
                    .then_inc(w_hi, 1)
                pool.wait_ge(w_hi, count)
                pool.tensor_tensor(WL[:, s, :], WR[:, r, :], WH[:, s, :].bitcast(F32), ALU.subtract)\
                    .then_inc(w_ready, 1)

            def angles():
                shape = [P, 12, NC]
                rows = TT[:, 0:3, :].rearrange("p a n -> p (a n)")
                x, u = PTR[:, 1, :, :], PTR[:, 0, :, :]
                t, rest = [rows[:, 12 * NC * r:12 * NC * (r + 1)].rearrange("p (g n) -> p g n", n=NC) for r in range(2)]
                count = c_("count").unsqueeze(1).broadcast_to(shape)

                def constant(i):
                    return few[:, 2 + i:3 + i].unsqueeze(2).broadcast_to(shape)

                pool.wait_ge(phi_ready, 1)
                pool.wait_ge(cst_in, 16)
                pool.wait_ge(xl_done, SPLIT["norm0"] + NCH * KT)
                pool.tensor_tensor(x, count, sm[:, 11, PQ:16].unsqueeze(2).broadcast_to(shape), ALU.mult).then_inc(pool_angles, 1)
                pool.tensor_tensor(rest, count, sm[:, 13, PQ:16].unsqueeze(2).broadcast_to(shape), ALU.mult).then_inc(pool_angles, 1)
                pool.wait_ge(pool_angles, 2)
                pool.tensor_tensor(t, x, rest, ALU.add).then_inc(pool_angles, 1)
                for n, (i, op) in enumerate(((0, ALU.mult), (1, ALU.add), (1, ALU.subtract))):
                    pool.wait_ge(pool_angles, 3 + n)
                    pool.tensor_tensor(t, t, constant(i), op).then_inc(pool_angles, 1)
                for n in range(3):
                    pool.wait_ge(pool_angles, 6 + 2 * n)
                    pool.tensor_tensor(u, t, constant(2 + n), ALU.mult).then_inc(pool_angles, 1)
                    pool.wait_ge(pool_angles, 7 + 2 * n)
                    pool.tensor_tensor(x, x, u, ALU.subtract).then_inc(pool_angles, 1)
                pool.wait_ge(pool_angles, 12)
                pool.tensor_tensor(x, x, rest, ALU.add).then_inc(pool_angles, 1)

            for n in range(RAW):
                pool.dma_start(WR[:, n, :], w_stream[n]).then_inc(w_first[n], 16)
            pool.wait_ge(const_ready, 1)
            at = POOL_LOADS
            while (NT - at) % 4:
                at += 1
            for n in range(at):
                if n == 6:
                    angles()
                if n == STREAM["glu1"] + SLOTS:
                    done_wait(pool, "glu3")
                    pool.memset(QM[1][:, :], 0.0).then_inc(qm_zero, 1)
                loaded = ((w_first[n % RAW], 16 * (n // RAW + 1)) if n < POOL_LOADS else
                          (w_in[n % RAW], 16 * ((n - POOL_LOADS) // RAW + 1)))
                split(n % RAW, n % SLOTS, loaded, n - SLOTS + 1 if n >= SLOTS else None, n + 1)
                if n + RAW < POOL_LOADS:
                    pool.wait_ge(w_ready, n + 1)
                    pool.dma_start(WR[:, n % RAW, :], w_stream[n + RAW]).then_inc(w_first[n % RAW], 16)
            with pool.Fori(0, (NT - at) // 4) as i:
                for j in range(4):
                    n = at + j
                    loaded = (w_in[n % RAW], i * 32 + 16 * ((n - POOL_LOADS) // RAW + 1))
                    split(n % RAW, n % SLOTS, loaded, i * 4 + (n - SLOTS + 1), i * 4 + (n + 1))

        @block.tensor
        def _(pe):
            held = [0]

            def mm(out, lhs, rhs, start, stop):
                ins = pe.matmul(out, lhs, rhs, start=start, stop=stop)
                if held[0]:
                    held[0] -= 1
                    ins.then_inc(w_used, 1)
                return ins

            PASSES = ((WH, 0), (WH, 1), (WL, 0))

            def claim(t):
                if t >= 2:
                    pe.wait_ge(acc_read[t % 2], t // 2)

            def product(t, slots, cols, ops, nk=KT, xn=None, last_w=False, ks=None):
                ks = ks or range(nk)
                for k in ks:
                    if xn is not None and (ks[0] == 0 or k < ks[0]):
                        pe.wait_ge(xl_done, xn + k + 1)
                    if last_w and k:
                        held[0] += 1
                    s, col = slots(k), cols(k)
                    for c in range(NCH):
                        for i, (w, x) in enumerate(PASSES):
                            last = mm(acc[:, t % 2, c, 0:CH], w[:, s, col:col + P],
                                      ops[x](k)[:, cols_of(c)], k == ks[0] and i == 0, k == ks[-1] and i == 2)
                last.then_inc(acc_done[t % 2], 1)

            XOPS = (lambda k: XH[:, k, :], lambda k: XL[:, k, :])

            def project(name, acc_name, xn=None, ks=None):
                n, t = STREAM[name], ACC[acc_name]
                pe.wait_ge(w_ready, n + 1)
                claim(t)
                product(t, lambda k: n % SLOTS, lambda k: k * P, XOPS, xn=xn, ks=ks)
                held[0] += 1

            def norm(r):
                t = ACC[f"norm{r}"]
                claim(t)
                for c in range(NCH):
                    if r == 0:
                        for k in range(KT):
                            n = c * KT + k
                            pe.wait_ge(sq_done, n + 1)
                            pe.matmul(acc[:, t % 2, c, 0:CH], ones[:, :], TT[:, 2, cols_of(n % NCH)],
                                      start=(k == 0), stop=(k == KT - 1))\
                              .then_inc(acc_done[t % 2] if n == NCH * KT - 1 else sq_used, 1)
                        continue
                    pe.wait_ge(ssq_add, SSQ_N * (r - 1) + KT + c)
                    if c == 0:
                        mm(acc[:, t % 2, 0, 0:CH // 2], ones[:, :], TT[:, 2, 0:CH // 2], True, True)
                        last = mm(acc[:, t % 2, 0, CH // 2:CH], ones[:, :], TT[:, 2, CH // 2:CH], True, True)
                    else:
                        last = mm(acc[:, t % 2, c, 0:CH], ones[:, :], TT[:, 2, cols_of(c)], True, True)
                    last.then_inc(acc_done[t % 2] if c == NCH - 1 else norm_sum, 1)

            def project_pair(names, acc_names, xn):
                n, t = STREAM[names[0]], ACC[acc_names[0]]
                claim(t)
                claim(t + 1)
                for c in range(NCH):
                    for k in range(KT):
                        pe.wait_ge(xl_done, xn + c * KT + k + 1)
                        for j in range(2):
                            if c == k == 0:
                                pe.wait_ge(w_ready, n + j + 1)
                            for i, (w, x) in enumerate(PASSES):
                                last = mm(acc[:, (t + j) % 2, c, 0:CH], w[:, (n + j) % SLOTS, k * P:(k + 1) * P],
                                          XOPS[x](k)[:, cols_of(c)], k == 0 and i == 0, k == KT - 1 and i == 2)
                            if c == NCH - 1 and k == KT - 1:
                                last.then_inc(acc_done[(t + j) % 2], 1)
                                held[0] += 1

            def ms_claim(step):
                if MS[step]:
                    pe.wait_ge(ms_read, MS[step])

            def step_a(q):
                pe.wait_ge(xa_ready, q + 1)
                ms_claim(f"a{q}")
                for r in range(2):
                    for g in range(PQ):
                        last = pe.transpose(ms[:, r, g * P:(g + 1) * P],
                                            XA[:, r, g, :, :].rearrange("p l c -> p (l c)"), ident)
                last.then_inc(ms_done, 1)

            def step_b(q):
                ms_claim(f"b{q}")
                for g in range(PQ):
                    for r in range(2):
                        last = pe.matmul(ms[:, 0, g * 32:(g + 1) * 32], XA[:, r, g, :, :].rearrange("p l c -> p (l c)"),
                                         CB[:, r, PQ * q + g, :], start=(r == 0), stop=(r == 1))
                last.then_inc(ms_done, 1)

            def step_cd(q, r):
                if r == 0:
                    pe.wait_ge(u_in[q % 2], 16 * L * (q // 2 + 1))
                ms_claim(("c", "d")[r] + str(q))
                for g in range(GQ):
                    h = 64 * (g % 2)
                    last = pe.matmul(ms[h:h + 64, g // 4, (g // 2 % 2) * YW:(g // 2 % 2 + 1) * YW],
                                     WIN[:, r, g // 2, h:h + 64], U[:, q % 2, g, NB:NB + YW], start=True, stop=True)
                last.then_inc(ms_done, 1)

            def step_ef(q, half):
                if half == 0:
                    pe.wait_ge(m_in, 16 * L * (q + 1))
                    pe.wait_ge(st_ready, q + 1)
                    pe.wait_ge(wo_ready, q + 1)
                ms_claim(("e", "f")[half] + str(q))
                for g in range(4 * half, 4 * half + 4):
                    h = 64 * (g % 2)
                    out = ms[:, g % 2, (g // 2 % 2) * YW:(g // 2 % 2 + 1) * YW]
                    pe.matmul(out, M[:, g, :, :].rearrange("p l c -> p (l c)"), U[:, q % 2, g, 0:YW], start=True, stop=False)
                    for r in range(2):
                        last = pe.matmul(out, WO[h:h + 64, r, g // 2, :, :].rearrange("p l c -> p (l c)"),
                                         HV(q)[h:h + 64, r, g // 2, 0:YW], start=False, stop=(r == 1))
                last.then_inc(ms_done, 1)

            def logits(p):
                t = ACC[f"lg{p}"]
                claim(t)
                for c in range(NCH):
                    last = mm(acc[:, t % 2, c, 0:CH], wa2[0:16, p * P:(p + 1) * P], ALR[:, c * CH:(c + 1) * CH], True, True)
                last.then_inc(acc_done[t % 2], 1)

            def values():
                n = STREAM["v0"]
                for j in range(3):
                    t = ACC[f"v{j}"]
                    claim(t)
                    for b in range(3):
                        at = min((3 * j + b) * GC, T - GC)
                        for k in range(KT):
                            if j == b == k % 2 == 0:
                                pe.wait_ge(w_ready, n + k // 2 + 1)
                            if j == b == 2 and k % 2 == 0 and k:
                                held[0] += 1
                            s, col = (n + k // 2) % SLOTS, (k % 2) * 512
                            for i, (w, x) in enumerate(((WH, XH), (WL, XH), (WH, XL))):
                                last = mm(acc[:, t % 2, b, :], x[:, k, at:at + GC], w[:, s, col:col + 512],
                                          k == 0 and i == 0, k == KT - 1 and i == 2)
                    last.then_inc(acc_done[t % 2], 1)
                held[0] += 1

            pe.wait_ge(const_ready, 1)
            norm(0)
            project_pair(("u0", "u1"), ("u0", "u1"), SPLIT["norm0"])
            project("u2", "u2")
            project("u3", "u3")
            pe.wait_ge(cst_in, 16)
            step_a(0)
            step_b(0)
            project("q0", "q0")
            step_cd(0, 0)
            step_cd(0, 1)
            step_a(1)
            step_b(1)
            project("q1", "q1")
            step_cd(1, 0)
            step_cd(1, 1)
            step_ef(0, 0)
            step_ef(0, 1)
            project("g0", "g0")
            step_a(2)
            step_b(2)
            step_ef(1, 0)
            step_ef(1, 1)
            step_cd(2, 0)
            step_cd(2, 1)
            project("g1", "g1")
            step_a(3)
            step_b(3)
            step_ef(2, 0)
            step_ef(2, 1)
            project("g2", "g2")
            step_cd(3, 0)
            step_cd(3, 1)
            project("g3", "g3")
            step_ef(3, 0)
            step_ef(3, 1)
            project("k0", "k0")
            project("k1", "k1")
            project("alr", "alr")
            pe.wait_ge(alr_ready, 1)
            pe.wait_ge(wa2_in, 16)
            logits(0)
            logits(1)
            values()
            for m in range(4):
                n, t = STREAM["glu0"] + m // 2, ACC[f"glu{m}"]
                pe.wait_ge(w_ready, n + 1)
                claim(t)
                product(t, lambda k: n % SLOTS, lambda k: (m % 2) * 512 + k * P, XOPS, nk=4,
                        xn=SPLIT["z"] if m == 0 else None)
                if m % 2:
                    held[0] += 1
            read_wait(pe, "glu2")
            read_wait(pe, "glu3")
            vs = V[0:32, NGC, :]

            def gla_front(it):
                p, c, b = it // NGC, it % NGC, it % 2
                pe.wait_ge(pair_ready, p + 1)
                if it == 0:
                    pe.wait_ge(ms_read, len(MS))
                if it >= 2:
                    pe.wait_ge(kt_ready, it - 1)
                pe.transpose(ms[:, b, 0:P], EE[p][:, c * GC:(c + 1) * GC], ident).then_inc(kt_done, 1)
                pe.wait_ge(kx_ready, it + 1)
                if it >= 2:
                    pe.wait_ge(sc_ready, it - 1)
                for i in range(NBL):
                    at = (c * NBL + i) * 2 * BL
                    last = pe.matmul(glb[:, b, i * 2 * BL:(i + 1) * 2 * BL], KX[:, b, i * GC:(i + 1) * GC],
                                     QM[p][:, at:at + 2 * BL], start=True, stop=True)
                last.then_inc(sc_done, 1)

            def gla_back(it):
                p, c, b = it // NGC, it % NGC, it % 2
                pe.wait_ge(sc_ready, it + 1)
                if it >= 2:
                    pe.wait_ge(o_read, it - 1)
                if c:
                    pe.wait_ge(s_ready, it)
                    pe.matmul(glb[:, 2 + b, 0:2 * GC], S[:, p, :], QI[p][:, c * 2 * GC:(c + 1) * 2 * GC],
                              start=True, stop=False)
                for e in range(2):
                    h = 2 * p + e
                    last = pe.matmul(glb[:, 2 + b, e * GC:(e + 1) * GC], V[:, c, h * P:(h + 1) * P],
                                     SC[:, b, e * GC:(e + 1) * GC], start=(c == 0), stop=(c == 0 or e == 1))
                last.then_inc(o_done, 1)
                pe.wait_ge(kt_ready, it + 1)
                if it:
                    pe.wait_ge(s_ready, it)
                for e in range(2):
                    h = 2 * p + e
                    last = pe.matmul(glb[64 * e:64 * e + 64, 5, 0:P], KTR[:, b, 64 * e:64 * e + 64],
                                     V[:, c, h * P:(h + 1) * P], start=True, stop=True)
                last.then_inc(kv_done, 1)

            def gla_sample(p):
                pe.wait_ge(sc_ready, 2 * NGC)
                if p:
                    pe.wait_ge(sst_ready, NB)
                pe.transpose(glb[0:32, 4, 0:P], EE[p][:, SEQ:T], ident).then_inc(sm_done, 1)
                qs = QM[p][:, 2 * SEQ:2 * T]
                pe.matmul(glb[0:32, 0, 0:64], KN[p][:, SEQ:T], qs, start=True, stop=True).then_inc(sm_done, 1)
                pe.wait_ge(smc_ready, p + 1)
                pe.wait_ge(ss_in[p], 16)
                pe.wait_ge(o_read, 2 * NGC)
                if p:
                    pe.wait_ge(so_read, 1)
                for e in range(2):
                    h = 2 * p + e
                    pe.matmul(glb[:, 2, e * 32:(e + 1) * 32], vs[:, h * P:(h + 1) * P], SC[0:32, 0, e * 32:(e + 1) * 32],
                              start=(e == 0), stop=False, skip_group_check=True)
                two = glb[:, 2, 0:64].rearrange("p (e n) -> p e n", e=2)
                qs2 = qs.rearrange("p (e n) -> p e n", e=2)
                for s in range(NB):
                    last = pe.matmul(two[:, :, s * NS:(s + 1) * NS], SS[p][:, s, :], qs2[:, :, s * NS:(s + 1) * NS],
                                     start=False, stop=(s == NB - 1), skip_group_check=True)
                last.then_inc(so_done, 1)
                pe.wait_ge(smk_ready, p + 1)
                pe.wait_ge(s_ready, 2 * NGC)
                kts = KX[0:32, :, :].rearrange("p a n -> p (a n)")
                for s in range(NB):
                    for e in range(2):
                        h = 2 * p + e
                        last = pe.matmul(glb[64 * e:64 * e + 64, 5 if s < 4 else 1, (s % 4) * P:(s % 4 + 1) * P],
                                         kts[:, s * P + 64 * e:s * P + 64 * e + 64], vs[:, h * P:(h + 1) * P],
                                         start=True, stop=True)
                last.then_inc(skv_done, 1)

            gla_front(0)
            for it in range(2 * NGC):
                if it + 1 < 2 * NGC:
                    gla_front(it + 1)
                gla_back(it)
            gla_sample(0)
            gla_sample(1)
            pe.wait_ge(sst_ready, 2 * NB)
            pe.wait_ge(so_read, 2)
            for h in range(4):
                t = ACC[f"head{h}"]
                pe.wait_ge(sq_done, NCH * KT + h + 1)
                claim(t)
                for c in range(NCH):
                    last = mm(acc[:, t % 2, c, 0:CH], ones[:, :], TT[:, h % 2, cols_of(c)], True, True)
                last.then_inc(acc_done[t % 2], 1)
            for m in range(KT):
                project(f"oute{m}", f"oute{m}", xn=SPLIT["o"] if m == 0 else None, ks=(4, 5, 6, 7, 0, 1, 2, 3))

            def mlp(layer, r):
                norm(r)
                w0, t0, xn = STREAM[f"mlp{layer}_0"], ACC[f"mlp{layer}_0"], SPLIT[f"norm{r}"]
                h0 = FT * layer

                def up(base_w, base_t, per):
                    for j in range(2):
                        n, t = base_w + j, base_t + j
                        pe.wait_ge(w_ready, per(4) + (n + 1))
                        pe.wait_ge(acc_read[t % 2], per(5) + t // 2)
                        product(t, lambda k: n % SLOTS, lambda k: k * P, XOPS)
                        held[0] += 1

                def down(hready, half, base_w, base_t, per):
                    pe.wait_ge(w_ready, per(4) + (base_w + 2))
                    pe.wait_ge(h_ready, hready)
                    ops = (lambda k: HH[:, 2 * half + k, :], lambda k: HL[:, 2 * half + k, :])
                    for m in range(KT):
                        t = base_t + m
                        pe.wait_ge(acc_read[t % 2], per(5) + t // 2)
                        product(t, lambda k: (base_w + k) % SLOTS, lambda k: m * P, ops, nk=2,
                                last_w=(m == KT - 1))
                    held[0] += 1

                project_pair((f"mlp{layer}_0", f"mlp{layer}_1"), (f"mlp{layer}_0", f"mlp{layer}_1"), xn)
                with pe.Fori(0, HG // 2 - 1) as i:
                    for j in range(2):
                        per = lambda x: i * (2 * x)
                        up(w0 + 2 + 4 * j, t0 + 2 + 10 * j, per)
                        down(i * 4 + (h0 + 2 * j + 2), j, w0 + 4 + 4 * j, t0 + 4 + 10 * j, per)
                a = HG - 2
                flat = lambda x: 0
                up(w0 + 2 + 4 * a, t0 + 2 + 10 * a, flat)
                down(h0 + 2 * a + 2, 0, w0 + 4 + 4 * a, t0 + 4 + 10 * a, flat)
                down(h0 + 2 * a + 4, 1, w0 + 6 + 4 * a, t0 + 12 + 10 * a, flat)

            mlp(0, 1)
            norm(2)

            def gates(n):
                pe.wait_ge(conv_done, n + 1)
                pe.wait_ge(wri_in[n % 2], 16 * (n // 2 + 1))
                for r, name in enumerate(("r", "i")):
                    t = ACC[f"{name}{n}"]
                    claim(t)
                    for c in range(NCH):
                        last = mm(acc[:, t % 2, c, 0:CH], WRI[:, n % 2, r, :], HB[:, n, c * CH:(c + 1) * CH], True, True)
                    last.then_inc(acc_done[t % 2], 1)

            project_pair(("xb0", "xb1"), ("xb0", "xb1"), SPLIT["norm2"])
            for n in range(KT):
                gates(n)
                if n + 2 < KT:
                    project(f"xb{n + 2}", f"xb{n + 2}")
                else:
                    project(f"gate{n + 2 - KT}", f"gate{n + 2 - KT}")
            for n in range(2, KT):
                project(f"gate{n}", f"gate{n}")
            for m in range(KT):
                project(f"outo{m}", f"outo{m}", xn=SPLIT["mix"] if m == 0 else None)
            mlp(1, 3)
            norm(4)

        def last_down(layer, k):
            return f"mlp{layer}_{2 * HG + KT * (HG - 1) + k}"

        X_FROM = [None, lambda k: f"oute{k}", lambda k: last_down(0, k), lambda k: f"outo{k}", lambda k: last_down(1, k)]
        G_NORM = ["g_mix_even", "g_mlp0", "g_mix_odd", "g_mlp1", "g_final"]

        def sq_base(r):
            return NCH * KT + 4 + SSQ_N * (r - 1)

        @block.scalar
        def _(act):
            def norm(r):
                t = ACC[f"norm{r}"]

                def first_square(c, k):
                    n = c * KT + k
                    act.wait_ge(x_in[c], 16)
                    if n >= NCH:
                        act.wait_ge(sq_used, n - NCH + 1)
                    act.activation(TT[:, 2, cols_of(n % NCH)], X0[:, k, cols_of(c)], ACT.Square).then_inc(sq_done, 1)

                def log(c):
                    if c == NCH - 1:
                        done_wait(act, f"norm{r}")
                    elif r == 0:
                        act.wait_ge(sq_used, KT * (c + 1))
                    else:
                        act.wait_ge(norm_sum, (NCH - 1) * (r - 1) + c + 1)
                    ins = act.activation(TT[:, 3, cols_of(c)], acc[:, t % 2, c, 0:CH], ACT.Ln, bias=few[:, 0:1],
                                         scale=1.0 / D)
                    ins.then_inc(ln_done if c < NCH - 1 else acc_read[t % 2], 1)

                def root(c):
                    if c < NCH - 1:
                        act.wait_ge(ln_done, (NCH - 1) * r + c + 1)
                    else:
                        read_wait(act, f"norm{r}")
                    act.activation(TT[:, 3, cols_of(c)], TT[:, 3, cols_of(c)], ACT.Exp, scale=-0.5).then_inc(rs_done, 1)

                if r == 0:
                    for k in range(KT):
                        first_square(0, k)
                else:
                    for k in range(KT - 1):
                        read_wait(act, X_FROM[r](k))
                        if k >= 2:
                            act.wait_ge(ssq_add, SSQ_N * (r - 1) + k - 1)
                        act.activation(TT[:, k % 2, :], X[:, k, :], ACT.Square).then_inc(sq_done, 1)
                    act.wait_ge(ssq_add, SSQ_N * (r - 1) + KT - 2)
                    for c in range(NCH):
                        if c < NCH - 1:
                            act.wait_ge(res_part, (NCH - 1) * (r - 1) + c + 1)
                        else:
                            read_wait(act, X_FROM[r](KT - 1))
                        act.activation(TT[:, (KT - 1) % 2, cols_of(c)], X[:, KT - 1, cols_of(c)], ACT.Square)\
                           .then_inc(sq_done, 1)
                if r == 0:
                    log(0)
                    root(0)
                else:
                    for c in range(NCH):
                        log(c)
                    for c in range(NCH):
                        root(c)
                for c in range(NCH if r < 4 else 0):
                    for k in range(KT):
                        act.wait_ge(xn_done, (NCH * r + c) * KT + k + 1)
                        act.activation(XH[:, k, cols_of(c)], TT[:, k % 2, cols_of(c)], ACT.Copy).then_inc(xh_done, 1)
                        if r == 0 and c + 1 < NCH:
                            first_square(c + 1, k)
                    if r == 0 and c + 1 < NCH:
                        log(c + 1)
                        root(c + 1)

            def read_ms(step, out, src):
                act.wait_ge(ms_done, MS[step] + 1)
                act.activation(out, src, ACT.Copy).then_inc(ms_read, 1)

            def read_a(q):
                read_ms(f"a{q}", WIN[:, :, :, :].rearrange("p r g n -> p r (g n)"), ms[:, :, :])

            def read_b(q):
                if q:
                    act.wait_ge(m_in, 16 * L * q)
                read_ms(f"b{q}", T7[:, :], ms[:, 0, 0:P])

            def read_cd(q, r):
                if r == 0 and q >= 2:
                    act.wait_ge(z_done, q - 1)
                read_ms(("c", "d")[r] + str(q), VV(q)[:, r, :, :].rearrange("p (b g) n -> p b (g n)", b=2),
                        ms[:, :, 0:2 * YW])

            def read_ef(q, half):
                if q and half == 0:
                    act.wait_ge(y_out, 16 * q)
                read_ms(("e", "f")[half] + str(q),
                        G[:, half * 4 * YW:(half + 1) * 4 * YW].rearrange("p (q e n) -> p e q n", q=2, e=2),
                        ms[:, :, 0:2 * YW].rearrange("p e (q n) -> p e q n", q=2))

            def read_u(q):
                t = ACC[f"u{q}"]
                done_wait(act, f"u{q}")
                if q:
                    act.wait_ge(u_out, 16 * q)
                for c in range(NCH):
                    n = min(CH, SEQ - c * CH) // L
                    at = NB + c * (CH // L)
                    act.activation(UR[:, :, at:at + n].rearrange("p l n -> p n l"),
                                   acc[:, t % 2, c, 0:n * L].rearrange("p (n l) -> p n l", l=L), ACT.Copy)
                tail = acc[:, t % 2, 2, CH - NB * NS:CH].rearrange("p (n s) -> p n s", s=NS)
                act.activation(UR[:, 0:NS, 0:NB].rearrange("p l n -> p n l"), tail, ACT.Copy)
                act.activation(UR[:, L - NS:L, NB + NC:CW].rearrange("p l n -> p n l"), tail, ACT.Copy)\
                   .then_inc(acc_read[t % 2], 1)

            def read_plain(name, out, func=ACT.Copy, **more):
                t = ACC[name]
                done_wait(act, name)
                act.activation(cut(out), bank(t), func, **more).then_inc(acc_read[t % 2], 1)

            def gelu(q):
                act.wait_ge(zin_done, q + 1)
                if q:
                    act.wait_ge(z_out, 16 * q)
                act.activation(TT[:, 2, 0:SEQ].rearrange("p (n l) -> p l n", l=L), YR(q)[:, :, NB:YW], ACT.Gelu_apprx_tanh)
                act.activation(TT[:, 2, SEQ:T].rearrange("p (n s) -> p s n", s=NS), YR(q)[:, 0:NS, 0:NB],
                               ACT.Gelu_apprx_tanh).then_inc(z_done, 1)

            def decay(p):
                if p:
                    act.wait_ge(lg_dve, 2)
                read_plain(f"lg{p}", TT[:, 0, :], ACT.Identity, bias=p_col("b_a2", p))
                act.wait_ge(lg_dve, 2 * p + 1)
                act.activation(TT[:, 2, :], TT[:, 2, :], ACT.Exp).then_inc(act_step, 1)
                act.wait_ge(act_step, p + 1)
                act.activation(TT[:, 2, :], TT[:, 2, :], ACT.Ln, bias=1.0).then_inc(lg_act, 1)

            def read_g(h):
                if h >= 2:
                    act.wait_ge(g_out[h % 2], 16)
                read_plain(f"g{h}", TT[:, h % 2, :], ACT.Silu)
                read_wait(act, f"g{h}")
                act.dma_start(g_scr[h], TT[:, h % 2, :]).then_inc(g_out[h % 2], 16)

            act.wait_ge(const_ready, 1)
            norm(0)
            act.wait_ge(par5_in, 16)
            act.activation(sm[:, 0, :], p5c("log_dt"), ACT.Exp).then_inc(prep_act, 1)
            act.wait_ge(prep_dve, 1)
            act.activation(sm[:, 3, :], sm[:, 2, :], ACT.Exp)
            act.activation(sm[:, 4, :], sm[:, 2, :], ACT.Exp, scale=float(L)).then_inc(prep_act, 1)
            act.wait_ge(prep_dve, 2)
            act.activation(rot[:, 1, :], sm[:, 6, :], ACT.Sin)
            act.activation(rot[:, 0, :], sm[:, 7, :], ACT.Sin, bias=few[:, 1:2]).then_inc(prep_act, 1)

            def turn_table(n):
                table = (PT0, PTR)[n]
                act.wait_ge(angle_ready, n + 1)
                act.activation(table[:, 1, :, :], table[:, 1, :, :], ACT.Sin)
                act.activation(table[:, 0, :, :], table[:, 0, :, :], ACT.Sin, bias=few[:, 1:2]).then_inc(pt_ready, 1)

            act.wait_ge(ur_ready, 1)
            for q in range(NG):
                read_u(q)
            read_a(0)
            read_b(0)
            turn_table(0)
            read_plain("q0", Q[:, 0, :])
            read_cd(0, 0)
            read_cd(0, 1)
            read_a(1)
            read_b(1)
            read_plain("q1", Q[:, 1, :])
            read_cd(1, 0)
            read_cd(1, 1)
            turn_table(1)
            read_ef(0, 0)
            read_ef(0, 1)
            read_g(0)
            read_a(2)
            read_b(2)
            gelu(0)
            read_ef(1, 0)
            read_ef(1, 1)
            read_cd(2, 0)
            read_cd(2, 1)
            read_g(1)
            read_a(3)
            read_b(3)
            gelu(1)
            read_ef(2, 0)
            read_ef(2, 1)
            read_g(2)
            read_cd(3, 0)
            read_cd(3, 1)
            read_g(3)
            gelu(2)
            read_ef(3, 0)
            read_ef(3, 1)
            act.wait_ge(st_ready, NG)
            read_plain("k0", K[:, 0, :])
            gelu(3)
            read_plain("k1", K[:, 1, :])
            t = ACC["alr"]
            done_wait(act, "alr")
            act.activation(cut(ALR), acc[0:16, t % 2, :, 0:CH], ACT.Copy).then_inc(acc_read[t % 2], 1)
            read_wait(act, "alr")
            act.nop().then_inc(alr_ready, 1)
            act.wait_ge(g_out[0], 32)
            decay(0)
            decay(1)
            def pair_decays(p):
                act.wait_ge(pair_sums, 2 * p + 1)
                act.activation(EX[p], LA[:, p, :], ACT.Exp).then_inc(pair_exps, 1)
                act.activation(EI[p], LA[:, p, :], ACT.Exp, scale=-1.0)
                act.activation(gs[p][:, 2:5, :], gs[p][:, 2:5, :], ACT.Exp)
                act.activation(GB[p][:, :, :, :], GB[p][:, :, :, :], ACT.Exp).then_inc(pair_exps, 1)

            def pair_rest(p):
                act.wait_ge(pair_sums, 2 * p + 2)
                act.activation(EX[p], EX[p], ACT.Exp).then_inc(pair_exps, 1)

            act.wait_ge(z_done, NG)
            for j in range(3):
                if j == 1:
                    pair_decays(0)
                if j == 2:
                    pair_rest(0)
                t = ACC[f"v{j}"]
                done_wait(act, f"v{j}")
                if j < 2:
                    act.activation(V[:, 3 * j:3 * j + 3, :], acc[:, t % 2, :, :], ACT.Copy).then_inc(acc_read[t % 2], 1)
                else:
                    act.activation(V[:, 6:8, :], acc[:, t % 2, 0:2, :], ACT.Copy)
                    act.activation(V[0:32, NGC, :], acc[96:P, t % 2, 2, :], ACT.Copy).then_inc(acc_read[t % 2], 1)
            for k in range(4):
                act.wait_ge(z_in[k % 2], 16 * (k // 2 + 1))
                act.activation(XH[:, k, :], TT[:, k % 2, :], ACT.Copy).then_inc(xh_done, 1)
            for m in range(4):
                act.wait_ge(xl_done, SPLIT["z"] + 4 if m < 2 else SPLIT["zg"] + m - 1)
                read_plain(f"glu{m}", TT[:, 2 + m % 2, :], ACT.Sigmoid, bias=p_col("b_glu", m))
                act.wait_ge(gg_done, m + 1)
                act.activation(XH[:, 4 + m, :], TT[:, 2 + m % 2, :], ACT.Copy).then_inc(xh_done, 1)

            def head_square(h):
                if h >= 2:
                    act.wait_ge(gg_done, 4 + h - 1)
                act.activation(TT[:, h % 2, :], (Q, K)[h % 2][:, h // 2, :], ACT.Square).then_inc(sq_done, 1)

            def read_kt(it):
                act.wait_ge(kt_done, it + 1)
                if it >= 2:
                    act.wait_ge(kv_done, it - 1)
                act.activation(KTR[:, it % 2, :], ms[:, it % 2, 0:P], ACT.Copy).then_inc(kt_ready, 1)

            read_kt(0)
            for it in range(2 * NGC):
                p, c, b = it // NGC, it % NGC, it % 2
                if it + 1 < 2 * NGC:
                    read_kt(it + 1)
                act.wait_ge(o_done, it + 1)
                act.activation(Q[:, p, c * GC:(c + 1) * GC], glb[:, 2 + b, 0:GC], ACT.Copy)
                act.activation(K[:, p, c * GC:(c + 1) * GC], glb[:, 2 + b, GC:2 * GC], ACT.Copy).then_inc(o_read, 1)
                if it == 1:
                    pair_decays(1)
                if it == 3:
                    pair_rest(1)
            for p in range(2):
                act.wait_ge(so_done, p + 1)
                act.activation(Q[:, p, SEQ:T], glb[:, 2, 0:32], ACT.Copy)
                act.activation(K[:, p, SEQ:T], glb[:, 2, 32:64], ACT.Copy).then_inc(so_read, 1)
                if p == 0:
                    act.wait_ge(so_read, 1)
                    for h in (0, 1):
                        head_square(h)
            act.wait_ge(so_read, 2)
            act.wait_ge(sst_ready, 2 * NB)
            def head_hi(h):
                act.wait_ge(gg_done, 4 + h + 1)
                act.activation(XH[:, h, :], (Q, K)[h % 2][:, h // 2, :], ACT.Copy).then_inc(xh_done, 1)

            for first in (0, 2):
                for h in (first, first + 1):
                    t = ACC[f"head{h}"]
                    done_wait(act, f"head{h}")
                    act.activation(cut(TT[:, h % 2, :]), bank(t), ACT.Ln, bias=few[:, 0:1], scale=1.0 / P)\
                       .then_inc(acc_read[t % 2], 1)
                for h in (first, first + 1):
                    read_wait(act, f"head{h}")
                    act.activation(TT[:, h % 2, :], TT[:, h % 2, :], ACT.Exp, scale=-0.5).then_inc(head_rs, 1)
                if first == 0:
                    for h in (2, 3):
                        head_square(h)
                        head_hi(h - 2)
            head_hi(2)
            head_hi(3)

            def mlp_hidden(base_t, per5, hcount, u, first):
                t = base_t
                act.wait_ge(acc_done[t % 2], per5 + (t // 2 + 1))
                if not first:
                    act.wait_ge(h_ready, hcount - 1)
                act.activation(cut(TT[:, u % 2, :]), bank(t), ACT.Relu).then_inc(acc_read[t % 2], 1)
                act.wait_ge(acc_read[t % 2], per5 + (t // 2 + 1))
                act.activation(TT[:, 2 + u % 2, :], TT[:, u % 2, :], ACT.Square).then_inc(h_sq, 1)

            def mlp(layer):
                t0, h0 = ACC[f"mlp{layer}_0"], FT * layer
                for j in range(2):
                    mlp_hidden(t0 + j, 0, None, j, True)
                with act.Fori(0, HG // 2 - 1) as i:
                    for a in range(2):
                        for j in range(2):
                            mlp_hidden(t0 + 2 + 10 * a + j, i * 10, i * 4 + (h0 + 2 * (a + 1) + j), j, False)
                a = HG - 2
                for j in range(2):
                    mlp_hidden(t0 + 2 + 10 * a + j, 0, h0 + 2 * (a + 1) + j, j, False)
                act.wait_ge(h_ready, h0 + FT)

            norm(1)
            mlp(0)
            norm(2)
            act.wait_ge(lam_dve, 1)
            act.activation(spt[:, :], spt[:, :], ACT.Exp).then_inc(act_step, 1)
            act.wait_ge(act_step, 3)
            act.activation(spt[:, :], spt[:, :], ACT.Ln, bias=1.0).then_inc(lam_act, 1)

            def load_ri(n):
                act.dma_start(WRI[:, n % 2, :, :], w_ri[n]).then_inc(wri_in[n % 2], 16)

            def read_xb(n):
                t = ACC[f"xb{n}"]
                done_wait(act, f"xb{n}")
                if n >= 2:
                    act.wait_ge(conv_done, n - 1)
                act.activation(XP[:, n % 2, 3:3 + 2 * CH].rearrange("p (c n) -> p c n", n=CH),
                               acc[:, t % 2, 0:2, 0:CH], ACT.Copy)
                act.activation(XP[:, n % 2, 3 + 2 * CH:3 + SEQ], acc[:, t % 2, 2, 0:SEQ - 2 * CH], ACT.Copy)
                smp = XP[:, n % 2, 3 + SEQ:].rearrange("p (b s) -> p b s", b=NB)
                act.activation(smp[:, :, 0:3], st_conv[:, n, :, :], ACT.Copy)
                act.activation(smp[:, :, 3:7], acc[:, t % 2, 2, SEQ - 2 * CH:CH].rearrange("p (b s) -> p b s", b=NB),
                               ACT.Copy).then_inc(acc_read[t % 2], 1)

            def gates(n):
                if n:
                    act.wait_ge(states_done, n)
                if n == KT - 1:
                    act.wait_ge(hb_ready, 1)
                read_plain(f"r{n}", TT[:, 0, :], ACT.Sigmoid, bias=p_col("b_r", n))
                read_plain(f"i{n}", TT[:, 1, :], ACT.Sigmoid, bias=p_col("b_i", n))
                read_wait(act, f"r{n}")
                act.activation(TT[:, 3, :], TT[:, 0, :], ACT.Tanh, scale=sp4[:, n:n + 1]).then_inc(gates_done, 1)
                act.activation(TT[:, 2, :], TT[:, 0, :], ACT.Exp, scale=sp8[:, n:n + 1]).then_inc(gates_done, 1)
                act.wait_ge(gates_done, 3 * n + 1)
                act.activation(TT[:, 3, :], TT[:, 3, :], ACT.Sqrt).then_inc(gates_done, 1)

            act.wait_ge(xl_done, SPLIT["norm2"] + NCH * KT)
            act.dma_start(st_lru[:, :, :], odd_lru).then_inc(odd_in, 16)
            act.dma_start(st_conv[:, :, :, :], odd_conv).then_inc(odd_in, 16)
            load_ri(0)
            load_ri(1)
            act.wait_ge(odd_in, 32)
            act.wait_ge(xp_ready, 1)
            read_xb(0)
            read_xb(1)
            act.wait_ge(lam_dve, 2)
            for n in range(KT):
                gates(n)
                if n + 2 < KT:
                    load_ri(n + 2)
                    read_xb(n + 2)
                if n >= KT - 2:
                    m = n + 2 - KT
                    act.wait_ge(states_done, n + 1)
                    read_plain(f"gate{m}", TT[:, m % 2, :], ACT.Gelu_apprx_tanh)
            for m in range(2, KT):
                act.wait_ge(hb_ready, m - 1)
                read_plain(f"gate{m}", TT[:, m % 2, :], ACT.Gelu_apprx_tanh)
            done_wait(act, f"gate{KT - 1}")
            act.dma_start(lru_out, LN[:, :, :]).then_inc(small_out, 16)
            act.dma_start(conv_out, CN[:, :, :]).then_inc(small_out, 16)
            act.dma_start(s5_out, SO[:, :, :, :]).then_inc(small_out, 16)
            for k in range(KT):
                act.wait_ge(hb_ready, k + 1)
                act.activation(XH[:, k, :], HB[:, k, :], ACT.Copy).then_inc(xh_done, 1)
            norm(3)
            mlp(1)
            norm(4)

        @block.vector
        def _(dve):
            step = Chain(dve, dve_step)
            link = step.link

            def tt(out, a, b, op):
                return dve.tensor_tensor(out, a, b, op)

            def stt(out, a, scalar, b, op0, op1):
                return dve.scalar_tensor_tensor(out=out, in0=a, scalar=scalar, in1=b, op0=op0, op1=op1)

            def lo_part(dst, src, hi, want):
                dve.wait_ge(xh_done, want)
                tt(dst, src, hi.bitcast(F32), ALU.subtract).then_inc(xl_done, 1)

            def add_square(r, k):
                dve.wait_ge(sq_done, sq_base(r) + k + 1)
                if k == 0:
                    dve.tensor_copy(TT[:, 2, :], TT[:, 0, :]).then_inc(ssq_add, 1)
                else:
                    dve.wait_ge(ssq_add, SSQ_N * (r - 1) + k)
                    tt(TT[:, 2, :], TT[:, 2, :], TT[:, k % 2, :], ALU.add).then_inc(ssq_add, 1)

            def norm(r):
                xs, at = (X0 if r == 0 else X), SPLIT.get(f"norm{r}")
                if r == 0:
                    dve.wait_ge(par_in, 16)
                else:
                    dve.wait_ge(ssq_add, SSQ_N * (r - 1) + KT - 1)
                    for c in range(NCH):
                        dve.wait_ge(sq_done, sq_base(r) + KT + c)
                        tt(TT[:, 2, cols_of(c)], TT[:, 2, cols_of(c)], TT[:, (KT - 1) % 2, cols_of(c)], ALU.add)\
                            .then_inc(ssq_add, 1)

                def lo(n):
                    c, k = n // KT, n % KT
                    dve.wait_ge(xn_done, NCH * KT * r + n + 1)
                    lo_part(XL[:, k, cols_of(c)], TT[:, k % 2, cols_of(c)], XH[:, k, cols_of(c)], at + n + 1)

                for n in range(NCH * KT):
                    c, k = n // KT, n % KT
                    if k == 0:
                        dve.wait_ge(rs_done, NCH * r + c + 1)
                    g = p_col(G_NORM[r], k)
                    if r == 4:
                        stt(X[:, k, cols_of(c)], X[:, k, cols_of(c)], g, TT[:, 3, cols_of(c)], ALU.mult, ALU.mult)\
                            .then_inc(xn_done, 1)
                        continue
                    if n >= 2:
                        dve.wait_ge(xl_done, at + n - 1)
                    stt(TT[:, k % 2, cols_of(c)], xs[:, k, cols_of(c)], g, TT[:, 3, cols_of(c)], ALU.mult, ALU.mult)\
                        .then_inc(xn_done, 1)
                    if n:
                        lo(n - 1)
                if r < 4:
                    lo(NCH * KT - 1)

            def cmul(out, a, b, t, neg=False):
                link(tt(t[0], a[0], b[0], ALU.mult))
                link(tt(t[1], a[1], b[1], ALU.mult))
                tt(out[0], t[0], t[1], ALU.subtract).then_inc(dve_step, 1)
                step.n += 1
                step.wait()
                link(tt(t[0], a[0], b[1], ALU.mult))
                link(tt(t[1], a[1], b[0], ALU.mult))
                if neg:
                    return stt(out[1], t[0], -1.0, t[1], ALU.mult, ALU.subtract)
                return tt(out[1], t[0], t[1], ALU.add)

            dve.memset(ones[:, :], 1.0)
            dve.memset(few[:, 0:1], EPS)
            for i, x in enumerate((0.15915494309189535, MAGIC, TWO_PI_1, TWO_PI_2, TWO_PI_3)):
                dve.memset(few[:, 2 + i:3 + i], x)
            dve.memset(few[:, 1:2], 1.5707963267948966).then_inc(const_ready, 1)
            dve.memset(UR[:, :, :], 0.0).then_inc(ur_ready, 1)
            dve.memset(M[:, :, :, :], 0.0)
            link(dve.memset(CB[:, :, :, :], 0.0))
            norm(0)

            link(dve.memset(pw[:, :, 0, :], 0.0))
            link(dve.memset(pw[:, 0, 0, :], 1.0))
            dve.wait_ge(par5_in, 16)
            cb = [p5c(n).rearrange("p (g c) -> p g c", c=16) for n in ("c_re", "c_im")]
            bb = [p5c(n).rearrange("p (g c) -> p g c", c=16) for n in ("b_re", "b_im")]
            for e in range(2):
                h = slice(64 * e, 64 * e + 64)
                dve.tensor_copy(CB[h, 0, :, 16 * e:16 * e + 16], cb[0][h])
                link(dve.tensor_scalar(CB[h, 1, :, 16 * e:16 * e + 16], cb[1][h], -1.0, None, ALU.mult))
            dve.wait_ge(prep_act, 1)
            are, aim = p5c("a_re"), p5c("a_im")
            link(tt(sm[:, 1, :], sm[:, 0, :], aim, ALU.mult))
            tt(sm[:, 2, :], sm[:, 0, :], are, ALU.mult).then_inc(prep_dve, 1)

            def reduce(x, t, near=None):
                link(dve.tensor_scalar(t, x if near is None else near, 0.15915494309189535, MAGIC, ALU.mult, ALU.add))
                link(dve.tensor_scalar(t, t, MAGIC, None, ALU.subtract))
                for part in (TWO_PI_1, TWO_PI_2, TWO_PI_3):
                    link(stt(x, t, -part, x, ALU.mult, ALU.add))

            def clamp(x):
                return dve.tensor_scalar(x, x, 3.1415925, -3.1415925, ALU.min, ALU.max)

            link(dve.tensor_scalar(sm[:, 12, :], sm[:, 1, :], float(L), None, ALU.mult))
            link(dve.tensor_copy(sm[:, 6, :], sm[:, 1, :]))
            reduce(sm[:, 6, :], sm[:, 5, :])
            link(clamp(sm[:, 6, :]))
            stt(sm[:, 7, :], sm[:, 6, :], -1.0, sm[:, 6, :], ALU.mult, ALU.min).then_inc(prep_dve, 1)
            reduce(sm[:, 12, :], sm[:, 5, :])
            link(dve.tensor_scalar(sm[:, 11, :], sm[:, 12, :], CUT12, None, ALU.add))
            link(dve.tensor_scalar(sm[:, 11, :], sm[:, 11, :], CUT12, None, ALU.subtract))
            tt(sm[:, 13, :], sm[:, 12, :], sm[:, 11, :], ALU.subtract).then_inc(phi_ready, 1)
            dve.wait_ge(phi_ready, 1)
            dve.wait_ge(prep_act, 3)
            sc2 = (sm[:, 8, :], sm[:, 9, :])
            a1 = (pw[:, 0, 1, :], pw[:, 1, 1, :])
            link(tt(a1[0], sm[:, 3, :], rot[:, 0, :], ALU.mult))
            link(tt(a1[1], sm[:, 3, :], rot[:, 1, :], ALU.mult))
            for n in (1, 2, 4):
                t = [TT[:, 3, 64 * r:64 * r + 16 * n].rearrange("p (k g) -> p k g", g=16) for r in range(2)]
                link(cmul([pw[:, r, n + 1:2 * n + 1, :] for r in range(2)], [pw[:, r, 1:n + 1, :] for r in range(2)],
                          [pw[:, r, n, :].unsqueeze(1).broadcast_to([P, n, 16]) for r in range(2)], t))
            link(dve.tensor_scalar(sm[:, 5, :], a1[0], 1.0, None, ALU.subtract))
            link(tt(sm[:, 8, :], are, are, ALU.mult))
            link(tt(sm[:, 9, :], aim, aim, ALU.mult))
            link(tt(sm[:, 8, :], sm[:, 8, :], sm[:, 9, :], ALU.add))
            link(dve.reciprocal(sm[:, 10, :], sm[:, 8, :]))
            link(tt(sm[:, 8, :], sm[:, 5, :], are, ALU.mult))
            link(tt(sm[:, 9, :], a1[1], aim, ALU.mult))
            link(tt(sm[:, 8, :], sm[:, 8, :], sm[:, 9, :], ALU.add))
            link(tt(sm[:, 6, :], sm[:, 8, :], sm[:, 10, :], ALU.mult))
            link(tt(sm[:, 8, :], a1[1], are, ALU.mult))
            link(tt(sm[:, 9, :], sm[:, 5, :], aim, ALU.mult))
            link(tt(sm[:, 8, :], sm[:, 8, :], sm[:, 9, :], ALU.subtract))
            link(tt(sm[:, 7, :], sm[:, 8, :], sm[:, 10, :], ALU.mult))

            def over(ap, shape):
                return ap.broadcast_to(shape)

            g16 = [P, 16, 16]
            coef = [over(sm[:, 6 + r, :].unsqueeze(2), g16) for r in range(2)]
            tq = [TT[:, 3, 256 * n:256 * (n + 1)].rearrange("p (g c) -> p g c", c=16) for n in range(4)]
            link(tt(tq[0], coef[0], bb[0], ALU.mult))
            link(tt(tq[1], coef[1], bb[1], ALU.mult))
            link(tt(tq[2], coef[0], bb[1], ALU.mult))
            link(tt(tq[3], coef[1], bb[0], ALU.mult))
            link(tt(bb[0], tq[0], tq[1], ALU.subtract))
            link(tt(bb[1], tq[2], tq[3], ALU.add))

            shp = [P, PQ, L, 16]
            tx = [TT[:, 3, 512 * n:512 * (n + 1)].rearrange("p (g l c) -> p g l c", g=PQ, l=L) for n in range(2)]
            tn = [TT[:, 3, 512 * n:512 * (n + 1)].rearrange("p (g n) -> p g n", g=PQ) for n in range(2)]

            def power_rows(first, last, q):
                d = 1 if last > first else -1
                stop = last + d
                return [over(pw[:, r, first:(stop if stop >= 0 else None):d, PQ * q:PQ * (q + 1)]
                             .rearrange("p l g -> p g l").unsqueeze(3), shp) for r in range(2)]

            def build_xa(q):
                if q:
                    dve.wait_ge(ms_done, MS[f"b{q - 1}"] + 1)
                b = [over(bb[r][:, PQ * q:PQ * (q + 1), :].unsqueeze(2), shp) for r in range(2)]
                cmul((XA[:, 0], XA[:, 1]), power_rows(L - 1, 0, q), b, tx).then_inc(xa_ready, 1)
                dve.wait_ge(xa_ready, q + 1)

            def build_wo(q):
                if q:
                    dve.wait_ge(ms_done, MS[f"f{q - 1}"] + 1)
                c = [over(cb[r][:, PQ * q:PQ * (q + 1), :].unsqueeze(2), shp) for r in range(2)]
                cmul((WO[:, 0], WO[:, 1]), power_rows(1, L, q), c, tx, neg=True).then_inc(wo_ready, 1)
                dve.wait_ge(wo_ready, q + 1)

            def build_angles():
                shape = [P, PQ, NC]
                x = PT0[:, 1, :, :]
                t, rest = tn
                count = over(c_("count").unsqueeze(1), shape)
                link(tt(x, count, over(sm[:, 11, 0:PQ].unsqueeze(2), shape), ALU.mult))
                link(tt(rest, count, over(sm[:, 13, 0:PQ].unsqueeze(2), shape), ALU.mult))
                link(tt(t, x, rest, ALU.add))
                reduce(x, t, t)
                link(tt(x, x, rest, ALU.add))
                link(clamp(x))
                stt(PT0[:, 0, :, :], x, -1.0, x, ALU.mult, ALU.min).then_inc(angle_ready, 1)

            def finish_angles():
                dve.wait_ge(pool_angles, 13)
                x = PTR[:, 1, :, :]
                link(clamp(x))
                stt(PTR[:, 0, :, :], x, -1.0, x, ALU.mult, ALU.min).then_inc(angle_ready, 1)

            def core(q):
                dve.wait_ge(ms_read, MS[f"d{q}"] + 1)
                dve.wait_ge(pt_ready, 2 if q else 1)
                qs = slice(PQ * q, PQ * (q + 1))
                pr, pi = [(PTR[:, r, PQ * (q - 1):PQ * q, :] if q else PT0[:, r, :, :]) for r in range(2)]
                vv, gv, h = VV(q), GV(q), HV(q)
                vr, vi = vv[:, 0, :, 0:NC], vv[:, 1, :, 0:NC]
                gr, gi = gv[:, 0], gv[:, 1]
                t = tn
                link(tt(t[0], pr, vr, ALU.mult))
                link(tt(t[1], pi, vi, ALU.mult))
                link(tt(gr, t[0], t[1], ALU.add))
                link(tt(t[0], pr, vi, ALU.mult))
                link(tt(t[1], pi, vr, ALU.mult))
                link(tt(gi, t[0], t[1], ALU.subtract))
                h0 = [p5c(n).rearrange("p (g b) -> p g b", b=NB)[:, qs, :] for n in ("h0_re", "h0_im")]
                a4 = [over(pw[:, r, NS, qs].unsqueeze(2), [P, PQ, NB]) for r in range(2)]
                ts = [x[:, :, 0:NB] for x in t]
                so = [SO[:, r, qs, 1:1 + NB] for r in range(2)]
                link(cmul(so, a4, h0, ts))
                for r in range(2):
                    link(tt(so[r], so[r], vv[:, r, :, NC:YW], ALU.add))
                link(dve.tensor_copy(t[0], over(sm[:, 4, qs].unsqueeze(2), [P, PQ, NC])))
                link(dve.memset(t[0][:, :, 0:1], 0.0))
                flat = t[0].rearrange("p g n -> p (g n)")
                for r in range(2):
                    g = gv[:, r].rearrange("p g n -> p (g n)")
                    link(dve.tensor_tensor_scan(g, flat, g, 0.0, ALU.mult, ALU.add))
                hv = [h[:, r, :, NB + 1:NB + 1 + NC] for r in range(2)]
                link(cmul(hv, (gr, gi), (pr, pi), t))
                for r in range(2):
                    dve.memset(h[:, r, :, NB:NB + 1], 0.0)
                    link(dve.tensor_copy(h[:, r, :, 0:NB], h0[r]))
                    last = dve.tensor_copy(SO[:, r, qs, 0:1], h[:, r, :, NB + NC:NB + NC + 1])
                    last.then_inc(st_ready, 1) if r else link(last)

            def z_in_sum(q):
                dve.wait_ge(y_in, 16 * GQ * (q + 1))
                dve.wait_ge(ud_in, 16 * (q + 1))
                u = U[:, q % 2, :, :].rearrange("p g w -> p (g w)").rearrange("p (l w) -> p l w", l=L)
                stt(YR(q), u[:, :, 0:YW], p_col("s5_d", q), YR(q), ALU.mult, ALU.add).then_inc(zin_done, 1)

            def decay(p):
                read_wait(dve, f"lg{p}")
                if p:
                    dve.wait_ge(lg_dve, 2)
                link(dve.tensor_scalar(TT[:, 1, :], TT[:, 0, :], 0.0, None, ALU.min))
                stt(TT[:, 2, :], TT[:, 1, :], 2.0, TT[:, 0, :], ALU.mult, ALU.subtract).then_inc(lg_dve, 1)
                dve.wait_ge(lg_act, p + 1)
                link(dve.tensor_scalar(TT[:, 2, :], TT[:, 2, :], 1.0 / 16, None, ALU.mult))
                stt(LA[:, p, :], TT[:, 1, :], 1.0 / 16, TT[:, 2, :], ALU.mult, ALU.subtract).then_inc(lg_dve, 1)

            NBK = SEQ // BL
            g4 = [P, NGC, NBL, NBL]

            def by_block(x):
                return x[:, 0:SEQ].rearrange("p (b n) -> p b n", n=BL)

            def by_sequence(x):
                return x[:, SEQ:T].rearrange("p (b n) -> p b n", n=NS)

            def pair_blocks(p):
                C16, g = LA[:, p, :], gs[p]
                link(dve.memset(g[:, 5, :], 1.0))
                link(dve.memset(g[:, 5, :].rearrange("p (c i) -> p c i", i=NBL)[:, :, 0:1], 0.0))
                link(dve.tensor_copy(g[:, 0, :], C16[:, BL - 1:SEQ:BL]))
                link(dve.tensor_tensor_scan(g[:, 1, :], g[:, 5, :], g[:, 0, :], 0.0, ALU.mult, ALU.add))
                link(tt(g[:, 2, :], g[:, 1, :], g[:, 0, :], ALU.subtract))
                e3 = [g[:, n, :].rearrange("p (c i) -> p c i", i=NBL) for n in range(4)]
                link(tt(e3[3], over(e3[1][:, :, NBL - 1:NBL], [P, NGC, NBL]), e3[1], ALU.subtract))
                link(dve.memset(g[:, 4, :], 0.0))
                link(dve.tensor_copy(g[:, 4, 0:NGC], g[:, 1, NBL - 1:NBK:NBL]))
                link(dve.tensor_copy(g[:, 4, 8:8 + NB], C16[:, SEQ + NS - 1:T:NS]))
                link(dve.tensor_copy(g[:, 5, 0:NB], C16[:, SEQ + NS - 1:T:NS]))
                gb = GB[p][:, :, :, :]
                link(tt(gb, over(e3[2].unsqueeze(3), g4), over(e3[1].unsqueeze(2), g4), ALU.subtract))
                dve.tensor_scalar(gb, gb, 0.0, None, ALU.min).then_inc(pair_sums, 1)

            def pair_queries(p):
                dve.wait_ge(pair_exps, 3 * p + 1)
                qp = QM[p][:, 0:2 * SEQ].rearrange("p (b e n) -> p e b n", e=2, n=BL)
                qsm = QM[p][:, 2 * SEQ:2 * T].rearrange("p (e n) -> p e n", e=2)
                for e in range(2):
                    h = slice(64 * e, 64 * e + 64)
                    stt(qp[h, e], by_block(Q[h, p, :]), 0.125, by_block(EX[p][h]), ALU.mult, ALU.mult)
                    link(stt(qsm[h, e], Q[h, p, SEQ:T], 0.125, EX[p][h, SEQ:T], ALU.mult, ALU.mult))

            def pair_keys(p):
                C16 = LA[:, p, :]
                link(tt(by_block(EX[p]), over(gs[p][:, 0, :].unsqueeze(2), [P, NBK, BL]), by_block(C16), ALU.subtract))
                tt(by_sequence(EX[p]), over(gs[p][:, 5, 0:NB].unsqueeze(2), [P, NB, NS]), by_sequence(C16), ALU.subtract)\
                    .then_inc(pair_sums, 1)
                dve.wait_ge(pair_exps, 3 * p + 2)
                link(tt(KN[p] if p else EI[p], K[:, p, :], EI[p], ALU.mult))

            def pair_key_ends(p):
                dve.wait_ge(pair_exps, 3 * p + 3)
                link(tt(KE[p], K[:, p, :], EX[p], ALU.mult))
                link(dve.tensor_copy(EE[p][:, SEQ:T], KE[p][:, SEQ:T]))
                tt(by_block(EE[p]), by_block(KE[p]), over(gs[p][:, 3, :].unsqueeze(2), [P, NBK, BL]), ALU.mult)\
                    .then_inc(pair_ready, 1)
                dve.wait_ge(pair_ready, p + 1)

            def pair_carried(p):
                dve.wait_ge(pair_exps, 3 * p + 2)
                gb = GB[p][:, :, :, :]
                link(tt(gb, gb, over(c_("tri8").rearrange("p (i j) -> p i j", j=NBL).unsqueeze(1), g4), ALU.mult))
                qc = QM[p][:, 0:2 * SEQ].rearrange("p (c i e n) -> p e c i n", i=NBL, e=2, n=BL)
                qi = QI[p][:, :].rearrange("p (c e i n) -> p e c i n", e=2, i=NBL, n=BL)
                before = gs[p][:, 2, :].rearrange("p (c i) -> p c i", i=NBL)
                for e in range(2):
                    link(tt(qi[:, e], qc[:, e], over(before.unsqueeze(3), [P, NGC, NBL, BL]), ALU.mult))

            build_xa(0)
            dve.wait_ge(cst_in, 16)
            build_angles()
            build_wo(0)
            build_xa(1)
            core(0)
            finish_angles()
            for q in range(NG):
                if q + 2 < NG:
                    build_xa(q + 2)
                if q + 1 < NG:
                    core(q + 1)
                if q + 1 < NG:
                    build_wo(q + 1)
                z_in_sum(q)
            dve.wait_ge(g_out[1], 32)
            dve.wait_ge(z_out, 16 * NG)
            decay(0)
            decay(1)
            mask = KX[:, 0, 0:T]
            link(dve.memset(mask, 1.0))
            link(dve.memset(mask[:, 0:SEQ].rearrange("p (b n) -> p b n", n=BL)[:, :, 0:1], 0.0))
            link(dve.memset(mask[:, SEQ:T].rearrange("p (b n) -> p b n", n=NS)[:, :, 0:1], 0.0))
            for p in range(2):
                link(dve.tensor_tensor_scan(LA[:, p, :], mask, LA[:, p, :], 0.0, ALU.mult, ALU.add))
            pair_blocks(0)
            link(dve.memset(QM[0][:, :], 0.0))
            pair_queries(0)
            pair_keys(0)
            pair_carried(0)

            for k in range(4):
                dve.wait_ge(z_in[k % 2], 16 * (k // 2 + 1))
                lo_part(XL[:, k, :], TT[:, k % 2, :], XH[:, k, :], SPLIT["z"] + k + 1)
            for m in range(4):
                dve.wait_ge(z_in[m % 2], 32 + 16 * (m // 2 + 1))
                read_wait(dve, f"glu{m}")
                row = TT[:, 2 + m % 2, :]
                tt(row, row, TT[:, m % 2, :], ALU.mult).then_inc(gg_done, 1)
                dve.wait_ge(gg_done, m + 1)
                lo_part(XL[:, 4 + m, :], row, XH[:, 4 + m, :], SPLIT["zg"] + m + 1)

            dve.wait_ge(xl_done, SPLIT["o"])
            def key_blocks(it):
                p, c, b = it // NGC, it % NGC, it % 2
                if it >= 2:
                    dve.wait_ge(sc_done, it - 1)
                dst = KX[:, b, 0:NBL * GC].rearrange("p (i j n) -> p i j n", i=NBL, j=NBL)
                src = KE[p][:, c * GC:(c + 1) * GC].rearrange("p (j n) -> p j n", n=BL)
                shape = [P, NBL, NBL, BL]
                link(tt(dst, over(src.unsqueeze(1), shape), over(GB[p][:, c, :, :].unsqueeze(3), shape), ALU.mult))
                own = KX[:, b, :].rearrange("p (i x) -> p i x", x=GC + BL)[:, :, 0:BL]
                dve.tensor_copy(own, KN[p][:, c * GC:(c + 1) * GC].rearrange("p (j n) -> p j n", n=BL))\
                   .then_inc(kx_ready, 1)

            link(dve.tensor_copy(KN[0], EI[0]))
            pair_key_ends(0)
            key_blocks(0)
            key_blocks(1)
            for it in range(2 * NGC):
                p, c, b = it // NGC, it % NGC, it % 2
                dve.wait_ge(sc_done, it + 1)
                if it >= 2:
                    dve.wait_ge(o_done, it - 1)
                tt(SC[:, b, :].rearrange("p (e i n) -> p i e n", e=2, n=BL),
                   glb[:, b, 0:2 * GC].rearrange("p (i e n) -> p i e n", e=2, n=BL),
                   over(tri.unsqueeze(2), [P, NBL, 2, BL]), ALU.mult).then_inc(sc_ready, 1)
                if it + 2 < 2 * NGC:
                    key_blocks(it + 2)
                dve.wait_ge(kv_done, it + 1)
                if c == 0:
                    dve.tensor_copy(S[:, p, :], glb[:, 5, 0:P]).then_inc(s_ready, 1)
                else:
                    dve.wait_ge(s_ready, it)
                    stt(S[:, p, :], S[:, p, :], gs[p][:, 4, c:c + 1], glb[:, 5, 0:P], ALU.mult, ALU.add)\
                        .then_inc(s_ready, 1)
                if it == 0:
                    pair_blocks(1)
                if it == 2:
                    dve.wait_ge(qm_zero, 1)
                    pair_queries(1)
                if it == 3:
                    pair_keys(1)
                if it == 4:
                    pair_carried(1)
                if it == 5:
                    pair_key_ends(1)
            for p in range(2):
                dve.wait_ge(sm_done, 2 * p + 2)
                dve.wait_ge(o_done, 2 * NGC)
                if p:
                    dve.wait_ge(so_done, 1)
                tt(SC[0:32, 0, 0:64].rearrange("p (e n) -> p e n", e=2), glb[0:32, 0, 0:64].rearrange("p (e n) -> p e n", e=2),
                   over(c_("smask")[0:32, :].unsqueeze(1), [32, 2, 32]), ALU.mult).then_inc(smc_ready, 1)
                kts = KX[0:32, :, :].rearrange("p a n -> p (a n)")[:, 0:NB * P].rearrange("p (s n) -> p s n", s=NB)
                tt(kts, over(glb[0:32, 4, 0:P].unsqueeze(1), [32, NB, P]),
                   over(c_("bmask")[0:32, :].unsqueeze(2), [32, NB, P]), ALU.mult).then_inc(smk_ready, 1)
                dve.wait_ge(skv_done, p + 1)
                for s in range(NB):
                    stt(SS[p][:, s, :], SS[p][:, s, :], gs[p][:, 4, 8 + s:9 + s], glb[:, 5 if s < 4 else 1, (s % 4) * P:(s % 4 + 1) * P],
                        ALU.mult, ALU.add).then_inc(sst_ready, 1)

            def head_gate(h):
                o = (Q, K)[h % 2][:, h // 2, :]
                dve.wait_ge(g_in[h % 2], 16 * (h // 2 + 1))
                dve.wait_ge(sq_done, NCH * KT + h + 1)
                stt(o, o, p_col("g_head", h), TT[:, 2 + h % 2, :], ALU.mult, ALU.mult).then_inc(head_g, 1)

            def head_norm(h):
                o = (Q, K)[h % 2][:, h // 2, :]
                dve.wait_ge(head_rs, h + 1)
                dve.wait_ge(head_g, h + 1)
                tt(o, o, TT[:, h % 2, :], ALU.mult).then_inc(gg_done, 1)

            def head_lo(h):
                dve.wait_ge(gg_done, 4 + h + 1)
                lo_part(XL[:, h, :], (Q, K)[h % 2][:, h // 2, :], XH[:, h, :], SPLIT["o"] + h + 1)

            head_gate(0)
            head_gate(1)
            head_norm(0)
            head_norm(1)
            head_gate(2)
            head_lo(0)
            head_gate(3)
            head_lo(1)
            head_norm(2)
            head_norm(3)
            head_lo(2)
            head_lo(3)
            dve.wait_ge(xr_in, 16 * KT)

            def add_to_residual(m, t, per5=0, before=None):
                dve.wait_ge(acc_done[t % 2], per5 + (t // 2 + 1))
                if before is not None:
                    dve.wait_ge(acc_read[t % 2], before)
                tt(cut(X[:, m, :]), cut(X[:, m, :]), bank(t), ALU.add).then_inc(acc_read[t % 2], 1)

            def residual_of_norm(r, m, t, before=None):
                if m < KT - 1:
                    add_to_residual(m, t, 0, before)
                    if m:
                        add_square(r, m - 1)
                    return
                add_square(r, m - 1)
                dve.wait_ge(acc_done[t % 2], t // 2 + 1)
                if before is not None:
                    dve.wait_ge(acc_read[t % 2], before)
                for c in range(NCH):
                    tt(X[:, m, cols_of(c)], X[:, m, cols_of(c)], acc[:, t % 2, c, 0:CH], ALU.add)\
                        .then_inc(res_part if c < NCH - 1 else acc_read[t % 2], 1)

            def mlp(layer):
                t0, h0 = ACC[f"mlp{layer}_0"], FT * layer

                def hidden(t, per5, hcount, slot, u):
                    dve.wait_ge(acc_read[t % 2], per5 + (t // 2 + 1))
                    link(tt(HH[:, slot, :], TT[:, u, :], TT[:, u, :], ALU.mult))
                    dve.wait_ge(h_sq, hcount + 1)
                    tt(HL[:, slot, :], TT[:, 2 + u, :], HH[:, slot, :].bitcast(F32), ALU.subtract).then_inc(h_ready, 1)

                for j in range(2):
                    hidden(t0 + j, 0, h0 + j, j, j)
                step.loop(None, 0)
                with dve.Fori(0, HG // 2 - 1) as i:
                    step.loop(i, 4)
                    for a in range(2):
                        for j in range(2):
                            hidden(t0 + 2 + 10 * a + j, i * 10, i * 4 + (h0 + 2 * (a + 1) + j), (2 * (a + 1) + j) % 4, j)
                        for m in range(KT):
                            t = t0 + 4 + 10 * a + m
                            add_to_residual(m, t, i * 10, i * 10 + (t // 2 - 4))
                    step.end(HG // 2 - 1)
                a = HG - 2
                for j in range(2):
                    hidden(t0 + 2 + 10 * a + j, 0, h0 + 2 * (a + 1) + j, (2 * (a + 1) + j) % 4, j)
                for a, at in ((HG - 2, t0 + 4 + 10 * a), (HG - 1, t0 + 12 + 10 * a)):
                    for m in range(KT):
                        if a == HG - 1:
                            residual_of_norm(2 * layer + 2, m, at + m, (at + m) // 2 - 3)
                        else:
                            add_to_residual(m, at + m, 0, (at + m) // 2 - 3)

            for m in range(KT):
                residual_of_norm(1, m, ACC[f"oute{m}"])
            norm(1)
            mlp(0)
            norm(2)
            link(dve.memset(XP[:, :, 0:3], 0.0))
            link(dve.tensor_scalar(spt[:, :], par[:, PAR["lam"][0]:PAR["lam"][1]], 0.0, None, ALU.min))
            stt(spt[:, :], spt[:, :], 2.0, par[:, PAR["lam"][0]:PAR["lam"][1]], ALU.mult, ALU.subtract).then_inc(lam_dve, 1)
            dve.nop().then_inc(xp_ready, 1)
            dve.wait_ge(lam_act, 1)
            dve.wait_ge(lam_dve, 1)
            link(dve.tensor_scalar(sp4[:, :], par[:, PAR["lam"][0]:PAR["lam"][1]], 0.0, -1.0, ALU.min, ALU.mult))
            link(tt(sp4[:, :], sp4[:, :], spt[:, :], ALU.add))
            link(dve.tensor_scalar(sp8[:, :], sp4[:, :], -8.0, None, ALU.mult))
            dve.tensor_scalar(sp4[:, :], sp4[:, :], 4.0, None, ALU.mult).then_inc(lam_dve, 1)
            dve.wait_ge(odd_in, 32)

            def conv(n):
                read_wait(dve, f"xb{n}")
                smp = XP[:, n % 2, 3 + SEQ:].rearrange("p (b s) -> p b s", b=NB)
                outs = HB[:, n, 0:SEQ], HB[:, n, SEQ:T].rearrange("p (b s) -> p b s", b=NB)
                for j in range(4):
                    w = par[:, PAR["conv_w"][0] + 4 * n + j:PAR["conv_w"][0] + 4 * n + j + 1]
                    for out, x in zip(outs, (XP[:, n % 2, j:j + SEQ], smp[:, :, j:j + NS])):
                        if j == 0:
                            link(dve.tensor_scalar(out, x, w, p_col("conv_b", n), ALU.mult, ALU.add))
                        elif j < 3:
                            link(stt(out, x, w, out, ALU.mult, ALU.add))
                        else:
                            step.run(stt(out, x, w, out, ALU.mult, ALU.add))
                dve.tensor_copy(CN[:, n, 0:3], XP[:, n % 2, SEQ:SEQ + 3])
                dve.tensor_copy(CN[:, n, 3:].rearrange("p (b s) -> p b s", b=NB), smp[:, :, NS:NS + 3]).then_inc(conv_done, 1)
                dve.wait_ge(conv_done, n + 1)

            def recur(n):
                dve.wait_ge(gates_done, 3 * n + 1)
                link(tt(TT[:, 1, :], TT[:, 1, :], HB[:, n, :], ALU.mult))
                dve.wait_ge(gates_done, 3 * n + 3)
                link(stt(TT[:, 3, :], TT[:, 2, :], 1.0, TT[:, 3, :], ALU.add, ALU.mult))
                link(tt(TT[:, 3, :], TT[:, 3, :], TT[:, 1, :], ALU.mult))
                a0, b0 = TT[:, 2, SEQ:T:NS], TT[:, 3, SEQ:T:NS]
                link(tt(spt[:, 0:NB], a0, st_lru[:, n, :], ALU.mult))
                link(tt(b0, b0, spt[:, 0:NB], ALU.add))
                link(dve.memset(a0, 0.0))
                dve.tensor_tensor_scan(HB[:, n, :], TT[:, 2, :], TT[:, 3, :], 0.0, ALU.mult, ALU.add).then_inc(states_done, 1)
                dve.wait_ge(states_done, n + 1)
                dve.tensor_copy(LN[:, n, 0:1], HB[:, n, SEQ - 1:SEQ])
                link(dve.tensor_copy(LN[:, n, 1:], HB[:, n, SEQ + NS - 1:T:NS]))

            def apply_gate(m):
                read_wait(dve, f"gate{m}")
                tt(HB[:, m, :], HB[:, m, :], TT[:, m % 2, :], ALU.mult).then_inc(hb_ready, 1)

            conv(0)
            for n in range(KT):
                if n + 1 < KT:
                    conv(n + 1)
                recur(n)
                if n >= KT - 2:
                    apply_gate(n + 2 - KT)
            for m in range(2, KT):
                apply_gate(m)
            for k in range(KT):
                dve.wait_ge(hb_ready, k + 1)
                lo_part(XL[:, k, :], HB[:, k, :], XH[:, k, :], SPLIT["mix"] + k + 1)
            for m in range(KT):
                residual_of_norm(3, m, ACC[f"outo{m}"])
            norm(3)
            mlp(1)
            norm(4)


def tiles(w, m):
    k = w.shape[0] // P
    return w.reshape(k, P, m, P).transpose(2, 1, 0, 3).reshape(m, P, k * P)


def kernel(**inputs):
    import numpy as np
    import concourse.bacc as bacc
    from concourse.bass_utils import run_bass_kernel_spmd as run

    x = {k: np.asarray(v) for k, v in inputs.items()}
    f32 = np.float32
    tok = np.concatenate([x["x_prompt"].reshape(SEQ, D), x["x_sample"].reshape(NB * NS, D)])
    x_t = np.ascontiguousarray(tok.T).reshape(KT, P, T)

    w = x["w_in_even"][0]
    wv = w[:, 512:1024].reshape(4, 2, P, 512).transpose(0, 2, 1, 3).reshape(4, P, 1024)
    walr = np.zeros((D, P), f32)
    walr[:, :16] = w[:, 1536:1552]
    glu = tiles(x["s5_w_glu"][0], 4).reshape(2, 2, P, 512).transpose(0, 2, 1, 3).reshape(2, P, 1024)

    def mlp_tiles(layer):
        up = tiles(x["w_up"][layer], FT)
        down = x["w_down"][layer].reshape(FT, P, D)
        order = [up[0:2]]
        for a in range(1, HG):
            order += [up[2 * a:2 * a + 2], down[2 * a - 2:2 * a]]
        return np.concatenate(order + [down[FT - 2:FT]])

    w_odd = x["w_in_odd"][0]
    w_stream = np.concatenate([
        tiles(w[:, 1552:], 4), tiles(w[:, 0:256], 2), tiles(w[:, 1024:1536], 4), tiles(w[:, 256:512], 2),
        tiles(walr, 1), wv, glu, tiles(x["w_out_even"][0], KT), mlp_tiles(0),
        tiles(w_odd[:, D:], KT), tiles(w_odd[:, :D], KT), tiles(x["w_out_odd"][0], KT), mlp_tiles(1)])
    assert w_stream.shape == (NT, P, 1024)

    def cols(v):
        return v.reshape(-1, P).T

    par = np.concatenate([
        cols(x["norm_mix_even"][0]), cols(x["norm_mlp"][0]), cols(x["norm_mix_odd"][0]), cols(x["norm_mlp"][1]),
        cols(x["norm_final"]), cols(x["gla_norm"][0]), cols(x["gla_b_a2"][0]), cols(x["s5_d"][0].reshape(-1)),
        cols(x["s5_b_glu"][0]), x["conv_w"][0].reshape(4, KT, P).transpose(2, 1, 0).reshape(P, 32),
        cols(x["conv_b"][0]), cols(x["lru_b_r"][0]), cols(x["lru_b_i"][0]), cols(x["lru_lam"][0])], axis=1)

    def states(v):
        v = v.reshape((16, 2, 64) + v.shape[2:])
        return np.moveaxis(v, 0, 2).reshape(P, -1)

    dt = np.broadcast_to(x["s5_log_dt"][0][:, None], (32, 64))
    par5 = np.concatenate([
        states(x["s5_a_re"][0]), states(x["s5_a_im"][0]), states(dt), states(x["s5_b_re"][0]), states(x["s5_b_im"][0]),
        states(x["s5_c_re"][0].transpose(0, 2, 1)), states(x["s5_c_im"][0].transpose(0, 2, 1)),
        states(x["state_s5_re"][0].transpose(1, 2, 0)), states(x["state_s5_im"][0].transpose(1, 2, 0))], axis=1)

    cst = np.zeros((P, NCST), f32)
    i = np.arange(P)
    cst[:, 0:128] = np.eye(P)
    cst[:, 128:256] = i[:, None] <= i[None, :]
    j = np.arange(32)
    cst[0:32, 256:288] = (j[:, None] <= j[None, :]) & (j[:, None] // NS == j[None, :] // NS)
    cst[0:32, 288:296] = j[:, None] // NS == np.arange(NB)[None, :]
    b = np.arange(NBL)
    cst[:, 296:360] = (b[None, :] < b[:, None]).reshape(1, -1)
    cst[:, 360:488] = np.arange(NC)[None, :]

    w_ri = np.stack([x["lru_w_r"][0], x["lru_w_i"][0]], axis=1).transpose(0, 2, 1, 3)
    st_gla = x["state_gla"][0].reshape(NB, 2, P, P).transpose(1, 2, 0, 3)
    odd_lru = x["state_lru"][0].reshape(NB, KT, P).transpose(2, 1, 0)
    odd_conv = x["state_conv"][0].reshape(NB, 3, KT, P).transpose(3, 2, 0, 1)

    nc = bacc.Bacc("TRN2", target_bir_lowering=False, num_devices=1)
    arrays, args = {}, []
    for name, a in (("x_t", x_t), ("w_stream", w_stream), ("par", par), ("par5", par5), ("cst", cst),
                    ("w_a2", x["gla_w_a2"][0]), ("w_ri", w_ri), ("st_gla", st_gla), ("odd_lru", odd_lru),
                    ("odd_conv", odd_conv)):
        arrays[f"in_{name}"] = np.ascontiguousarray(a)
        args.append(nc.dram_tensor(f"in_{name}", a.shape, F32, kind="ExternalInput").ap())
    for name, shape in (("y_t", (KT, P, T)), ("s5_out", (P, 2, 16, 1 + NB)), ("lru_out", (P, KT, 1 + NB)),
                        ("conv_out", (P, KT, 3 * (1 + NB))), ("gla_p", (P, 2, P)), ("gla_s", (2, P, NB, P))):
        args.append(nc.dram_tensor(f"out_{name}", shape, F32, kind="ExternalOutput").ap())
    trunk_kernel(nc, *args)
    r = run(nc, [arrays], core_ids=[0]).results[0]
    r = {k.removeprefix("out_"): np.asarray(v) for k, v in r.items()}

    y = r["y_t"].reshape(D, T).T
    s5 = r["s5_out"].reshape(2, 64, 2, 16, 1 + NB).transpose(2, 4, 3, 0, 1).reshape(2, 1 + NB, 32, 64)
    lru = r["lru_out"].transpose(2, 1, 0).reshape(1 + NB, D)
    conv = r["conv_out"].reshape(P, KT, 1 + NB, 3).transpose(2, 3, 1, 0).reshape(1 + NB, 3, D)
    gla_prompt = r["gla_p"].reshape(2, 64, 2, P).transpose(2, 0, 1, 3).reshape(1, 1, 4, 64, P)
    gla_sample = r["gla_s"].reshape(2, 2, 64, NB, P).transpose(3, 0, 1, 2, 4).reshape(1, NB, 4, 64, P)
    c = np.ascontiguousarray
    return (c(y[:SEQ]).reshape(1, SEQ, D), c(y[SEQ:]).reshape(NB, NS, D),
            c(gla_prompt), c(s5[0, :1])[None], c(s5[1, :1])[None], c(lru[:1])[None], c(conv[:1])[None],
            c(gla_sample), c(s5[0, 1:])[None], c(s5[1, 1:])[None], c(lru[1:])[None], c(conv[1:])[None])
```
